# Optimizing a Trainium2 kernel written in Bass

```python
import math
import jax
import jax.numpy as jnp
from jax import lax
import numpy as np

D_MODEL = 1024
BATCH = 1
SEQ = 512
DEPTH = 4

N_MIXERS = 3
N_MLA_LAYERS = (DEPTH + 2) // 3
N_NSA_LAYERS = (DEPTH + 1) // 3
N_S5_LAYERS = DEPTH // 3
NORM_EPS = 1e-6
N_MOD = 6
Q_BLOCK = 128

MLA_HEADS = 8
MLA_Q_LORA = 512
MLA_KV_LORA = 256
MLA_NOPE = 128
MLA_ROPE = 64
MLA_V = 128
MLA_QK = MLA_NOPE + MLA_ROPE
ROPE_THETA = 10000.0

NSA_HEADS = 8
NSA_GROUPS = 2
NSA_HPG = NSA_HEADS // NSA_GROUPS
NSA_DK = 128
NSA_DV = 128
CMP_BLOCK = 32
CMP_STRIDE = 16
CMP_RATIO = CMP_BLOCK // CMP_STRIDE
CMP_HIDDEN = 256
SLC_BLOCK = 64
SLC_TOPN = 16
N_LOCAL = 2
FORCE_BONUS = 1e4
WINDOW = 512
SLC_Q_CHUNK = 16
NSA_SPLITS = (NSA_HEADS * NSA_DK,
              NSA_GROUPS * NSA_DK, NSA_GROUPS * NSA_DV,
              NSA_GROUPS * NSA_DK, NSA_GROUPS * NSA_DV,
              NSA_GROUPS * NSA_DK, NSA_GROUPS * NSA_DV,
              3 * NSA_HEADS)
NSA_PROJ = NSA_HEADS * NSA_DK + 3 * NSA_GROUPS * (NSA_DK + NSA_DV) + 3 * NSA_HEADS

REL_BUCKETS = 32
REL_MAX_DIST = 128

S5_GROUP = 16
S5_STATE = 64
S5_NGROUPS = D_MODEL // S5_GROUP
DT_MIN = 1e-3
DT_MAX = 1e-1

D_FF = 2816
CONV_WIDTH = 3

kernel_name = 'hybrid_mla_nsa_s5_conv_glu_trunk'

def _split(t, sizes):
    return jnp.split(t, np.cumsum(sizes)[:-1].tolist(), axis=-1)

def rms_norm(x, g):
    xf = x.astype(jnp.float32)
    y = xf * lax.rsqrt(jnp.mean(xf * xf, axis=-1, keepdims=True) + NORM_EPS)
    return (y * g.astype(jnp.float32)).astype(x.dtype)

def masked_softmax(s, mask):
    s = jnp.where(mask, s, -jnp.inf)
    m = jnp.max(s, axis=-1, keepdims=True)
    m = jnp.where(jnp.isfinite(m), m, 0.0)
    p = jnp.exp(s - m)
    return p / jnp.maximum(jnp.sum(p, axis=-1, keepdims=True), 1e-30)

def rope(t, pos):
    half = t.shape[-1] // 2
    inv = ROPE_THETA ** (-jnp.arange(half, dtype=jnp.float32) / half)
    ang = pos.astype(jnp.float32)[:, None] * inv[None, :]
    cos = jnp.cos(ang)[None, :, None, :]
    sin = jnp.sin(ang)[None, :, None, :]
    t1, t2 = t[..., :half], t[..., half:]
    return jnp.concatenate([t1 * cos - t2 * sin, t1 * sin + t2 * cos], axis=-1).astype(t.dtype)

def t5_bucket(dist):
    n = jnp.maximum(dist, 0)
    max_exact = REL_BUCKETS // 2
    nf = jnp.maximum(n, 1).astype(jnp.float32)
    large = max_exact + (jnp.log(nf / max_exact) / math.log(REL_MAX_DIST / max_exact)
                         * (REL_BUCKETS - max_exact)).astype(jnp.int32)
    large = jnp.minimum(large, REL_BUCKETS - 1)
    return jnp.where(n < max_exact, n, large)

def mla_mixer(h, w_dkv, g_q, g_kv, w_uq, w_ukv, w_o):
    bsz, seq, _ = h.shape
    c_q, c_kv, k_rope = _split(h @ w_dkv, (MLA_Q_LORA, MLA_KV_LORA, MLA_ROPE))
    c_q = rms_norm(c_q, g_q)
    c_kv = rms_norm(c_kv, g_kv)
    q = (c_q @ w_uq).reshape(bsz, seq, MLA_HEADS, MLA_QK)
    kv = (c_kv @ w_ukv).reshape(bsz, seq, MLA_HEADS, MLA_NOPE + MLA_V)
    pos = jnp.arange(seq)
    q = jnp.concatenate([q[..., :MLA_NOPE], rope(q[..., MLA_NOPE:], pos)], axis=-1)
    k_r = jnp.broadcast_to(rope(k_rope[:, :, None, :], pos), (bsz, seq, MLA_HEADS, MLA_ROPE))
    k = jnp.concatenate([kv[..., :MLA_NOPE], k_r], axis=-1).transpose(0, 2, 1, 3)
    v = kv[..., MLA_NOPE:].transpose(0, 2, 1, 3)
    nb = seq // Q_BLOCK
    q_blocks = q.reshape(bsz, nb, Q_BLOCK, MLA_HEADS, MLA_QK).transpose(1, 0, 3, 2, 4)
    scale = MLA_QK ** -0.5

    def attend(args):
        qb, i = args
        qpos = i * Q_BLOCK + jnp.arange(Q_BLOCK)
        s = jnp.einsum('bhqd,bhkd->bhqk', qb, k).astype(jnp.float32) * scale
        p = masked_softmax(s, pos[None, :] <= qpos[:, None])
        return jnp.einsum('bhqk,bhkd->bhqd', p.astype(v.dtype), v)

    o = lax.map(attend, (q_blocks, jnp.arange(nb)))
    o = o.transpose(1, 0, 3, 2, 4).reshape(bsz, seq, MLA_HEADS * MLA_V)
    return o @ w_o

def _compress(t, pe, w1, w2):
    bsz, ng, seq, d = t.shape
    n_chunk = seq // CMP_STRIDE
    nc = n_chunk - CMP_RATIO + 1
    ch = t.reshape(bsz, ng, n_chunk, CMP_STRIDE, d)
    blocks = jnp.concatenate([ch[:, :, r:r + nc] for r in range(CMP_RATIO)], axis=3)
    flat = (blocks + pe).reshape(bsz, ng, nc, CMP_BLOCK * d)
    return jax.nn.gelu(flat @ w1) @ w2

def nsa_mixer(h, w_in, pe_k, w1_k, w2_k, pe_v, w1_v, w2_v, rel_bias, w_o):
    bsz, seq, _ = h.shape
    G, HP = NSA_GROUPS, NSA_HPG
    q, k_c, v_c, k_s, v_s, k_w, v_w, gates = _split(h @ w_in, NSA_SPLITS)
    q = q.reshape(bsz, seq, G, HP, NSA_DK).transpose(0, 2, 3, 1, 4)

    def heads_kv(t):
        return t.reshape(bsz, seq, G, -1).transpose(0, 2, 1, 3)

    k_c, v_c, k_s, v_s, k_w, v_w = (heads_kv(t) for t in (k_c, v_c, k_s, v_s, k_w, v_w))
    pos = jnp.arange(seq)
    scale = NSA_DK ** -0.5
    rel_g = rel_bias.reshape(G, HP, REL_BUCKETS)

    kc = _compress(k_c, pe_k, w1_k, w2_k)
    vc = _compress(v_c, pe_v, w1_v, w2_v)
    nc = kc.shape[2]
    cmp_start = jnp.arange(nc) * CMP_STRIDE
    cmp_end = cmp_start + CMP_BLOCK - 1
    dist_c = pos[:, None] - cmp_end[None, :]
    bias_c = rel_bias[:, t5_bucket(dist_c)].reshape(G, HP, seq, nc)
    s_c = jnp.einsum('bghqd,bgkd->bghqk', q, kc).astype(jnp.float32) * scale + bias_c
    p_cmp = masked_softmax(s_c, dist_c >= 0)
    o_cmp = jnp.einsum('bghqk,bgkd->bghqd', p_cmp.astype(vc.dtype), vc)

    ns = seq // SLC_BLOCK
    n_sel = min(SLC_TOPN, ns)
    blk = jnp.arange(ns)
    blk_start = blk * SLC_BLOCK
    overlap = ((cmp_start[:, None] < blk_start[None, :] + SLC_BLOCK)
               & (cmp_start[:, None] + CMP_BLOCK > blk_start[None, :])).astype(jnp.float32)
    imp = jnp.einsum('bghqk,kj->bgqj', p_cmp, overlap)
    back = (pos // SLC_BLOCK)[:, None] - blk[None, :]
    forced = (blk[None, :] == 0) | ((back >= 0) & (back < N_LOCAL))
    causal_blk = blk_start[None, :] <= pos[:, None]
    score = jnp.where(causal_blk, imp + jnp.where(forced, FORCE_BONUS, 0.0), -jnp.inf)
    top_val, top_idx = lax.top_k(score, n_sel)
    top_ok = jnp.isfinite(top_val)

    ks_blocks = k_s.reshape(bsz, G, ns, SLC_BLOCK, NSA_DK)
    vs_blocks = v_s.reshape(bsz, G, ns, SLC_BLOCK, NSA_DV)
    gather = jax.vmap(jax.vmap(lambda blocks, ids: blocks[ids]))
    nq = seq // SLC_Q_CHUNK
    q_ch = q.reshape(bsz, G, HP, nq, SLC_Q_CHUNK, NSA_DK).transpose(3, 0, 1, 2, 4, 5)
    idx_ch = top_idx.reshape(bsz, G, nq, SLC_Q_CHUNK, n_sel).transpose(2, 0, 1, 3, 4)
    ok_ch = top_ok.reshape(bsz, G, nq, SLC_Q_CHUNK, n_sel).transpose(2, 0, 1, 3, 4)
    pos_ch = pos.reshape(nq, SLC_Q_CHUNK)
    n_keys = n_sel * SLC_BLOCK

    def select_chunk(args):
        qc, idc, okc, qpos = args
        kg = gather(ks_blocks, idc).reshape(bsz, G, SLC_Q_CHUNK, n_keys, NSA_DK)
        vg = gather(vs_blocks, idc).reshape(bsz, G, SLC_Q_CHUNK, n_keys, NSA_DV)
        kpos = (idc[..., None] * SLC_BLOCK + jnp.arange(SLC_BLOCK)).reshape(bsz, G, SLC_Q_CHUNK, n_keys)
        mask = jnp.repeat(okc, SLC_BLOCK, axis=-1) & (kpos <= qpos[:, None])
        bucket = t5_bucket(qpos[:, None] - kpos)
        bias = rel_g[jnp.arange(G)[:, None, None, None], jnp.arange(HP)[None, :, None, None],
                     bucket[:, :, None]]
        s = jnp.einsum('bghqd,bgqkd->bghqk', qc, kg).astype(jnp.float32) * scale + bias
        p = masked_softmax(s, mask[:, :, None])
        return jnp.einsum('bghqk,bgqkd->bghqd', p.astype(vg.dtype), vg)

    o_slc = lax.map(select_chunk, (q_ch, idx_ch, ok_ch, pos_ch))
    o_slc = o_slc.transpose(1, 2, 3, 0, 4, 5).reshape(bsz, G, HP, seq, NSA_DV)

    span = Q_BLOCK + WINDOW
    kwp = jnp.pad(k_w, ((0, 0), (0, 0), (WINDOW, 0), (0, 0)))
    vwp = jnp.pad(v_w, ((0, 0), (0, 0), (WINDOW, 0), (0, 0)))
    nb = seq // Q_BLOCK
    q_blocks = q.reshape(bsz, G, HP, nb, Q_BLOCK, NSA_DK).transpose(3, 0, 1, 2, 4, 5)

    def window_block(args):
        qb, i = args
        start = i * Q_BLOCK
        kb = lax.dynamic_slice_in_dim(kwp, start, span, axis=2)
        vb = lax.dynamic_slice_in_dim(vwp, start, span, axis=2)
        qpos = start + jnp.arange(Q_BLOCK)
        kpos = start - WINDOW + jnp.arange(span)
        dist = qpos[:, None] - kpos[None, :]
        mask = (dist >= 0) & (dist < WINDOW) & (kpos >= 0)[None, :]
        bias = rel_bias[:, t5_bucket(dist)].reshape(G, HP, Q_BLOCK, span)
        s = jnp.einsum('bghqd,bgkd->bghqk', qb, kb).astype(jnp.float32) * scale + bias
        p = masked_softmax(s, mask)
        return jnp.einsum('bghqk,bgkd->bghqd', p.astype(vb.dtype), vb)

    o_win = lax.map(window_block, (q_blocks, jnp.arange(nb)))
    o_win = o_win.transpose(1, 2, 3, 0, 4, 5).reshape(bsz, G, HP, seq, NSA_DV)

    g = jax.nn.sigmoid(gates.astype(jnp.float32)).reshape(bsz, seq, 3, G, HP)
    g = g.transpose(2, 0, 3, 4, 1)[..., None].astype(h.dtype)
    o = g[0] * o_cmp + g[1] * o_slc + g[2] * o_win
    o = o.transpose(0, 3, 1, 2, 4).reshape(bsz, seq, NSA_HEADS * NSA_DV)
    return o @ w_o

def _ssm_combine(e1, e2):
    a1r, a1i, b1r, b1i = e1
    a2r, a2i, b2r, b2i = e2
    return (a2r * a1r - a2i * a1i,
            a2r * a1i + a2i * a1r,
            a2r * b1r - a2i * b1i + b2r,
            a2r * b1i + a2i * b1r + b2i)

def s5_mixer(h, lam_re, lam_im, log_dt, b_re, b_im, c_re, c_im, d_skip, w_glu):
    bsz, seq, dm = h.shape
    f32 = jnp.float32
    lam_re, lam_im = lam_re.astype(f32), lam_im.astype(f32)
    b_re, b_im, c_re, c_im = b_re.astype(f32), b_im.astype(f32), c_re.astype(f32), c_im.astype(f32)
    u = h.astype(f32).reshape(bsz, seq, S5_NGROUPS, S5_GROUP)
    dt = jnp.exp(log_dt.astype(f32))[:, None]
    mag = jnp.exp(lam_re * dt)
    lb_re = mag * jnp.cos(lam_im * dt)
    lb_im = mag * jnp.sin(lam_im * dt)
    den = lam_re * lam_re + lam_im * lam_im
    f_re = ((lb_re - 1.0) * lam_re + lb_im * lam_im) / den
    f_im = (lb_im * lam_re - (lb_re - 1.0) * lam_im) / den
    bb_re = f_re[..., None] * b_re - f_im[..., None] * b_im
    bb_im = f_re[..., None] * b_im + f_im[..., None] * b_re
    bu_re = jnp.einsum('bsgi,gpi->sbgp', u, bb_re)
    bu_im = jnp.einsum('bsgi,gpi->sbgp', u, bb_im)
    a_shape = (seq, 1, S5_NGROUPS, S5_STATE)
    a_re = jnp.broadcast_to(lb_re[None, None], a_shape)
    a_im = jnp.broadcast_to(lb_im[None, None], a_shape)
    _, _, x_re, x_im = lax.associative_scan(_ssm_combine, (a_re, a_im, bu_re, bu_im), axis=0)
    y = (jnp.einsum('sbgp,gip->bsgi', x_re, c_re) - jnp.einsum('sbgp,gip->bsgi', x_im, c_im)
         + d_skip.astype(f32) * u)
    y = jax.nn.gelu(y.reshape(bsz, seq, dm)).astype(h.dtype)
    za, zb = jnp.split(y @ w_glu, 2, axis=-1)
    return za * jax.nn.sigmoid(zb)

def conv_glu_ffn(h, w_up, conv_w, conv_b, w_down):
    z = h @ w_up
    ch = z.shape[-1]
    z = lax.conv_general_dilated(z, conv_w[:, None, :].astype(z.dtype), window_strides=(1,),
                                 padding=[(CONV_WIDTH - 1, 0)],
                                 dimension_numbers=('NWC', 'WIO', 'NWC'),
                                 feature_group_count=ch) + conv_b
    val, gate = jnp.split(z, 2, axis=-1)
    return (val * jax.nn.silu(gate)) @ w_down

def _nrm(k, shape, scale):
    return jax.random.normal(k, shape, jnp.float32) * scale

def setup_inputs(seed: int = 0) -> dict:
    key = jax.random.key(seed)
    ks = jax.random.split(key, 40)
    D = D_MODEL
    NA, NB, NC = N_MLA_LAYERS, N_NSA_LAYERS, N_S5_LAYERS
    return {
        'x': _nrm(ks[0], (BATCH, SEQ, D), 1.0),
        'c': _nrm(ks[1], (BATCH, D), 1.0),
        'ada_w': _nrm(ks[2], (DEPTH, D, N_MOD * D), 0.5 * D ** -0.5),
        'ada_b': _nrm(ks[3], (DEPTH, N_MOD * D), 0.02),
        'norm1_g': 1.0 + _nrm(ks[4], (DEPTH, D), 0.02),
        'norm2_g': 1.0 + _nrm(ks[5], (DEPTH, D), 0.02),
        'final_g': 1.0 + _nrm(ks[6], (D,), 0.02),
        'rel_bias': _nrm(ks[7], (NSA_HEADS, REL_BUCKETS), 0.5),
        'mla_w_dkv': _nrm(ks[8], (NA, D, MLA_Q_LORA + MLA_KV_LORA + MLA_ROPE), D ** -0.5),
        'mla_g_q': 1.0 + _nrm(ks[9], (NA, MLA_Q_LORA), 0.02),
        'mla_g_kv': 1.0 + _nrm(ks[10], (NA, MLA_KV_LORA), 0.02),
        'mla_w_uq': _nrm(ks[11], (NA, MLA_Q_LORA, MLA_HEADS * MLA_QK), MLA_Q_LORA ** -0.5),
        'mla_w_ukv': _nrm(ks[12], (NA, MLA_KV_LORA, MLA_HEADS * (MLA_NOPE + MLA_V)), MLA_KV_LORA ** -0.5),
        'mla_w_o': _nrm(ks[13], (NA, MLA_HEADS * MLA_V, D), (MLA_HEADS * MLA_V) ** -0.5),
        'nsa_w_in': _nrm(ks[14], (NB, D, NSA_PROJ), D ** -0.5),
        'nsa_pe_k': _nrm(ks[15], (NB, CMP_BLOCK, NSA_DK), 0.1),
        'nsa_w1_k': _nrm(ks[16], (NB, CMP_BLOCK * NSA_DK, CMP_HIDDEN), (CMP_BLOCK * NSA_DK) ** -0.5),
        'nsa_w2_k': _nrm(ks[17], (NB, CMP_HIDDEN, NSA_DK), CMP_HIDDEN ** -0.5),
        'nsa_pe_v': _nrm(ks[18], (NB, CMP_BLOCK, NSA_DV), 0.1),
        'nsa_w1_v': _nrm(ks[19], (NB, CMP_BLOCK * NSA_DV, CMP_HIDDEN), (CMP_BLOCK * NSA_DV) ** -0.5),
        'nsa_w2_v': _nrm(ks[20], (NB, CMP_HIDDEN, NSA_DV), CMP_HIDDEN ** -0.5),
        'nsa_w_o': _nrm(ks[21], (NB, NSA_HEADS * NSA_DV, D), (NSA_HEADS * NSA_DV) ** -0.5),
        's5_lam_re': -0.5 + _nrm(ks[22], (NC, S5_NGROUPS, S5_STATE), 0.01),
        's5_lam_im': jnp.broadcast_to(math.pi * jnp.arange(S5_STATE, dtype=jnp.float32),
                                      (NC, S5_NGROUPS, S5_STATE)),
        's5_log_dt': jax.random.uniform(ks[23], (NC, S5_NGROUPS), jnp.float32,
                                        math.log(DT_MIN), math.log(DT_MAX)),
        's5_b_re': _nrm(ks[24], (NC, S5_NGROUPS, S5_STATE, S5_GROUP), (2 * S5_GROUP) ** -0.5),
        's5_b_im': _nrm(ks[25], (NC, S5_NGROUPS, S5_STATE, S5_GROUP), (2 * S5_GROUP) ** -0.5),
        's5_c_re': _nrm(ks[26], (NC, S5_NGROUPS, S5_GROUP, S5_STATE), S5_STATE ** -0.5),
        's5_c_im': _nrm(ks[27], (NC, S5_NGROUPS, S5_GROUP, S5_STATE), S5_STATE ** -0.5),
        's5_d': _nrm(ks[28], (NC, S5_NGROUPS, S5_GROUP), 1.0),
        's5_w_glu': _nrm(ks[29], (NC, D, 2 * D), D ** -0.5),
        'ffn_w_up': _nrm(ks[30], (DEPTH, D, 2 * D_FF), D ** -0.5),
        'ffn_conv_w': _nrm(ks[31], (DEPTH, CONV_WIDTH, 2 * D_FF), CONV_WIDTH ** -0.5),
        'ffn_conv_b': _nrm(ks[32], (DEPTH, 2 * D_FF), 0.02),
        'ffn_w_down': _nrm(ks[33], (DEPTH, D_FF, D), D_FF ** -0.5),
    }

def reference(x, c, ada_w, ada_b, norm1_g, norm2_g, final_g, rel_bias,
              mla_w_dkv, mla_g_q, mla_g_kv, mla_w_uq, mla_w_ukv, mla_w_o,
              nsa_w_in, nsa_pe_k, nsa_w1_k, nsa_w2_k, nsa_pe_v, nsa_w1_v, nsa_w2_v, nsa_w_o,
              s5_lam_re, s5_lam_im, s5_log_dt, s5_b_re, s5_b_im, s5_c_re, s5_c_im, s5_d, s5_w_glu,
              ffn_w_up, ffn_conv_w, ffn_conv_b, ffn_w_down):
    bsz = x.shape[0]
    c_act = jax.nn.silu(c)
    for i in range(DEPTH):
        mod = (c_act @ ada_w[i] + ada_b[i]).reshape(bsz, N_MOD, D_MODEL)[:, :, None, :]
        shift1, scale1, gate1 = mod[:, 0], mod[:, 1], mod[:, 2]
        shift2, scale2, gate2 = mod[:, 3], mod[:, 4], mod[:, 5]
        h = rms_norm(x, norm1_g[i]) * (1.0 + scale1) + shift1
        kind, j = i % N_MIXERS, i // N_MIXERS
        if kind == 0:
            y = mla_mixer(h, mla_w_dkv[j], mla_g_q[j], mla_g_kv[j], mla_w_uq[j], mla_w_ukv[j], mla_w_o[j])
        elif kind == 1:
            y = nsa_mixer(h, nsa_w_in[j], nsa_pe_k[j], nsa_w1_k[j], nsa_w2_k[j],
                          nsa_pe_v[j], nsa_w1_v[j], nsa_w2_v[j], rel_bias, nsa_w_o[j])
        else:
            y = s5_mixer(h, s5_lam_re[j], s5_lam_im[j], s5_log_dt[j], s5_b_re[j], s5_b_im[j],
                         s5_c_re[j], s5_c_im[j], s5_d[j], s5_w_glu[j])
        x = x + gate1 * y
        h = rms_norm(x, norm2_g[i]) * (1.0 + scale2) + shift2
        x = x + gate2 * conv_glu_ffn(h, ffn_w_up[i], ffn_conv_w[i], ffn_conv_b[i], ffn_w_down[i])
    return rms_norm(x, final_g)


_drawn_inputs = setup_inputs


def setup_inputs(seed=0):
    import zlib

    import numpy as np

    out = dict(_drawn_inputs(seed))
    spreads = {}
    factors = {'norm1_g': 8.0,
     'norm2_g': 4.596,
     'final_g': 7.571,
     'rel_bias': 2.741,
     'mla_g_q': 8.0,
     'mla_g_kv': 8.0,
     'nsa_pe_k': 8.0,
     'nsa_w1_k': 2.964,
     'nsa_w2_k': 3.058,
     'nsa_pe_v': 6.627,
     's5_lam_re': 64.0,
     's5_lam_im': 38.824,
     's5_log_dt': 46.312,
     's5_b_re': 52.336,
     's5_b_im': 54.672,
     's5_c_re': 51.36,
     's5_c_im': 56.048,
     'ffn_conv_b': 4.984}
    for name, (base, spread) in spreads.items():
        noise = np.random.default_rng([zlib.crc32(name.encode()), seed]).standard_normal(out[name].shape)
        drawn = base * np.exp(spread * noise) if base else spread * noise
        out[name] = jnp.asarray(drawn.astype(out[name].dtype))
    for name, factor in factors.items():
        out[name] = (out[name] * factor).astype(out[name].dtype)
    return out
```

```python
import math
from contextlib import ExitStack, contextmanager

import concourse.bass as bass
from concourse import mybir

ALU = mybir.AluOpType
ACT = mybir.ActivationFunctionType
AX = mybir.AxisListType.X
F32 = mybir.dt.float32
F32R = mybir.dt.float32r
BF16 = mybir.dt.bfloat16

P = 128
D = 1024
S = 512
LAYERS = (0, 1, 2, 3)
DEPTH = 4
KT = D // P
TT = S // P
EPS = 1e-6
N_MOD = 6
MODS = N_MOD * KT

Q_LORA, KV_LORA, ROPE, NOPE = 512, 256, 64, 128
HEADS = 8
QK = NOPE + ROPE
CQ, CKV = Q_LORA // P, KV_LORA // P
MLA_SCALE = float(QK) ** -0.5
DKV_UNITS = 7

GROUPS, HPG, DK = 2, 4, 128
NSA_SCALE = float(DK) ** -0.5
CB, CS = 32, 16
NC = S // CS - 1
CH = 256
BUCKETS = 32
FAR = 2 * P
NSA_COL = {"q": 0, "kc": 1024, "vc": 1280, "ks": 1536, "vs": 1792, "kw": 2048, "vw": 2304, "gate": 2560}
MASKED = -1e30

SG, SN, SI = 64, 64, 16
ST = SG * SN // P
FINE, COARSE = 32, S // 32

FF = 2816
PAIRS = FF // P
HALF = PAIRS // 2
TAPS = 3
CHT = 2 * PAIRS

SERIES = 8
ROUND = 1.5 * 2.0 ** 23
TWO_PI = (6.28125, 0.0019350051879882812, 2 * math.pi - 6.28125 - 0.0019350051879882812)
PI_IN = 3.1415925
LN_2 = (0.693359375, math.log(2) - 0.693359375)

UNIT = HALF * P
TRI = P * TT * (TT + 1) // 2
ROW_AT = [P * i * (i + 1) // 2 for i in range(TT)]
COL_AT = [P * sum(TT - c for c in range(j)) for j in range(TT)]

NORM_COLS = {"norm1": 0, "norm2": 32, "final": 64, "gq": 72, "gkv": 80, "d": 84}
MISC_ROWS = 92
CW_ROWS, CB_ROWS, AB_ROWS = 88, 88, 96


def reached(eng, sem, value):
    if not (isinstance(value, int) and value <= 0):
        eng.wait_ge(sem, value)


def repeat(eng, trips, per, total, step, chain=None, links=0):
    if trips:
        with ExitStack() as ctx:
            i = ctx.enter_context(eng.Fori(0, trips))
            if chain is not None:
                ctx.enter_context(chain.loop(i, trips, per * links))
            for r in range(per):
                step(i, r)
    for n in range(trips * per, total):
        step(n // per, n % per)


class Chain:

    def __init__(self, eng, sem):
        self.eng, self.sem, self.n, self.i, self.per = eng, sem, 0, None, 0

    def step(self, ins):
        ins.then_inc(self.sem, 1)
        self.n += 1

    def wait(self):
        self.eng.wait_ge(self.sem, self.n if self.i is None else self.i * self.per + self.n)

    def link(self, ins):
        self.step(ins)
        self.wait()

    @contextmanager
    def loop(self, i, trips, per):
        first, self.i, self.per = self.n, i, per
        yield
        assert self.n == first + per, (self.n, first, per)
        self.n, self.i = first + per * trips, None


def units_of(layer):
    kind = layer % 3
    mixer = (DKV_UNITS + 2 * HEADS + KT) if kind == 0 else (8 + 16 + 4 + 1 + HEADS + KT) if kind == 1 else 2 * KT
    return mixer


def trunk(nc, t, out, scratch):
    with ExitStack() as ctx:
        def sb(name, shape, dt=F32, stack=ctx):
            return stack.enter_context(nc.sbuf_tensor(name, shape, dt))

        def sem(name):
            return ctx.enter_context(nc.semaphore(name))

        bank = ctx.enter_context(nc.psum_tensor("bank", [P, 8, 512], F32))

        x = sb("x", [P, KT, S])
        hf = sb("hf", [P, KT, S])
        h_hi = sb("h_hi", [P, KT, S], F32R)
        h_lo = sb("h_lo", [P, KT, S], F32R)
        stage = sb("stage", [P, 2, UNIT])
        w_hi = sb("w_hi", [P, 2, UNIT], F32R)
        w_lo = sb("w_lo", [P, 2, UNIT], F32R)
        rs = sb("rs", [P, S])
        ident = sb("ident", [P, P])
        ones = sb("ones", [P, P])
        eps = sb("eps", [P, 1])
        ident_b = sb("ident_b", [P, P], BF16)
        mask_b = sb("mask_b", [P, P], BF16)
        mask = sb("mask", [P, P])
        mod = sb("mod", [P, DEPTH * MODS])
        misc = sb("misc", [P, MISC_ROWS])
        cw = sb("cw", [P, DEPTH * TAPS * CHT])
        cb = sb("cb", [P, DEPTH * CHT])
        amp = sb("amp", [P, DEPTH * 2 * KT])

        landed = [sem("landed0"), sem("landed1")]
        hi_made, lo_made, weights_used, drained = sem("hi_made"), sem("lo_made"), sem("weights_used"), sem("drained")
        phase_end = sem("phase_end")
        act_chain, dve_chain, pool_chain = sem("act_chain"), sem("dve_chain"), sem("pool_chain")
        params_in, consts_in, turned_in, copied_in = sem("params_in"), sem("consts_in"), sem("turned_in"), sem("copied_in")
        rooted = sem("rooted")
        squares, summed, h_made, h_high = sem("squares"), sem("summed"), sem("h_made"), sem("h_high")
        cv_made, silu_made, g_made, g_high, g_low = sem("cv_made"), sem("silu_made"), sem("g_made"), sem("g_high"), sem("g_low")
        stored = sem("stored")
        ada_in = [sem(f"ada_in{s}") for s in range(4)]
        ada_used = sem("ada_used")
        side_in = sem("side_in")

        with ExitStack() as own:
            rows = sb("rows", [P, 20, P], stack=own)
            x_rows = sb("x_rows", [P, TT, D], stack=own)
            ada_w = sb("ada_w", [P, 4, KT * 256], stack=own)
            c_col = sb("c_col", [P, KT], stack=own)
        with ExitStack() as own:
            g_hi = sb("g_hi", [P, HALF, S], F32R, stack=own)
            g_lo = sb("g_lo", [P, HALF, S], F32R, stack=own)
            cv = sb("cv", [P, 2, 2, S], stack=own)
            sg = sb("sg", [P, 2, S], stack=own)
            gf = sb("gf", [P, 2, S], stack=own)
        with ExitStack() as own:
            out_rows = sb("out_rows", [P, TT, D], stack=own)
        with ExitStack() as own:
            sq = sb("sq", [P, CQ + CKV, S], stack=own)
            c_hi = sb("c_hi", [P, CQ + CKV, S], F32R, stack=own)
            c_lo = sb("c_lo", [P, CQ + CKV, S], F32R, stack=own)
            rope = sb("rope", [ROPE, 2, S], stack=own)
            k_rope = sb("k_rope", [ROPE, S], stack=own)
            swapped = sb("swapped", [ROPE, 2, S], stack=own)
            rs_kv = sb("rs_kv", [P, S], stack=own)
            with ExitStack() as part:
                q_nope = sb("q_nope", [P, 2, S], stack=part)
                q_rope = sb("q_rope", [ROPE, 2, S], stack=part)
                k_nope = sb("k_nope", [P, 2, S], stack=part)
                v_tok = sb("v_tok", [P, 2, S], stack=part)
                m_probs = sb("m_probs", [P, 2, TRI], stack=part)
                m_turned = sb("m_turned", [P, 2, TRI], stack=part)
        neg_max = sb("neg_max", [P, 2, TT])
        row_sum = sb("row_sum", [P, 2, TT])
        factor = sb("factor", [P, 2, TT])
        lat_summed, lat_rooted, c_made, c_high = sem("lat_summed"), sem("lat_rooted"), sem("c_made"), sem("c_high")
        mla_side = sem("mla_side")
        projected, fetched, roped = sem("projected"), sem("fetched"), sem("roped")
        scored, maxed, exped, factored, scaled = sem("scored"), sem("maxed"), sem("exped"), sem("factored"), sem("scaled")
        turned, pt_act, pt_dve = sem("turned"), sem("pt_act"), sem("pt_dve")
        valued, o_high, o_low = sem("valued"), sem("o_high"), sem("o_low")

        def score_tile(r, i):
            b, at = {3: (0, 0), 2: (1, 0), 1: (2, P), 0: (2, 0)}[i]
            return bank[:, 3 * r + b, at:at + P * (i + 1)]

        def turned_tile(r, j, i):
            b, at = min(j, 2), (i - j) * P + (2 * P if j == 3 else 0)
            return bank[:, 3 * r + b, at:at + P]
        with ExitStack() as own:
            kf = sb("kf", [P, 2 * GROUPS, S], stack=own)
            vt = sb("vt", [P, 2 * GROUPS, S], stack=own)
            kc_t = sb("kc_t", [P, GROUPS, NC], stack=own)
            vc_t = sb("vc_t", [NC, GROUPS, P], stack=own)
            gates = sb("gates", [P, TT, 3 * HEADS], stack=own)
            near_b = sb("near_b", [P, HEADS, FAR], stack=own)
            cmp_b = sb("cmp_b", [P, HEADS, TT, NC], stack=own)
            hid = sb("hid", [P, 2, 2, GROUPS * NC], stack=own)
            w2 = sb("w2", [P, 2, 2, P], stack=own)
            pe_rows = sb("pe_rows", [CB, 2, P], stack=own)
            pe_col = sb("pe_col", [P, 2, CB], stack=own)
            with ExitStack() as part:
                b_hi = sb("b_hi", [P, 2, CB, GROUPS, NC], F32R, stack=part)
                b_lo = sb("b_lo", [P, 2, CB, GROUPS, NC], F32R, stack=part)
                b_new = sb("b_new", [P, 2, CS, GROUPS, NC], stack=part)
                near_hot = sb("near_hot", [BUCKETS + 1, 3 * P], stack=part)
                far_hot = sb("far_hot", [BUCKETS + 1, 2 * S], stack=part)
                flip = sb("flip", [P, P], stack=part)
                rel = sb("rel", [HEADS, BUCKETS], stack=part)
                rel_t = sb("rel_t", [BUCKETS + 1, HEADS], stack=part)
                near_rows = sb("near_rows", [HEADS, 3 * P], stack=part)
                far_rows = sb("far_rows", [HEADS, 2 * S], stack=part)
            with ExitStack() as part:
                q_t = sb("q_t", [P, 2, S], stack=part)
                n_probs = sb("n_probs", [P, 2, TRI], stack=part)
                n_turned = sb("n_turned", [P, 2, TRI], stack=part)
                cmp_p = sb("cmp_p", [P, TT, NC], stack=part)
                cmp_t = sb("cmp_t", [NC, S], stack=part)
                o_hi = sb("o_hi", [P, KT, S], F32R, stack=part)
                o_lo = sb("o_lo", [P, KT, S], F32R, stack=part)
                cmp_max = sb("cmp_max", [P, TT], stack=part)
                cmp_sum = sb("cmp_sum", [P, TT], stack=part)
                cmp_f = sb("cmp_f", [P, TT], stack=part)
        near_back = hf[:, 4:8, :].rearrange("p k s -> p (k s)").rearrange("p (h n) -> p h n", h=HEADS)
        cmp_back = hf[0:NC, :, :]
        nsa_side, nsa_small, nsa_copied, b_made, b_high = (sem(n) for n in ("nsa_side", "nsa_small", "nsa_copied", "b_made", "b_high"))
        rows_out, rows_back, b_low = sem("rows_out"), sem("rows_back"), sem("b_low")
        cmp_scored, cmp_maxed, cmp_exped, cmp_scaled, cmp_turned = (sem(n) for n in ("cmp_scored", "cmp_maxed", "cmp_exped", "cmp_scaled", "cmp_turned"))
        bank7_free, q_ready, gates_in = sem("bank7_free"), sem("q_ready"), sem("gates_in")
        with ExitStack() as own:
            in_map = sb("in_map", [P, 2, KT, P], stack=own)
            out_map = sb("out_map", [P, 2, KT, 5 * P], stack=own)
            fine = sb("fine", [P, 2, ST, FINE], stack=own)
            coarse = sb("coarse", [P, 2, ST, COARSE], stack=own)
            decay = sb("decay", [P, ST], stack=own)
            with ExitStack() as part:
                small = sb("small", [P, 24, ST], stack=part)
                lam_rows = sb("lam_rows", [ST, 3, P], stack=part)
                dt_rows = sb("dt_rows", [ST, 2], stack=part)
                b_in = sb("b_in", [P, 2, ST, SI], stack=part)
                b_bar = sb("b_bar", [P, 2, ST, 2 * SI], stack=part)
                c_rows = sb("c_rows", [P, 2, KT, 2, SN], stack=part)
                work = sb("work", [P, 2, ST, SI], stack=part)
            with ExitStack() as part:
                turn_t = sb("turn_t", [P, 2, 2, S], stack=part)
                turn_w = sb("turn_w", [P, 2, S], stack=part)
                scan_w = sb("scan_w", [P, 4, S], stack=part)
                state_w = sb("state_w", [P, 2, 4, S], stack=part)
            with ExitStack() as part:
                sig = sb("sig", [P, 2, S], stack=part)
                gated = sb("gated", [P, 2, S], stack=part)
        s5_side, s5_small, s5_act, s5_dve = (sem(n) for n in ("s5_side", "s5_small", "s5_act", "s5_dve"))
        table_made, bu_made, bu_free, products_made, x_made, y_made = (
            sem(n) for n in ("table_made", "bu_made", "bu_free", "products_made", "x_made", "y_made"))
        products_used, s5_exp, s5_dve2, s5_ready = (sem(n) for n in ("products_used", "s5_exp", "s5_dve2", "s5_ready"))
        y_in, y_gelu, y_high, y_low, sig_made = (sem(n) for n in ("y_in", "y_gelu", "y_high", "y_low", "sig_made"))
        block = ctx.enter_context(nc.Block())

        plan, units, drains, norms = [], 0, 0, 0
        for l in LAYERS:
            kind = l % 3
            plan.append(("norm", l, 0, units, drains, norms))
            plan.append((("mla", "nsa", "s5")[kind], l, l // 3, units, drains, norms))
            units += units_of(l)
            drains += (DKV_UNITS + KT, 8 + 4 + 4 + 1 + KT, 2 * KT)[kind]
            plan.append(("norm", l, 1, units, drains, norms + 1))
            plan.append(("ffn", l, 0, units, drains, norms + 1))
            units += 2 * (2 * HALF + KT)
            drains += 2 * (2 * HALF + KT)
            norms += 2
        plan.append(("final", 0, 0, units, drains, norms))
        l_at = {l: n for n, l in enumerate(LAYERS)}
        mla_at, passes_at, heads_at, a, b, c = {}, {}, {}, 0, 0, 0
        for l in LAYERS:
            mla_at[l], passes_at[l], heads_at[l] = a, b, c
            a, b, c = a + (l % 3 == 0), b + (HEADS, 2 * HEADS, 0)[l % 3], c + (HEADS, HEADS, 0)[l % 3]

        def mod_col(l, part, m):
            return l * MODS + part * KT + m

        def end_phase(eng, state):
            state[0] += 1
            eng.drain().then_inc(phase_end, 1)
            eng.wait_ge(phase_end, 4 * state[0])

        met = {}
        count = 1
        for entry in plan:
            met[entry[:3]] = 4 * count
            count += {"norm": 1, "mla": 3, "nsa": 5, "s5": 3, "ffn": 1, "final": 1}[entry[0]]

        def load_unit(sp, U, i, per, r, src, width):
            reached(sp, lo_made, i * per + (U + r - 1))
            dst = stage[:, (U + r) % 2, 0:width].rearrange("p (k m) -> p k m", m=src.shape[-1])
            sp.dma_start(dst, src).then_inc(landed[(U + r) % 2], 16)

        def split_high(act, U, i, per, r, width):
            s = (U + r) % 2
            act.wait_ge(landed[s], (i * (per // 2) + ((U + r) // 2 + 1)) * 16)
            reached(act, weights_used, i * per + (U + r - 1))
            nc.scalar.copy(w_hi[:, s, 0:width], stage[:, s, 0:width]).then_inc(hi_made, 1)

        def split_low(dve, U, i, per, r, width):
            s = (U + r) % 2
            dve.wait_ge(hi_made, i * per + (U + r + 1))
            nc.vector.tensor_tensor(w_lo[:, s, 0:width], stage[:, s, 0:width], w_hi[:, s, 0:width].bitcast(F32),
                                    ALU.subtract).then_inc(lo_made, 1)

        def three(dst, a_hi, a_lo, b_hi, b_lo, first, last):
            nc.tensor.matmul(dst, a_hi, b_hi, start=first, stop=False)
            nc.tensor.matmul(dst, a_hi, b_lo, start=False, stop=False)
            return nc.tensor.matmul(dst, a_lo, b_hi, start=False, stop=last)

        def feature_product(dst, s, k_tiles, stride, at, r_hi, r_lo):
            for k in range(k_tiles):
                a_hi = w_hi[:, s, k * stride + at:k * stride + at + P]
                a_lo = w_lo[:, s, k * stride + at:k * stride + at + P]
                last = three(dst, a_hi, a_lo, r_hi[:, k, :], r_lo[:, k, :], k == 0, k == k_tiles - 1)
            return last

        def token_product(dst, s, k_tiles, stride, at, m, a_hi, a_lo):
            for tt in range(TT):
                for k in range(k_tiles):
                    last = three(dst[:, tt * m:(tt + 1) * m], a_hi[:, k, tt * P:(tt + 1) * P], a_lo[:, k, tt * P:(tt + 1) * P],
                                 w_hi[:, s, k * stride + at:k * stride + at + m],
                                 w_lo[:, s, k * stride + at:k * stride + at + m], k == 0, k == k_tiles - 1)
            return last

        def w_view(w):
            return w.rearrange("(k p) m -> p k m", p=P)

        ab = t["ada_b"].rearrange("l (r f) -> (l r) f", f=P)
        cwr = t["ffn_conv_w"].rearrange("l w (c f) -> (l w c) f", f=P)
        cbr = t["ffn_conv_b"].rearrange("l (c f) -> (l c) f", f=P)
        row_loads = [(0, 0, ab[0:96]), (1, 0, ab[96:192])]
        row_loads += [(3 + g, 0, cwr[CW_ROWS * g:CW_ROWS * (g + 1)]) for g in range(6)]
        row_loads += [(9 + g, 0, cbr[CB_ROWS * g:CB_ROWS * (g + 1)]) for g in range(2)]
        row_loads += [(11, 0, t["c"].rearrange("b (r f) -> (b r) f", f=P))]
        for key, name in (("norm1", "norm1_g"), ("norm2", "norm2_g"), ("gq", "mla_g_q"), ("gkv", "mla_g_kv")):
            row_loads.append((2, NORM_COLS[key], t[name].rearrange("l (r f) -> (l r) f", f=P)))
        row_loads.append((2, NORM_COLS["final"], t["final_g"].rearrange("(r f) -> r f", f=P)))
        row_loads.append((2, NORM_COLS["d"], t["s5_d"].rearrange("n (r g) i -> (n r) (g i)", g=P // SI)))
        turns = [(0, AB_ROWS, mod, 0), (1, AB_ROWS, mod, AB_ROWS), (2, MISC_ROWS, misc, 0)]
        turns += [(3 + g, CW_ROWS, cw, CW_ROWS * g) for g in range(6)]
        turns += [(9 + g, CB_ROWS, cb, CB_ROWS * g) for g in range(2)]
        turns += [(11, KT, c_col, 0)]
        N_TURN = len(turns)
        x_view = t["x"].rearrange("b (t p) f -> p (b t) f", p=P)
        ADA_PIECES = MODS * P // 256
        ADA_TRIPS = ADA_PIECES // 4

        @block.sync
        def _(sp):
            for slot, at, src in row_loads:
                sp.dma_start(rows[at:at + src.shape[0], slot, :], src).then_inc(params_in, 16)
            sp.dma_start(x_rows[:], x_view).then_inc(params_in, 16)
            for dst, name in ((ident, "ident"), (mask, "mask")):
                sp.dma_start(dst[:], t[name]).then_inc(consts_in, 16)
            for l in range(DEPTH):
                view = w_view(t["ada_w"][l])
                with sp.Fori(0, ADA_TRIPS) as i:
                    for s in range(4):
                        sp.wait_ge(ada_used, i * 4 + (l * ADA_PIECES + s + 1))
                        sp.dma_start(ada_w[:, s, :].rearrange("p (k m) -> p k m", m=256),
                                     view[:, :, bass.ds((i * 4 + s) * 256, 256)]).then_inc(ada_in[s], 16)
            for name, l, j, U, _, _ in plan:
                if name == "ffn":
                    up, down = w_view(t["ffn_w_up"][l]), t["ffn_w_down"][l].rearrange("(k p) m -> p k m", p=P)
                    for half in range(2):
                        V = U + half * (2 * HALF + KT)

                        def up_pair(i, r):
                            for e in range(2):
                                load_unit(sp, V, i, 4, 2 * r + e,
                                          up[:, :, bass.ds((i * 2 + r) * P + (e * FF + half * HALF * P), P)], KT * P)

                        def down_unit(i, r):
                            load_unit(sp, V + 2 * HALF, i, 2, r,
                                      down[:, half * HALF:(half + 1) * HALF, bass.ds((i * 2 + r) * P, P)], UNIT)

                        repeat(sp, 5, 2, HALF, up_pair)
                        repeat(sp, 4, 2, KT, down_unit)
                if name == "mla":
                    dkv, uq, ukv, wo = (w_view(t[n][j]) for n in ("mla_w_dkv", "mla_w_uq", "mla_w_ukv", "mla_w_o"))
                    for n in range(DKV_UNITS):
                        c = min(n * P, Q_LORA + KV_LORA + ROPE - P)
                        load_unit(sp, U, 0, 2, n, dkv[:, :, c:c + P], KT * P)
                    W = U + DKV_UNITS

                    def head_units(i, r):
                        load_unit(sp, W, i, 4, 2 * r, uq[:, :, bass.ds((i * 2 + r) * QK, QK)], CQ * QK)
                        load_unit(sp, W, i, 4, 2 * r + 1, ukv[:, :, bass.ds((i * 2 + r) * 2 * P, 2 * P)], CKV * 2 * P)

                    repeat(sp, 4, 2, HEADS, head_units)
                    V = W + 2 * HEADS
                    repeat(sp, 4, 2, KT, lambda i, r: load_unit(sp, V, i, 2, r, wo[:, :, bass.ds((i * 2 + r) * P, P)], KT * P))
                if name == "nsa":
                    w_in, wo = w_view(t["nsa_w_in"][j]), w_view(t["nsa_w_o"][j])
                    first = NSA_COL["kc"]
                    repeat(sp, 2, 2, 4, lambda i, r: load_unit(sp, U, i, 2, r, w_in[:, :, bass.ds((i * 2 + r) * P + first, P)], KT * P))
                    for w, w1 in enumerate(("nsa_w1_k", "nsa_w1_v")):
                        w1 = w_view(t[w1][j])
                        for hh in range(2):
                            repeat(sp, 2, 2, 4, lambda i, r: load_unit(
                                sp, U + 4 + 8 * w + 4 * hh, i, 2, r,
                                w1[:, bass.ds((i * 2 + r) * KT, KT), hh * P:(hh + 1) * P], KT * P))
                    for n, key in enumerate(("ks", "kw", "vs", "vw")):
                        for g in range(GROUPS):
                            c = NSA_COL[key] + g * P
                            load_unit(sp, U + 20, 0, 2, 2 * n + g, w_in[:, :, c:c + P], KT * P)
                    load_unit(sp, U + 28, 0, 2, 0, w_in[:, :, NSA_COL["gate"]:], KT * 3 * HEADS)
                    repeat(sp, 4, 2, HEADS, lambda i, r: load_unit(sp, U + 29, i, 2, r, w_in[:, :, bass.ds((i * 2 + r) * P, P)], KT * P))
                    V = U + 29 + HEADS
                    repeat(sp, 4, 2, KT, lambda i, r: load_unit(sp, V, i, 2, r, wo[:, :, bass.ds((i * 2 + r) * P, P)], KT * P))
                if name == "s5":
                    glu = w_view(t["s5_w_glu"][j])

                    def glu_pair(i, r):
                        for e in range(2):
                            load_unit(sp, U, i, 4, 2 * r + e, glu[:, :, bass.ds((i * 2 + r) * P + e * D, P)], KT * P)

                    repeat(sp, 4, 2, KT, glu_pair)
            sp.wait_ge(copied_in, N_TURN + KT + KT)
            sp.dma_start(out.rearrange("b (t p) f -> p (b t) f", p=P), out_rows[:]).then_inc(stored, 16)
            sp.wait_ge(stored, 16)

        @block.tensor
        def _(pe):
            state = [0]
            pe.wait_ge(params_in, 16 * (len(row_loads) + 1))
            pe.wait_ge(consts_in, 32)
            for n, (slot, size, _, _) in enumerate(turns):
                reached(pe, copied_in, n - 3)
                nc.tensor.transpose(bank[:, n % 4, 0:size], rows[0:size, slot, :], ident[0:size, 0:size]).then_inc(turned_in, 1)
            for k in range(KT):
                reached(pe, copied_in, N_TURN + k - 3)
                for tt in range(TT):
                    last = nc.tensor.transpose(bank[:, (N_TURN + k) % 4, tt * P:(tt + 1) * P],
                                               x_rows[:, tt, k * P:(k + 1) * P], ident[:, :])
                last.then_inc(turned_in, 1)
            pe.wait_ge(silu_made, 1)
            for l in range(DEPTH):
                with pe.Fori(0, ADA_TRIPS) as i:
                    for s in range(4):
                        pe.wait_ge(ada_in[s], (i + (l * ADA_TRIPS + 1)) * 16)
                        for f in range(2):
                            for k in range(KT):
                                last = nc.tensor.matmul(bank[:, 4, bass.ds(i * 8 + (l * MODS + s * 2 + f), 1)],
                                                        ada_w[:, s, k * 256 + f * P:k * 256 + (f + 1) * P],
                                                        c_col[:, k:k + 1], start=(k == 0), stop=(k == KT - 1))
                        last.then_inc(ada_used, 1)
            end_phase(pe, state)

            def norm(l, which, idx):
                for k in range(KT):
                    pe.wait_ge(squares, KT * idx + k + 1)
                    last = nc.tensor.matmul(bank[:, 7, :], ones[:, :], hf[:, k, :], start=(k == 0), stop=(k == KT - 1))
                last.then_inc(summed, 1)

            def ffn(l, U, drains):
                for half in range(2):
                    V, G = U + half * (2 * HALF + KT), drains + half * (2 * HALF + KT)

                    def up_pair(i, r):
                        for e in range(2):
                            u = 2 * r + e
                            pe.wait_ge(lo_made, i * 4 + (V + u + 1))
                            reached(pe, drained, i * 4 + (G + u - 3))
                            feature_product(bank[:, u, :], (V + u) % 2, KT, P, 0, h_hi, h_lo).then_inc(weights_used, 1)

                    def down_unit(i, r):
                        W = V + 2 * HALF
                        pe.wait_ge(lo_made, i * 2 + (W + r + 1))
                        reached(pe, drained, i * 2 + (G + 2 * HALF + r - 1))
                        feature_product(bank[:, 4 + r, :], (W + r) % 2, HALF, P, 0, g_hi, g_lo).then_inc(weights_used, 1)

                    repeat(pe, 5, 2, HALF, up_pair)
                    pe.wait_ge(g_low, HALF * (2 * l_at[l] + half + 1))
                    repeat(pe, 4, 2, KT, down_unit)

            def output_projection(U, G, a_hi, a_lo):
                def unit(i, r):
                    pe.wait_ge(lo_made, i * 2 + (U + r + 1))
                    pe.wait_ge(drained, i * 2 + (G + r - 1))
                    feature_product(bank[:, r, :], (U + r) % 2, KT, P, 0, a_hi, a_lo).then_inc(weights_used, 1)

                repeat(pe, 4, 2, KT, unit)

            def turn(p, r, probs):
                pe.wait_ge(scaled, p + 1)
                for j in range(TT):
                    for i in range(j, TT):
                        last = nc.tensor.transpose(turned_tile(r, j, i), probs[:, r, ROW_AT[i] + j * P:ROW_AT[i] + (j + 1) * P],
                                                   ident[:, :])
                last.then_inc(turned, 1)

            def values(p, r, turned_sb, v, first, last):
                pe.wait_ge(pt_act, p + 3)
                pe.wait_ge(pt_dve, p + 3)
                for j in range(TT):
                    ins = nc.tensor.matmul(bank[:, 6, j * P:S], v[:, j * P:(j + 1) * P],
                                           turned_sb[:, r, COL_AT[j]:COL_AT[j] + S - j * P],
                                           start=first and j == 0, stop=last and j == TT - 1, skip_group_check=True)
                return ins

            def mla(l, j, U, dr, state):
                o = mla_at[l]
                for n in range(DKV_UNITS):
                    pe.wait_ge(lo_made, U + n + 1)
                    reached(pe, drained, dr + n - 1)
                    feature_product(bank[:, n % 2, :], (U + n) % 2, KT, P, 0, h_hi, h_lo).then_inc(weights_used, 1)
                for n in range(CQ + CKV):
                    pe.wait_ge(drained, dr + n + 1)
                    last = nc.tensor.matmul(bank[:, 4 if n < CQ else 5, :], ones[:, :], sq[:, n, :],
                                            start=n in (0, CQ), stop=n in (CQ - 1, CQ + CKV - 1))
                    if n in (CQ - 1, CQ + CKV - 1):
                        last.then_inc(lat_summed, 1)
                end_phase(pe, state)
                W, pb = U + DKV_UNITS, passes_at[l]

                def project(i, r):
                    s, c = r % 2, 4 * (HEADS * o + r)
                    pe.wait_ge(lo_made, i * 4 + (W + 2 * r + 1))
                    reached(pe, fetched, i * 8 + c)
                    feature_product(bank[:, 7, :], W % 2, CQ, QK, 0, c_hi, c_lo).then_inc(projected, 1)
                    pe.wait_ge(fetched, i * 8 + (c + 1))
                    feature_product(bank[:, 7, :], W % 2, CQ, QK, QK - P, c_hi, c_lo).then_inc(weights_used, 1)
                    pe.wait_ge(lo_made, i * 4 + (W + 2 * r + 2))
                    pe.wait_ge(fetched, i * 8 + (c + 2))
                    feature_product(bank[:, 7, :], (W + 1) % 2, CKV, 2 * P, 0, c_hi[:, CQ:], c_lo[:, CQ:]).then_inc(projected, 1)
                    pe.wait_ge(fetched, i * 8 + (c + 3))
                    token_product(bank[:, 7, :], (W + 1) % 2, CKV, 2 * P, P, P, c_hi[:, CQ:], c_lo[:, CQ:]) \
                        .then_inc(weights_used, 1)

                def scores(i, r):
                    s = r % 2
                    pe.wait_ge(fetched, i * 8 + 4 * (HEADS * o + r + 1))
                    pe.wait_ge(roped, i * 2 + (HEADS * o + r + 1))
                    pe.wait_ge(pt_act, i * 2 + (pb + r + 1))
                    pe.wait_ge(pt_dve, i * 2 + (pb + r + 1))
                    for q in reversed(range(TT)):
                        at, n = slice(q * P, (q + 1) * P), P * (q + 1)
                        nc.tensor.matmul(score_tile(s, q), q_nope[:, s, at], k_nope[:, s, 0:n], start=True, stop=False)
                        nc.tensor.matmul(score_tile(s, q), q_rope[:, s, at], k_rope[:, 0:n], start=False, stop=False)
                        last = nc.tensor.matmul(score_tile(s, q)[:, n - P:n], ident_b[:, :], mask_b[:, :], start=False, stop=True)
                    last.then_inc(scored, 1)

                def head(i, r):
                    s = r % 2
                    whole = not isinstance(i, int)
                    if whole or 2 * i + r + 1 < HEADS:
                        scores(i, r + 1)
                    turn(i * 2 + (pb + r), s, m_probs)
                    pe.wait_ge(o_low, i * 2 + (heads_at[l] + r + 1))
                    values(i * 2 + (pb + r), s, m_turned, v_tok[:, s, :], True, True).then_inc(valued, 1)
                    if whole or 2 * i + r + 2 < HEADS:
                        project(i, r + 2)

                project(0, 0)
                scores(0, 0)
                project(0, 1)
                repeat(pe, 3, 2, HEADS, head)
                end_phase(pe, state)
                output_projection(W + 2 * HEADS, dr + DKV_UNITS, h_hi, h_lo)
            def nsa(l, j, U, dr, state):
                for n in range(4):
                    pe.wait_ge(lo_made, U + n + 1)
                    reached(pe, drained, dr + n - 1)
                    feature_product(bank[:, n % 2, :], (U + n) % 2, KT, P, 0, h_hi, h_lo).then_inc(weights_used, 1)
                pe.wait_ge(nsa_side, 16 * 8)
                for w in range(2):
                    nc.tensor.transpose(bank[:, 4, w * CB:(w + 1) * CB], pe_rows[:, w, :], ident[0:CB, 0:CB])
                nc.tensor.transpose(bank[0:BUCKETS, 5, 0:HEADS], rel[:, :], ident[0:HEADS, 0:HEADS]).then_inc(nsa_small, 1)
                pe.wait_ge(nsa_copied, 1)
                nc.tensor.matmul(bank[0:HEADS, 6, 0:3 * P], rel_t[:, :], near_hot[:, :], start=True, stop=True)
                for w in range(2):
                    last = nc.tensor.matmul(bank[0:HEADS, 2 + w, :], rel_t[:, :], far_hot[:, w * S:(w + 1) * S], start=True, stop=True)
                last.then_inc(nsa_small, 1)
                end_phase(pe, state)
                for w in range(2):
                    for hh in range(2):
                        n = 2 * w + hh
                        for q in range(4):
                            s = (U + 4 + 4 * n + q) % 2
                            pe.wait_ge(lo_made, U + 4 + 4 * n + q + 1)
                            if q == 0:
                                pe.wait_ge(drained, dr + 4 + n - 1)
                            for c in range(KT):
                                at = slice(c * P, (c + 1) * P)
                                last = three(bank[:, n % 2, 0:GROUPS * NC], w_hi[:, s, at], w_lo[:, s, at],
                                             b_hi[:, w, q * KT + c, :, :], b_lo[:, w, q * KT + c, :, :],
                                             q == 0 and c == 0, q == 3 and c == KT - 1)
                            last.then_inc(weights_used, 1)
                pe.wait_ge(drained, dr + 8)
                for hh in range(2):
                    nc.tensor.matmul(bank[:, 4, 0:GROUPS * NC], w2[:, 0, hh, :], hid[:, 0, hh, :], start=hh == 0, stop=hh == 1)
                for g in range(GROUPS):
                    for hh in range(2):
                        last = nc.tensor.matmul(bank[0:NC, 5, g * P:(g + 1) * P], hid[:, 1, hh, g * NC:(g + 1) * NC], w2[:, 1, hh, :],
                                                start=hh == 0, stop=hh == 1)
                last.then_inc(nsa_small, 1)
                end_phase(pe, state)
                for n in range(9):
                    pe.wait_ge(lo_made, U + 20 + n + 1)
                    pe.wait_ge(drained, dr + 8 + n - 1)
                    s, b = (U + 20 + n) % 2, bank[:, n % 2, :]
                    if n < 4:
                        last = feature_product(b, s, KT, P, 0, h_hi, h_lo)
                    elif n < 8:
                        last = token_product(b, s, KT, P, 0, P, h_hi, h_lo)
                    else:
                        last = token_product(b, s, KT, 3 * HEADS, 0, 3 * HEADS, h_hi, h_lo)
                    last.then_inc(weights_used, 1)
                pe.wait_ge(rows_back, 16)
                for n in range(4):
                    last = nc.tensor.matmul(bank[:, 2 + n, :], flip[:, :], near_back[:, 2 * n:2 * n + 2, :], start=True, stop=True)
                last.then_inc(nsa_small, 1)
                pe.wait_ge(nsa_copied, 3)
                pe.wait_ge(rows_back, 32)
                for tt in range(TT):
                    for h in range(HEADS):
                        last = nc.tensor.matmul(bank[:, 2 + tt, h * NC:(h + 1) * NC], cmp_back[:, h, tt * P:(tt + 1) * P],
                                                flip[0:NC, P - NC:P], start=True, stop=True)
                last.then_inc(nsa_small, 1)
                end_phase(pe, state)

                W, pb, hb = U + 29, passes_at[l], heads_at[l]

                def project(h):
                    pe.wait_ge(lo_made, W + h + 1)
                    reached(pe, bank7_free, 3 * h)
                    feature_product(bank[:, 7, :], (W + h) % 2, KT, P, 0, h_hi, h_lo).then_inc(weights_used, 1)

                def scores(h, w):
                    pe.wait_ge(q_ready, h + 1)
                    p = pb + 2 * h + w
                    pe.wait_ge(pt_act, p + 1)
                    pe.wait_ge(pt_dve, p + 1)
                    for q in reversed(range(TT)):
                        last = nc.tensor.matmul(score_tile(w, q), q_t[:, h % 2, q * P:(q + 1) * P],
                                                kf[:, 2 * w + h // HPG, 0:P * (q + 1)], start=True, stop=True)
                    last.then_inc(scored, 1)

                project(0)
                scores(0, 0)
                for h in range(HEADS):
                    g = h // HPG
                    pe.wait_ge(bank7_free, 3 * h + 1)
                    for q in range(TT):
                        last = nc.tensor.matmul(bank[:, 7, q * NC:(q + 1) * NC], q_t[:, h % 2, q * P:(q + 1) * P], kc_t[:, g, :],
                                                start=True, stop=True)
                    last.then_inc(cmp_scored, 1)
                    scores(h, 1)
                    turn(pb + 2 * h, 0, n_probs)
                    pe.wait_ge(o_low, hb + h + 1)
                    values(pb + 2 * h, 0, n_turned, vt[:, g, :], True, False)
                    pe.wait_ge(cmp_scaled, h + 1)
                    for q in range(TT):
                        last = nc.tensor.transpose(bank[0:NC, 7, q * P:(q + 1) * P], cmp_p[:, q, :], ident[:, :])
                    last.then_inc(cmp_turned, 1)
                    pe.wait_ge(bank7_free, 3 * h + 3)
                    nc.tensor.matmul(bank[:, 6, :], vc_t[:, g, :], cmp_t[:, :], start=False, stop=False, skip_group_check=True)
                    if h + 1 < HEADS:
                        project(h + 1)
                        scores(h + 1, 0)
                    turn(pb + 2 * h + 1, 1, n_probs)
                    values(pb + 2 * h + 1, 1, n_turned, vt[:, GROUPS + g, :], False, True).then_inc(valued, 1)
                end_phase(pe, state)
                output_projection(W + HEADS, dr + 17, o_hi, o_lo)
            def s5(l, j, U, dr, state):
                pe.wait_ge(s5_side, 16 * 9)
                pe.wait_ge(s5_dve, 1)
                for n in range(3):
                    last = nc.tensor.transpose(bank[:, 0, n * ST:(n + 1) * ST], lam_rows[:, n, :], ident[0:ST, 0:ST])
                last.then_inc(s5_small, 1)
                for k in range(KT):
                    for w in range(2):
                        n = 2 * k + w
                        reached(pe, s5_act, n - 1)
                        nc.tensor.transpose(bank[:, 1 + n % 2, 0:P], c_rows[:, w, k, :, :], ident[:, :]).then_inc(s5_small, 1)
                pe.wait_ge(s5_dve, 2)
                for k in range(KT):
                    for w in range(2):
                        n = 2 * k + w
                        pe.wait_ge(s5_act, 16 + n - 1)
                        nc.tensor.transpose(bank[:, 1 + n % 2, 0:P], b_bar[:, w, 4 * k:4 * k + 4, :], ident[:, :]).then_inc(s5_small, 1)
                end_phase(pe, state)

                def enter(q):
                    k, a, r = q // 4, 32 * (q % 4), q % 2
                    reached(pe, bu_free, q - 1)
                    for w in range(2):
                        last = nc.tensor.matmul(bank[:, 2 * r + w, :], in_map[a:a + 32, w, k, :], hf[a:a + 32, k, :],
                                                start=True, stop=True)
                    last.then_inc(bu_made, 1)

                enter(0)
                enter(1)
                for q in range(ST):
                    k, a, r = q // 4, q % 4, q % 2
                    if q + 2 < ST:
                        enter(q + 2)
                    pe.wait_ge(x_made, q + 1)
                    if a == 0:
                        reached(pe, y_in, k - 1)
                    for w in range(2):
                        last = nc.tensor.matmul(bank[:, 4 + k % 2, :], out_map[:, w, k, a * P:(a + 1) * P], state_w[:, r, 2 * w, :],
                                                start=(a == 0 and w == 0), stop=(a == 3 and w == 1))
                    if a == 3:
                        last.then_inc(y_made, 1)
                    else:
                        last.then_inc(products_used, 1)
                end_phase(pe, state)

                def glu_pair(i, r):
                    for e in range(2):
                        u = 2 * r + e
                        pe.wait_ge(lo_made, i * 4 + (U + u + 1))
                        reached(pe, drained, i * 4 + (dr + 2 * r - 2))
                        feature_product(bank[:, u, :], (U + u) % 2, KT, P, 0, h_hi, h_lo).then_inc(weights_used, 1)

                repeat(pe, 4, 2, KT, glu_pair)
            for name, l, j, U, dr, idx in plan:
                if name == "norm":
                    norm(l, j, idx + 0)
                elif name == "mla":
                    mla(l, j, U, dr, state)
                elif name == "nsa":
                    nsa(l, j, U, dr, state)
                elif name == "s5":
                    s5(l, j, U, dr, state)
                elif name == "ffn":
                    ffn(l, U, dr)
                else:
                    norm(0, 2, idx)
                    for k in range(KT):
                        pe.wait_ge(h_made, KT * (idx + 1))
                        reached(pe, copied_in, N_TURN + KT + k - 1)
                        for tt in range(TT):
                            last = nc.tensor.transpose(bank[:, 4 + k % 2, tt * P:(tt + 1) * P],
                                                       hf[:, k, tt * P:(tt + 1) * P], ident[:, :])
                        last.then_inc(turned_in, 1)
                end_phase(pe, state)

        @block.scalar
        def _(act):
            state, chain = [0], Chain(act, act_chain)
            act.wait_ge(copied_in, N_TURN)
            nc.scalar.activation(c_col[:, :], c_col[:, :], ACT.Silu).then_inc(silu_made, 1)
            end_phase(act, state)

            def norm(idx, split):
                for k in range(KT):
                    nc.scalar.activation(hf[:, k, :], x[:, k, :], ACT.Square).then_inc(squares, 1)
                act.wait_ge(summed, idx + 1)
                nc.scalar.activation(rs[:, :], bank[:, 7, :], ACT.Sqrt, bias=eps[:, :], scale=1.0 / D).then_inc(rooted, 1)
                for k in range(KT if split else 0):
                    act.wait_ge(h_made, KT * idx + k + 1)
                    nc.scalar.copy(h_hi[:, k, :], hf[:, k, :]).then_inc(h_high, 1)

            def ffn(l, U, drains):
                for half in range(2):
                    V, G = U + half * (2 * HALF + KT), drains + half * (2 * HALF + KT)
                    Q = HALF * (2 * l_at[l] + half)
                    nc.scalar.preload_act_table(ACT.Silu)
                    for e in range(2):
                        split_high(act, V, 0, 4, e, KT * P)

                    def up_pair(i, r):
                        if not (isinstance(i, int) and 2 * i + r + 1 >= HALF):
                            for e in range(2):
                                split_high(act, V, i, 4, 2 * (r + 1) + e, KT * P)
                        act.wait_ge(g_made, i * 2 + (Q + r + 1))
                        for e in range(2):
                            u, col = 2 * r + e, l * CHT + e * PAIRS + half * HALF
                            act.wait_ge(weights_used, i * 4 + (V + u + 1))
                            nc.scalar.activation(cv[:, r, e, :], bank[:, u, :], ACT.Identity,
                                                 bias=cb[:, bass.ds(i * 2 + (col + r), 1)],
                                                 scale=cw[:, bass.ds(i * 2 + ((TAPS * l + 2) * CHT + col - l * CHT + r), 1)]
                                                 ).then_inc(cv_made, 1)
                        act.wait_ge(drained, i * 4 + (G + 2 * r + 2))
                        nc.scalar.activation(sg[:, r, :], cv[:, r, 1, :], ACT.Silu).then_inc(silu_made, 1)
                        act.wait_ge(g_made, i * 2 + (Q + r + 3))
                        nc.scalar.copy(g_hi[:, bass.ds(i * 2 + r, 1), :], gf[:, r:r + 1, :]).then_inc(g_high, 1)

                    repeat(act, 5, 2, HALF, up_pair)
                    W = V + 2 * HALF
                    for n in range(KT):
                        split_high(act, W, 0, 2, n, UNIT)

            def output_splits(U):
                for n in range(KT):
                    split_high(act, U, 0, 2, n, KT * P)

            def exponents(p, r, probs):
                act.wait_ge(maxed, p + 1)
                for q in reversed(range(TT)):
                    last = nc.scalar.activation(probs[:, r, ROW_AT[q]:ROW_AT[q] + P * (q + 1)], score_tile(r, q), ACT.Exp,
                                                bias=neg_max[:, r, q:q + 1], accum_out=row_sum[:, r, q:q + 1])
                last.then_inc(exped, 1)

            def copy_turned(p, r, turned_sb):
                act.wait_ge(turned, p + 1)
                nc.scalar.copy(turned_sb[:, r, 0:S], bank[:, 3 * r, :]).then_inc(pt_act, 1)

            def head_high(h, m, dst):
                act.wait_ge(valued, h + 1)
                nc.scalar.copy(dst[:, m, :] if isinstance(m, int) else dst[:, bass.ds(m, 1), :].squeeze(1), bank[:, 6, :]) \
                    .then_inc(o_high, 1)

            def mla(l, j, U, dr, state):
                o = mla_at[l]
                split_high(act, U, 0, 2, 0, KT * P)
                for n in range(DKV_UNITS):
                    if n + 1 < DKV_UNITS:
                        split_high(act, U, 0, 2, n + 1, KT * P)
                    act.wait_ge(weights_used, U + n + 1)
                    b = bank[:, n % 2, :]
                    if n < CQ + CKV:
                        nc.scalar.copy(hf[:, n, :], b)
                        nc.scalar.activation(sq[:, n, :], b, ACT.Square).then_inc(drained, 1)
                    else:
                        half = ROPE // 2
                        nc.scalar.copy(k_rope[:, :], b[ROPE:P])
                        nc.scalar.copy(swapped[0:half, 0, :], b[P - half:P])
                        nc.scalar.copy(swapped[half:ROPE, 0, :], b[ROPE:P - half]).then_inc(drained, 1)
                for b, dst, count in ((4, rs, Q_LORA), (5, rs_kv, KV_LORA)):
                    act.wait_ge(lat_summed, 2 * o + b - 3)
                    nc.scalar.activation(dst[:, :], bank[:, b, :], ACT.Sqrt, bias=eps[:, :], scale=1.0 / count).then_inc(lat_rooted, 1)
                for n in range(CQ + CKV):
                    act.wait_ge(c_made, 6 * o + n + 1)
                    nc.scalar.copy(c_hi[:, n, :], hf[:, n, :]).then_inc(c_high, 1)
                end_phase(act, state)
                W, pb = U + DKV_UNITS, passes_at[l]

                def splits(i, r):
                    split_high(act, W, i, 4, 2 * r, CQ * QK)
                    split_high(act, W, i, 4, 2 * r + 1, CKV * 2 * P)

                def fetch(i, r):
                    s, c, half = r % 2, 4 * (HEADS * o + r), ROPE // 2
                    act.wait_ge(projected, i * 4 + (2 * (HEADS * o + r) + 1))
                    nc.scalar.mul(q_nope[:, s, :], bank[:, 7, :], MLA_SCALE).then_inc(fetched, 1)
                    act.wait_ge(weights_used, i * 4 + (W + 2 * r + 1))
                    nc.scalar.mul(q_rope[:, s, :], bank[ROPE:P, 7, :], MLA_SCALE)
                    nc.scalar.mul(swapped[0:half, s, :], bank[P - half:P, 7, :], MLA_SCALE)
                    nc.scalar.mul(swapped[half:ROPE, s, :], bank[ROPE:P - half, 7, :], MLA_SCALE).then_inc(fetched, 1)
                    act.wait_ge(fetched, i * 8 + (c + 3))
                    act.wait_ge(weights_used, i * 4 + (W + 2 * r + 2))
                    nc.scalar.copy(v_tok[:, s, :], bank[:, 7, :]).then_inc(fetched, 1)

                def head(i, r):
                    s, whole = r % 2, not isinstance(i, int)
                    if whole or 2 * i + r + 2 < HEADS:
                        splits(i, r + 2)
                    if whole or 2 * i + r + 1 < HEADS:
                        exponents(i * 2 + (pb + r + 1), 1 - s, m_probs)
                    copy_turned(i * 2 + (pb + r), s, m_turned)
                    head_high(i * 2 + (heads_at[l] + r), i * 2 + r, h_hi)
                    if whole or 2 * i + r + 2 < HEADS:
                        fetch(i, r + 2)

                splits(0, 0)
                fetch(0, 0)
                splits(0, 1)
                exponents(pb, 0, m_probs)
                fetch(0, 1)
                nc.scalar.preload_act_table(ACT.Exp)
                repeat(act, 3, 2, HEADS, head)
                end_phase(act, state)
                output_splits(W + 2 * HEADS)
            def nsa(l, j, U, dr, state):
                for n in range(4):
                    split_high(act, U, 0, 2, n, KT * P)
                for n in range(4):
                    act.wait_ge(b_made, n + 1)
                    nc.scalar.copy(b_hi[:, n // 2, (n % 2) * CS:(n % 2 + 1) * CS], b_new[:, n % 2]).then_inc(b_high, 1)
                end_phase(act, state)
                split_high(act, U + 4, 0, 2, 0, KT * P)
                for n in range(16):
                    if n + 1 < 16:
                        split_high(act, U + 4, 0, 2, n + 1, KT * P)
                    if n % 4 == 3:
                        act.wait_ge(weights_used, U + 4 + n + 1)
                        nc.scalar.activation(hid[:, n // 8, (n // 4) % 2, :], bank[:, (n // 4) % 2, 0:GROUPS * NC],
                                             ACT.Gelu_apprx_tanh).then_inc(drained, 1)
                end_phase(act, state)
                for n in range(9):
                    split_high(act, U + 20, 0, 2, n, KT * (P if n < 8 else 3 * HEADS))
                act.wait_ge(weights_used, U + 29)
                nc.scalar.activation(gates[:, :, :], bank[:, 0, 0:TT * 3 * HEADS], ACT.Sigmoid).then_inc(drained, 1)
                end_phase(act, state)
                W, pb, hb = U + 29, passes_at[l], heads_at[l]

                def fetch(h):
                    act.wait_ge(weights_used, W + h + 1)
                    nc.scalar.mul(q_t[:, h % 2, :], bank[:, 7, :], NSA_SCALE).then_inc(q_ready, 1)

                split_high(act, W, 0, 2, 0, KT * P)
                fetch(0)
                exponents(pb, 0, n_probs)
                for h in range(HEADS):
                    if h + 1 < HEADS:
                        split_high(act, W, 0, 2, h + 1, KT * P)
                    act.wait_ge(cmp_maxed, h + 1)
                    for q in range(TT):
                        last = nc.scalar.activation(cmp_p[:, q, :], cmp_p[:, q, :], ACT.Exp, bias=cmp_max[:, q:q + 1],
                                                    accum_out=cmp_sum[:, q:q + 1])
                    last.then_inc(cmp_exped, 1)
                    exponents(pb + 2 * h + 1, 1, n_probs)
                    copy_turned(pb + 2 * h, 0, n_turned)
                    act.wait_ge(cmp_turned, h + 1)
                    nc.scalar.copy(cmp_t[:, :], bank[0:NC, 7, :]).then_inc(bank7_free, 1)
                    if h + 1 < HEADS:
                        fetch(h + 1)
                        exponents(pb + 2 * h + 2, 0, n_probs)
                    copy_turned(pb + 2 * h + 1, 1, n_turned)
                    head_high(hb + h, h, o_hi)
                end_phase(act, state)
                output_splits(W + HEADS)
            def s5(l, j, U, dr, state):
                act.wait_ge(s5_ready, 1)
                nc.scalar.activation(small[:, 11, :], small[:, 11, :], ACT.Exp).then_inc(s5_exp, 1)
                for k in range(KT):
                    for w in range(2):
                        n = 2 * k + w
                        act.wait_ge(s5_small, 2 + n)
                        src = bank[:, 1 + n % 2, 0:P].rearrange("p (q i) -> p q i", q=4)
                        dst = out_map[:, w, k, 0:640].rearrange("p (q i) -> p q i", q=4)
                        nc.scalar.mul(dst[0:SN, :, 0:SI], src[0:SN, :, 0:SI], 1.0 - 2 * w)
                        nc.scalar.mul(dst[SN:P, :, SI:2 * SI], src[SN:P, :, SI:2 * SI], 1.0 - 2 * w).then_inc(s5_act, 1)
                act.wait_ge(s5_dve2, 1)
                nc.scalar.activation(small[:, 5, :], small[:, 3, :], ACT.Exp).then_inc(s5_exp, 1)
                nc.scalar.activation(small[:, 6, :], small[:, 4, :], ACT.Sin)
                nc.scalar.activation(small[:, 7, :], small[:, 4, :], ACT.Sin, scale=0.5).then_inc(s5_exp, 1)
                for n in range(2 * KT):
                    act.wait_ge(s5_small, 18 + n)
                    nc.scalar.copy(in_map[:, n % 2, n // 2, :], bank[:, 1 + n % 2, 0:P]).then_inc(s5_act, 1)
                end_phase(act, state)
                for k in range(KT):
                    act.wait_ge(y_in, k + 1)
                    nc.scalar.activation(hf[:, k, :], hf[:, k, :], ACT.Gelu_apprx_tanh).then_inc(y_gelu, 1)
                    act.wait_ge(y_gelu, k + 1)
                    nc.scalar.copy(h_hi[:, k, :], hf[:, k, :]).then_inc(y_high, 1)
                end_phase(act, state)
                for e in range(2):
                    split_high(act, U, 0, 4, e, KT * P)

                def glu_pair(i, r):
                    if not (isinstance(i, int) and 2 * i + r + 1 >= KT):
                        for e in range(2):
                            split_high(act, U, i, 4, 2 * (r + 1) + e, KT * P)
                    act.wait_ge(weights_used, i * 4 + (U + 2 * r + 2))
                    nc.scalar.activation(sig[:, r, :], bank[:, 2 * r + 1, :], ACT.Sigmoid).then_inc(sig_made, 1)

                nc.scalar.preload_act_table(ACT.Sigmoid)
                repeat(act, 3, 2, KT, glu_pair)
            for name, l, j, U, dr, idx in plan:
                if name == "norm":
                    norm(idx, True)
                elif name == "mla":
                    mla(l, j, U, dr, state)
                elif name == "nsa":
                    nsa(l, j, U, dr, state)
                elif name == "s5":
                    s5(l, j, U, dr, state)
                elif name == "ffn":
                    ffn(l, U, dr)
                else:
                    norm(idx, False)
                end_phase(act, state)

        @block.vector
        def _(dve):
            state, chain = [0], Chain(dve, dve_chain)
            chain.link(nc.vector.memset(ones[:, :], 1.0))
            chain.link(nc.vector.memset(eps[:, :], EPS))
            dve.wait_ge(consts_in, 32)
            chain.link(nc.vector.tensor_copy(ident_b[:, :], ident[:, :]))
            chain.link(nc.vector.tensor_copy(mask_b[:, :], mask[:, :]))
            for n, (slot, size, dst, col) in enumerate(turns):
                dve.wait_ge(turned_in, n + 1)
                nc.vector.tensor_copy(dst[:, col:col + size], bank[:, n % 4, 0:size]).then_inc(copied_in, 1)
            for k in range(KT):
                dve.wait_ge(turned_in, N_TURN + k + 1)
                nc.vector.tensor_copy(x[:, k, :], bank[:, (N_TURN + k) % 4, :]).then_inc(copied_in, 1)
            dve.wait_ge(ada_used, 4 + DEPTH * ADA_PIECES)
            dve.wait_ge(copied_in, N_TURN)
            chain.link(nc.vector.tensor_tensor(mod[:, :], bank[:, 4, 0:DEPTH * MODS], mod[:, :], ALU.add))
            for l in range(DEPTH):
                for w in range(2):
                    a = mod_col(l, 3 * w + 1, 0)
                    chain.step(nc.vector.scalar_tensor_tensor(
                        out=amp[:, (2 * l + w) * KT:(2 * l + w + 1) * KT], in0=mod[:, a:a + KT], scalar=1.0,
                        in1=misc[:, 32 * w + KT * l:32 * w + KT * (l + 1)], op0=ALU.add, op1=ALU.mult))
            end_phase(dve, state)

            def inverse_root(dst, count):
                dve.wait_ge(rooted, count)
                chain.link(nc.vector.reciprocal(dst, dst))

            def norm(l, which, idx):
                inverse_root(rs[:, :], idx + 1)
                for k in range(KT):
                    chain.step(nc.vector.tensor_tensor(hf[:, k, :], x[:, k, :], rs[:, :], ALU.mult))
                chain.wait()
                for k in range(KT):
                    if which == 2:
                        a = NORM_COLS["final"] + k
                        nc.vector.tensor_scalar(hf[:, k, :], hf[:, k, :], misc[:, a:a + 1], None, ALU.mult).then_inc(h_made, 1)
                    else:
                        a, b = (2 * l + which) * KT + k, mod_col(l, 3 * which, k)
                        nc.vector.tensor_scalar(hf[:, k, :], hf[:, k, :], amp[:, a:a + 1], mod[:, b:b + 1],
                                                ALU.mult, ALU.add).then_inc(h_made, 1)
                for k in range(0 if which == 2 else KT):
                    dve.wait_ge(h_high, KT * idx + k + 1)
                    dve.wait_ge(h_made, KT * idx + k + 1)
                    nc.vector.tensor_tensor(h_lo[:, k, :], hf[:, k, :], h_hi[:, k, :].bitcast(F32), ALU.subtract)

            def residual(l, part, m, src, mark):
                nc.vector.scalar_tensor_tensor(
                    out=x[:, bass.ds(m, 1), :].squeeze(1) if not isinstance(m, int) else x[:, m, :], in0=src,
                    scalar=mod[:, bass.ds(m + mod_col(l, part, 0), 1)],
                    in1=x[:, bass.ds(m, 1), :].squeeze(1) if not isinstance(m, int) else x[:, m, :],
                    op0=ALU.mult, op1=ALU.add).then_inc(mark, 1)

            def ffn(l, U, drains):
                for half in range(2):
                    V, G = U + half * (2 * HALF + KT), drains + half * (2 * HALF + KT)
                    Q = HALF * (2 * l_at[l] + half)
                    for e in range(2):
                        split_low(dve, V, 0, 4, e, KT * P)

                    def up_pair(i, r):
                        if not (isinstance(i, int) and 2 * i + r + 1 >= HALF):
                            for e in range(2):
                                split_low(dve, V, i, 4, 2 * (r + 1) + e, KT * P)
                        for tap in (1, 0):
                            back = 2 - tap
                            for e in range(2):
                                if tap == 1:
                                    dve.wait_ge(cv_made, i * 4 + (2 * Q + 2 * r + e + 1))
                                col = (TAPS * l + tap) * CHT + e * PAIRS + half * HALF
                                ins = nc.vector.scalar_tensor_tensor(
                                    out=cv[:, r, e, back:], in0=bank[:, 2 * r + e, 0:S - back],
                                    scalar=cw[:, bass.ds(i * 2 + (col + r), 1)], in1=cv[:, r, e, back:],
                                    op0=ALU.mult, op1=ALU.add)
                                if tap == 1:
                                    chain.step(ins)
                                else:
                                    ins.then_inc(drained, 1)
                            if tap == 1:
                                chain.wait()
                        dve.wait_ge(silu_made, i * 2 + (1 + Q + r + 1))
                        dve.wait_ge(drained, i * 4 + (G + 2 * r + 2))
                        nc.vector.tensor_tensor(gf[:, r, :], cv[:, r, 0, :], sg[:, r, :], ALU.mult).then_inc(g_made, 1)
                        dve.wait_ge(g_high, i * 2 + (Q + r + 1))
                        dve.wait_ge(g_made, i * 2 + (Q + r + 3))
                        nc.vector.tensor_tensor(g_lo[:, bass.ds(i * 2 + r, 1), :], gf[:, r:r + 1, :],
                                                g_hi[:, bass.ds(i * 2 + r, 1), :].bitcast(F32),
                                                ALU.subtract).then_inc(g_low, 1)

                    repeat(dve, 5, 2, HALF, up_pair, chain, 2)
                    W = V + 2 * HALF
                    split_low(dve, W, 0, 2, 0, UNIT)
                    for n in range(KT):
                        if n + 1 < KT:
                            split_low(dve, W, 0, 2, n + 1, UNIT)
                        dve.wait_ge(weights_used, W + n + 1)
                        residual(l, 5, n, bank[:, 4 + n % 2, :], drained)

            def output_residual(U, l):
                split_low(dve, U, 0, 2, 0, KT * P)
                for n in range(KT):
                    if n + 1 < KT:
                        split_low(dve, U, 0, 2, n + 1, KT * P)
                    dve.wait_ge(weights_used, U + n + 1)
                    residual(l, 2, n, bank[:, n % 2, :], drained)

            def maxima(p, r, bias=None):
                dve.wait_ge(scored, p + 1)
                if bias is not None:
                    for q in reversed(range(TT)):
                        n = P * (q + 1)
                        w = min(n, FAR)
                        dst = score_tile(r, q)[:, n - w:n]
                        chain.step(nc.vector.tensor_tensor(dst, dst, bias[:, FAR - w:FAR], ALU.add))
                    chain.wait()
                for q in reversed(range(TT)):
                    last = nc.vector.tensor_reduce(neg_max[:, r, q:q + 1], score_tile(r, q), AX, ALU.max, negate=True)
                last.then_inc(maxed, 1)

            def factors(p, r, gate=None):
                dve.wait_ge(exped, p + 1)
                chain.link(nc.vector.tensor_scalar(row_sum[:, r, :], row_sum[:, r, :], 1e-30, None, ALU.max))
                if gate is None:
                    nc.vector.reciprocal(factor[:, r, :], row_sum[:, r, :]).then_inc(factored, 1)
                else:
                    chain.link(nc.vector.reciprocal(factor[:, r, :], row_sum[:, r, :]))
                    nc.vector.tensor_tensor(factor[:, r, :], factor[:, r, :], gate, ALU.mult).then_inc(factored, 1)

            def copy_turned(p, r, turned_sb):
                dve.wait_ge(turned, p + 1)
                nc.vector.tensor_copy(turned_sb[:, r, S:TRI].rearrange("p (b n) -> p b n", b=2),
                                      bank[:, 3 * r + 1:3 * r + 3, 0:3 * P]).then_inc(pt_dve, 1)

            def head_low(h, m, dst, high):
                dve.wait_ge(o_high, h + 1)
                if isinstance(m, int):
                    a, b = dst[:, m, :], high[:, m, :]
                else:
                    a, b = dst[:, bass.ds(m, 1), :].squeeze(1), high[:, bass.ds(m, 1), :].squeeze(1)
                nc.vector.tensor_tensor(a, bank[:, 6, :], b.bitcast(F32), ALU.subtract).then_inc(o_low, 1)

            def rotate(dst, swap, mark=None):
                chain.step(nc.vector.tensor_tensor(dst, dst, rope[:, 0, :], ALU.mult))
                chain.link(nc.vector.tensor_tensor(swap, swap, rope[:, 1, :], ALU.mult))
                ins = nc.vector.tensor_tensor(dst, dst, swap, ALU.add)
                if mark is not None:
                    ins.then_inc(mark, 1)

            def mla(l, j, U, dr, state):
                o = mla_at[l]
                for n in range(DKV_UNITS):
                    split_low(dve, U, 0, 2, n, KT * P)
                dve.wait_ge(mla_side, 16 * (o + 1))
                dve.wait_ge(drained, dr + DKV_UNITS)
                rotate(k_rope[:, :], swapped[:, 0, :])
                dve.wait_ge(lat_rooted, 2 * o + 2)
                chain.step(nc.vector.reciprocal(rs[:, :], rs[:, :]))
                chain.link(nc.vector.reciprocal(rs_kv[:, :], rs_kv[:, :]))
                for n in range(CQ + CKV):
                    g = NORM_COLS["gq"] + CQ * j + n if n < CQ else NORM_COLS["gkv"] + CKV * j + n - CQ
                    nc.vector.scalar_tensor_tensor(out=hf[:, n, :], in0=hf[:, n, :], scalar=misc[:, g:g + 1],
                                                   in1=(rs if n < CQ else rs_kv)[:, :], op0=ALU.mult,
                                                   op1=ALU.mult).then_inc(c_made, 1)
                for n in range(CQ + CKV):
                    dve.wait_ge(c_high, 6 * o + n + 1)
                    dve.wait_ge(c_made, 6 * o + n + 1)
                    nc.vector.tensor_tensor(c_lo[:, n, :], hf[:, n, :], c_hi[:, n, :].bitcast(F32), ALU.subtract)
                end_phase(dve, state)
                W, pb = U + DKV_UNITS, passes_at[l]

                def splits(i, r):
                    split_low(dve, W, i, 4, 2 * r, CQ * QK)
                    split_low(dve, W, i, 4, 2 * r + 1, CKV * 2 * P)

                def fetch(i, r):
                    s, c = r % 2, 4 * (HEADS * o + r)
                    dve.wait_ge(fetched, i * 8 + (c + 2))
                    rotate(q_rope[:, s, :], swapped[:, s, :], roped)
                    dve.wait_ge(projected, i * 4 + (2 * (HEADS * o + r) + 2))
                    nc.vector.tensor_copy(k_nope[:, s, :], bank[:, 7, :]).then_inc(fetched, 1)

                def head(i, r):
                    s, whole = r % 2, not isinstance(i, int)
                    factors(i * 2 + (pb + r), s)
                    if whole or 2 * i + r + 1 < HEADS:
                        maxima(i * 2 + (pb + r + 1), 1 - s)
                    if whole or 2 * i + r + 2 < HEADS:
                        splits(i, r + 2)
                    copy_turned(i * 2 + (pb + r), s, m_turned)
                    head_low(i * 2 + (heads_at[l] + r), i * 2 + r, h_lo, h_hi)
                    if whole or 2 * i + r + 2 < HEADS:
                        fetch(i, r + 2)

                splits(0, 0)
                fetch(0, 0)
                splits(0, 1)
                maxima(pb, 0)
                fetch(0, 1)
                repeat(dve, 3, 2, HEADS, head, chain, 3)
                end_phase(dve, state)
                output_residual(W + 2 * HEADS, l)
            def nsa(l, j, U, dr, state):
                split_low(dve, U, 0, 2, 0, KT * P)
                for n in range(4):
                    if n + 1 < 4:
                        split_low(dve, U, 0, 2, n + 1, KT * P)
                    dve.wait_ge(weights_used, U + n + 1)
                    nc.vector.tensor_copy(hf[:, n, :], bank[:, n % 2, :]).then_inc(drained, 1)
                chain.link(nc.vector.memset(rel_t[:, :], 1.0))
                dve.wait_ge(nsa_small, 1)
                chain.link(nc.vector.tensor_copy(pe_col[:, :, :], bank[:, 4, 0:2 * CB]))
                nc.vector.tensor_copy(rel_t[0:BUCKETS, :], bank[0:BUCKETS, 5, 0:HEADS]).then_inc(nsa_copied, 1)
                dve.wait_ge(drained, dr + 4)
                for n in range(4):
                    w, a = n // 2, n % 2
                    if n >= 2:
                        dve.wait_ge(b_low, n - 1)
                    src = hf[:, 2 * w:2 * w + 2, :].rearrange("p g (m b) -> p b g m", b=CS)[:, :, :, a:a + NC]
                    emb = pe_col[:, w, a * CS:(a + 1) * CS].unsqueeze(2).unsqueeze(3).broadcast_to([P, CS, GROUPS, NC])
                    for g in range(GROUPS):
                        ins = nc.vector.tensor_tensor(b_new[:, a, :, g, :], src[:, :, g, :], emb[:, :, g, :], ALU.add)
                        if g == 0:
                            chain.step(ins)
                        else:
                            ins.then_inc(b_made, 1)
                    dve.wait_ge(b_high, n + 1)
                    dve.wait_ge(b_made, n + 1)
                    chain.wait()
                    nc.vector.tensor_tensor(b_lo[:, w, a * CS:(a + 1) * CS], b_new[:, a],
                                            b_hi[:, w, a * CS:(a + 1) * CS].bitcast(F32), ALU.subtract).then_inc(b_low, 1)
                dve.wait_ge(nsa_small, 2)
                chain.step(nc.vector.tensor_scalar(near_rows[:, :], bank[0:HEADS, 6, 0:3 * P], rel[:, BUCKETS - 1:BUCKETS], None,
                                                   ALU.subtract))
                nc.vector.tensor_copy(far_rows[:, :].rearrange("p (b n) -> p b n", b=2), bank[0:HEADS, 2:4, :]).then_inc(nsa_copied, 1)
                end_phase(dve, state)
                for n in range(16):
                    split_low(dve, U + 4, 0, 2, n, KT * P)
                dve.wait_ge(nsa_small, 3)
                nc.vector.tensor_copy(kc_t[:, :, :], bank[:, 4, 0:GROUPS * NC])
                nc.vector.tensor_copy(vc_t[:, :, :], bank[0:NC, 5, 0:GROUPS * P])
                end_phase(dve, state)
                split_low(dve, U + 20, 0, 2, 0, KT * P)
                for n in range(8):
                    split_low(dve, U + 20, 0, 2, n + 1, KT * (P if n + 1 < 8 else 3 * HEADS))
                    dve.wait_ge(weights_used, U + 20 + n + 1)
                    dst = kf[:, n, :] if n < 4 else vt[:, n - 4, :]
                    nc.vector.tensor_copy(dst, bank[:, n % 2, :]).then_inc(drained, 1)
                dve.wait_ge(nsa_small, 4)
                nc.vector.tensor_copy(near_b[:, :, :].rearrange("p (b h) n -> p b (h n)", b=4), bank[:, 2:6, :]).then_inc(nsa_copied, 1)
                dve.wait_ge(nsa_small, 5)
                for tt in range(TT):
                    last = nc.vector.tensor_copy(cmp_b[:, :, tt, :], bank[:, 2 + tt, 0:HEADS * NC].rearrange("p (h n) -> p h n", h=HEADS))
                end_phase(dve, state)
                W, pb, hb = U + 29, passes_at[l], heads_at[l]

                def low_of_query(h):
                    split_low(dve, W, 0, 2, h, KT * P)

                low_of_query(0)
                dve.wait_ge(q_ready, 1)
                dve.sem_inc(bank7_free, 1)
                maxima(pb, 0, near_b[:, 0, :])
                for h in range(HEADS):
                    dve.wait_ge(cmp_scored, h + 1)
                    nc.vector.tensor_tensor(cmp_p[:, :, :], bank[:, 7, 0:TT * NC].rearrange("p (t n) -> p t n", t=TT),
                                            cmp_b[:, h, :, :], ALU.add).then_inc(bank7_free, 1)
                    dve.wait_ge(bank7_free, 3 * h + 2)
                    chain.link(nc.vector.tensor_reduce(cmp_max[:, :], cmp_p[:, :, :], AX, ALU.max))
                    nc.vector.tensor_scalar(cmp_max[:, :], cmp_max[:, :], MASKED * 1e-10, -1.0, ALU.max, ALU.mult).then_inc(cmp_maxed, 1)
                    maxima(pb + 2 * h + 1, 1, near_b[:, h, :])
                    factors(pb + 2 * h, 0, gates[:, :, HEADS + h])
                    dve.wait_ge(cmp_exped, h + 1)
                    chain.link(nc.vector.tensor_scalar(cmp_sum[:, :], cmp_sum[:, :], 1e-30, None, ALU.max))
                    chain.link(nc.vector.reciprocal(cmp_f[:, :], cmp_sum[:, :]))
                    chain.link(nc.vector.tensor_tensor(cmp_f[:, :], cmp_f[:, :], gates[:, :, h], ALU.mult))
                    nc.vector.tensor_tensor(cmp_p[:, :, :], cmp_p[:, :, :],
                                            cmp_f[:, :].unsqueeze(2).broadcast_to([P, TT, NC]), ALU.mult).then_inc(cmp_scaled, 1)
                    copy_turned(pb + 2 * h, 0, n_turned)
                    factors(pb + 2 * h + 1, 1, gates[:, :, 2 * HEADS + h])
                    if h + 1 < HEADS:
                        low_of_query(h + 1)
                        dve.wait_ge(q_ready, h + 2)
                        dve.sem_inc(bank7_free, 1)
                        maxima(pb + 2 * h + 2, 0, near_b[:, h + 1, :])
                    copy_turned(pb + 2 * h + 1, 1, n_turned)
                    head_low(hb + h, h, o_lo, o_hi)
                end_phase(dve, state)
                output_residual(W + HEADS, l)
            def s5(l, j, U, dr, state):
                T = nc.vector.tensor_tensor
                TS = nc.vector.tensor_scalar

                def complex_product(o_re, o_im, a_re, a_im, b_re, b_im, w1, w2):
                    chain.step(T(w1, a_re, b_re, ALU.mult))
                    chain.link(T(w2, a_im, b_im, ALU.mult))
                    chain.link(T(o_re, w1, w2, ALU.subtract))
                    chain.step(T(w1, a_re, b_im, ALU.mult))
                    chain.link(T(w2, a_im, b_re, ALU.mult))
                    chain.link(T(o_im, w1, w2, ALU.add))

                dve.wait_ge(s5_side, 16 * 9)
                nc.vector.tensor_copy(lam_rows[:, 2, :].rearrange("q (a n) -> q a n", a=2),
                                      dt_rows[:, :].unsqueeze(2).broadcast_to([ST, 2, SN])).then_inc(s5_dve, 1)
                chain.step(nc.vector.memset(out_map[:, :, :, :], 0.0))
                chain.link(nc.vector.memset(b_bar[:, :, :, :], 0.0))
                dve.wait_ge(s5_small, 1)
                chain.link(nc.vector.tensor_copy(small[:, 0:3, :], bank[:, 0, 0:3 * ST].rearrange("p (n q) -> p n q", n=3)))
                lre, lim, dt, grow, ang = (small[:, n, :] for n in range(5))
                e_grow, sin, sin_half, cos, mag1, w1, w2, f_re, f_im, lb1, lb_im, turns, inside, poly = (small[:, n, :] for n in range(5, 19))
                chain.link(TS(turns, dt, 1.0 / math.log(2), ROUND, ALU.mult, ALU.add))
                chain.link(TS(turns, turns, ROUND, None, ALU.subtract))
                TS(w2, turns, math.log(2), 0.35, ALU.mult, ALU.add).then_inc(s5_ready, 1)
                for part in LN_2:
                    chain.link(nc.vector.scalar_tensor_tensor(out=dt, in0=turns, scalar=-part, in1=dt, op0=ALU.mult, op1=ALU.add))
                chain.link(TS(dt, dt, 1.0, -1.0, ALU.min, ALU.max))
                chain.link(TS(poly, dt, 1.0 / math.factorial(SERIES), 1.0 / math.factorial(SERIES - 1), ALU.mult, ALU.add))
                for n in range(SERIES - 2, -1, -1):
                    chain.link(T(poly, poly, dt, ALU.mult))
                    chain.link(TS(poly, poly, 1.0 / math.factorial(n), None, ALU.add))
                dve.wait_ge(s5_exp, 1)
                bits = w2.bitcast(mybir.dt.uint32)
                chain.link(TS(bits, bits, 0x7F800000, None, ALU.bitwise_and))
                chain.link(T(dt, poly, w2, ALU.mult))
                chain.step(T(grow, lre, dt, ALU.mult))
                chain.link(T(ang, lim, dt, ALU.mult))
                chain.link(TS(turns, ang, 1.0 / (2 * math.pi), ROUND, ALU.mult, ALU.add))
                chain.link(TS(turns, turns, ROUND, None, ALU.subtract))
                for part in TWO_PI:
                    chain.link(nc.vector.scalar_tensor_tensor(out=ang, in0=turns, scalar=-part, in1=ang, op0=ALU.mult, op1=ALU.add))
                TS(ang, ang, PI_IN, -PI_IN, ALU.min, ALU.max).then_inc(s5_dve2, 1)
                chain.link(TS(w1, grow, 0.5, -0.5, ALU.min, ALU.max))
                chain.link(TS(poly, w1, 1.0 / math.factorial(SERIES), 1.0 / math.factorial(SERIES - 1), ALU.mult, ALU.add))
                for n in range(SERIES - 2, 0, -1):
                    chain.link(T(poly, poly, w1, ALU.mult))
                    chain.link(TS(poly, poly, 1.0 / math.factorial(n), None, ALU.add))
                chain.link(T(poly, poly, w1, ALU.mult))
                chain.link(T(inside, w1, grow, ALU.is_equal))
                dve.wait_ge(s5_exp, 3)
                chain.link(TS(e_grow, e_grow, 1.0, None, ALU.subtract))
                chain.link(nc.vector.tensor_copy(mag1, e_grow))
                chain.link(nc.vector.copy_predicated(mag1, inside.bitcast(mybir.dt.uint32), poly))
                chain.link(T(w1, sin_half, sin_half, ALU.mult))
                chain.link(TS(w1, w1, -2.0, None, ALU.mult))
                chain.step(TS(cos, w1, 1.0, None, ALU.add))
                chain.link(TS(decay[:, :], mag1, 1.0, None, ALU.add))
                chain.link(T(w2, mag1, cos, ALU.mult))
                chain.step(T(lb1, w2, w1, ALU.add))
                chain.link(T(lb_im, decay[:, :], sin, ALU.mult))
                chain.step(T(w1, lre, lre, ALU.mult))
                chain.link(T(w2, lim, lim, ALU.mult))
                chain.link(T(turns, w1, w2, ALU.add))
                chain.link(nc.vector.reciprocal(turns, turns))
                chain.step(T(w1, lb1, lre, ALU.mult))
                chain.link(T(w2, lb_im, lim, ALU.mult))
                chain.link(T(f_re, w1, w2, ALU.add))
                chain.step(T(f_re, f_re, turns, ALU.mult))
                chain.step(T(w1, lb_im, lre, ALU.mult))
                chain.link(T(w2, lb1, lim, ALU.mult))
                chain.link(T(f_im, w1, w2, ALU.subtract))
                chain.link(T(f_im, f_im, turns, ALU.mult))
                fr, fi = (f.unsqueeze(2).broadcast_to([P, ST, SI]) for f in (f_re, f_im))
                for w, (x0, x1, op) in enumerate((((fr, 0), (fi, 1), ALU.subtract), ((fr, 1), (fi, 0), ALU.add))):
                    chain.step(T(work[:, 0], x0[0], b_in[:, x0[1]], ALU.mult))
                    chain.link(T(work[:, 1], x1[0], b_in[:, x1[1]], ALU.mult))
                    for g in range(2):
                        half = slice(g * SN, (g + 1) * SN)
                        chain.step(T(b_bar[half, w, :, g * SI:(g + 1) * SI], work[half, 0], work[half, 1], op))
                    chain.wait()
                dve.sem_inc(s5_dve, 1)
                p_re, p_im, n_re, n_im = sin_half, e_grow, mag1, poly
                chain.step(nc.vector.tensor_copy(p_re, cos))
                chain.step(nc.vector.tensor_copy(p_im, sin))
                for tab in (fine, coarse):
                    chain.step(nc.vector.memset(tab[:, 0, :, 0:1], 1.0))
                    chain.link(nc.vector.memset(tab[:, 1, :, 0:1], 0.0))
                    n, size = 1, tab.shape[-1]
                    while n < size:
                        b_re, b_im = (v.unsqueeze(2).broadcast_to([P, ST, n]) for v in (p_re, p_im))
                        complex_product(tab[:, 0, :, n:2 * n], tab[:, 1, :, n:2 * n], tab[:, 0, :, 0:n], tab[:, 1, :, 0:n],
                                        b_re, b_im, work[:, 0, :, 0:n], work[:, 1, :, 0:n])
                        complex_product(n_re, n_im, p_re, p_im, p_re, p_im, w1, w2)
                        p_re, p_im, n_re, n_im = n_re, n_im, p_re, p_im
                        n *= 2
                end_phase(dve, state)

                def leave(k):
                    dve.wait_ge(y_made, k + 1)
                    d = NORM_COLS["d"] + KT * j + k
                    nc.vector.scalar_tensor_tensor(out=hf[:, k, :], in0=hf[:, k, :], scalar=misc[:, d:d + 1],
                                                   in1=bank[:, 4 + k % 2, :], op0=ALU.mult, op1=ALU.add).then_inc(y_in, 1)

                for q in range(ST):
                    r = q % 2
                    if q >= 1:
                        dve.wait_ge(products_made, q)
                    dve.wait_ge(table_made, q + 1)
                    dve.wait_ge(bu_made, q + 1)
                    t_re, t_im, b_re, b_im = turn_t[:, r, 0, :], turn_t[:, r, 1, :], bank[:, 2 * r, :], bank[:, 2 * r + 1, :]
                    sw = [scan_w[:, n, :] for n in range(4)]
                    chain.step(T(sw[0], b_re, t_re, ALU.mult))
                    chain.step(T(sw[1], b_im, t_im, ALU.mult))
                    chain.step(T(sw[2], b_im, t_re, ALU.mult))
                    T(sw[3], b_re, t_im, ALU.mult).then_inc(bu_free, 1)
                    dve.wait_ge(bu_free, q + 1)
                    chain.wait()
                    chain.step(T(sw[0], sw[0], sw[1], ALU.add))
                    chain.link(T(sw[2], sw[2], sw[3], ALU.subtract))
                    mag = decay[:, q:q + 1].broadcast_to([P, S])
                    chain.step(nc.vector.tensor_tensor_scan(sw[1], mag, sw[0], 0.0, ALU.mult, ALU.add))
                    chain.link(nc.vector.tensor_tensor_scan(sw[3], mag, sw[2], 0.0, ALU.mult, ALU.add))
                    st = [state_w[:, r, n, :] for n in range(4)]
                    for need in ([q - 2] if q >= 2 else []):
                        if need % 4 == 3:
                            dve.wait_ge(y_made, need // 4 + 1)
                        else:
                            dve.wait_ge(products_used, 3 * (need // 4) + need % 4 + 1)
                    T(st[0], sw[1], t_re, ALU.mult)
                    T(st[1], sw[3], t_im, ALU.mult)
                    T(st[2], sw[3], t_re, ALU.mult)
                    T(st[3], sw[1], t_im, ALU.mult).then_inc(products_made, 1)
                    if q >= 5 and q % 4 == 1:
                        leave(q // 4 - 1)
                leave(KT - 1)
                for k in range(KT):
                    dve.wait_ge(y_high, k + 1)
                    T(h_lo[:, k, :], hf[:, k, :], h_hi[:, k, :].bitcast(F32), ALU.subtract)
                end_phase(dve, state)
                for e in range(2):
                    split_low(dve, U, 0, 4, e, KT * P)

                def glu_pair(i, r):
                    if not (isinstance(i, int) and 2 * i + r + 1 >= KT):
                        for e in range(2):
                            split_low(dve, U, i, 4, 2 * (r + 1) + e, KT * P)
                    m = i * 2 + r
                    dve.wait_ge(sig_made, i * 2 + (r + 1))
                    nc.vector.scalar_tensor_tensor(out=gated[:, r, :], in0=bank[:, 2 * r, :], scalar=mod[:, bass.ds(i * 2 + (mod_col(l, 2, 0) + r), 1)],
                                                   in1=sig[:, r, :], op0=ALU.mult, op1=ALU.mult).then_inc(drained, 1)
                    dve.wait_ge(drained, i * 4 + (dr + 2 * r + 1))
                    at = x[:, m, :] if isinstance(m, int) else x[:, bass.ds(m, 1), :].squeeze(1)
                    nc.vector.tensor_tensor(at, at, gated[:, r, :], ALU.add).then_inc(drained, 1)

                repeat(dve, 3, 2, KT, glu_pair)
            for name, l, j, U, dr, idx in plan:
                if name == "norm":
                    norm(l, j, idx)
                elif name == "mla":
                    mla(l, j, U, dr, state)
                elif name == "nsa":
                    nsa(l, j, U, dr, state)
                elif name == "s5":
                    s5(l, j, U, dr, state)
                elif name == "ffn":
                    ffn(l, U, dr)
                else:
                    norm(0, 2, idx)
                    for k in range(KT):
                        dve.wait_ge(turned_in, N_TURN + KT + k + 1)
                        nc.vector.tensor_copy(out_rows[:, :, k * P:(k + 1) * P],
                                              bank[:, 4 + k % 2, :].rearrange("p (t f) -> p t f", t=TT)).then_inc(copied_in, 1)
                end_phase(dve, state)

        @block.gpsimd
        def _(pool):
            state, chain = [0], Chain(pool, pool_chain)
            pool.sem_inc(ada_used, 4)
            pool.sem_inc(g_made, 2)
            end_phase(pool, state)
            pool.sem_inc(pt_act, 2)
            pool.sem_inc(pt_dve, 2)
            pool.sem_inc(o_low, 1)

            def scale(p, r, probs):
                pool.wait_ge(factored, p + 1)
                for q in range(TT):
                    at = probs[:, r, ROW_AT[q]:ROW_AT[q] + P * (q + 1)]
                    last = nc.gpsimd.tensor_tensor(at, at, factor[:, r, q:q + 1].broadcast_to([P, P * (q + 1)]), ALU.mult)
                last.then_inc(scaled, 1)

            def mla(l, j, U, dr, state):
                pool.dma_start(rope[:], t["rope"]).then_inc(mla_side, 16)
                end_phase(pool, state)
                repeat(pool, 4, 2, HEADS, lambda i, r: scale(i * 2 + (passes_at[l] + r), r, m_probs))
                end_phase(pool, state)
            def nsa(l, j, U, dr, state):
                for dst, src in ((pe_rows[:, 0, :], t["nsa_pe_k"][j]), (pe_rows[:, 1, :], t["nsa_pe_v"][j]),
                                 (w2[:, 0], t["nsa_w2_k"][j].rearrange("(k p) m -> p k m", p=P)),
                                 (w2[:, 1], t["nsa_w2_v"][j].rearrange("(k p) m -> p k m", p=P)),
                                 (near_hot[:], t["near"]), (far_hot[:], t["far"]), (flip[:], t["flip"]), (rel[:], t["rel_bias"])):
                    pool.dma_start(dst, src).then_inc(nsa_side, 16)
                end_phase(pool, state)
                near_d, far_d = scratch[:, 0:3 * P], scratch[:, 1024:1024 + 2 * S]
                pool.dma_start(near_d, near_rows[:]).then_inc(rows_out, 16)
                pool.dma_start(far_d, far_rows[:]).then_inc(rows_out, 16)
                end_phase(pool, state)
                pool.wait_ge(rows_out, 32)
                row = scratch.shape[1]
                pool.dma_start(near_back, bass.AP(tensor=scratch.tensor, offset=0, ap=[[1, P], [row, HEADS], [1, FAR]])).then_inc(rows_back, 16)
                pool.wait_ge(nsa_small, 4)
                pool.dma_start(cmp_back, bass.AP(tensor=scratch.tensor, offset=1024, ap=[[CS, NC], [row, HEADS], [1, S]])).then_inc(rows_back, 16)
                end_phase(pool, state)
                for h in range(HEADS):
                    scale(passes_at[l] + 2 * h, 0, n_probs)
                    scale(passes_at[l] + 2 * h + 1, 1, n_probs)
                end_phase(pool, state)
            def s5(l, j, U, dr, state):
                for w, key in enumerate(("s5_lam_re", "s5_lam_im")):
                    pool.dma_start(lam_rows[:, w, :], t[key][j].rearrange("(q a) n -> q (a n)", a=2)).then_inc(s5_side, 16)
                pool.dma_start(dt_rows[:], t["s5_log_dt"][j].rearrange("(q a) -> q a", a=2)).then_inc(s5_side, 16)
                for w, key in enumerate(("s5_b_re", "s5_b_im")):
                    pool.dma_start(b_in[:, w], t[key][j].rearrange("(q a) n i -> (a n) q i", a=2)).then_inc(s5_side, 16)
                for w, key in enumerate(("s5_c_re", "s5_c_im")):
                    for twice in range(2):
                        src = t[key][j].rearrange("(k g) i n -> (g i) k n", g=P // SI)
                        pool.dma_start(c_rows[:, w, :, twice, :], src).then_inc(s5_side, 16)
                end_phase(pool, state)

                def sums(q):
                    r = q % 2
                    pool.wait_ge(products_made, q + 1)
                    st = [state_w[:, r, n, :] for n in range(4)]
                    nc.gpsimd.tensor_tensor(st[0], st[0], st[1], ALU.subtract)
                    nc.gpsimd.tensor_tensor(st[2], st[2], st[3], ALU.add).then_inc(x_made, 1)

                for q in range(ST):
                    r = q % 2
                    if q >= 2:
                        pool.wait_ge(products_made, q - 1)
                    if q >= 1:
                        pool.wait_ge(table_made, q)
                    shape = [P, COARSE, FINE]
                    c_re, c_im = (coarse[:, w, q, :].unsqueeze(2).broadcast_to(shape) for w in range(2))
                    f_re, f_im = (fine[:, w, q, :].unsqueeze(1).broadcast_to(shape) for w in range(2))
                    to, w1, w2 = (v.rearrange("p (c f) -> p c f", c=COARSE) for v in (turn_t[:, r, 0, :], turn_w[:, 0, :], turn_w[:, 1, :]))
                    ti = turn_t[:, r, 1, :].rearrange("p (c f) -> p c f", c=COARSE)
                    chain.step(nc.gpsimd.tensor_tensor(w1, c_re, f_re, ALU.mult))
                    chain.link(nc.gpsimd.tensor_tensor(w2, c_im, f_im, ALU.mult))
                    chain.link(nc.gpsimd.tensor_tensor(to, w1, w2, ALU.subtract))
                    chain.step(nc.gpsimd.tensor_tensor(w1, c_re, f_im, ALU.mult))
                    chain.link(nc.gpsimd.tensor_tensor(w2, c_im, f_re, ALU.mult))
                    nc.gpsimd.tensor_tensor(ti, w1, w2, ALU.add).then_inc(table_made, 1)
                    if q >= 1:
                        sums(q - 1)
                sums(ST - 1)
                end_phase(pool, state)
            for name, l, j, U, dr, idx in plan:
                if name == "mla":
                    mla(l, j, U, dr, state)
                elif name == "nsa":
                    nsa(l, j, U, dr, state)
                elif name == "s5":
                    s5(l, j, U, dr, state)
                end_phase(pool, state)


_INS = ["x", "c", "ada_w", "ada_b", "norm1_g", "norm2_g", "final_g", "rel_bias",
        "mla_w_dkv", "mla_g_q", "mla_g_kv", "mla_w_uq", "mla_w_ukv", "mla_w_o",
        "nsa_w_in", "nsa_pe_k", "nsa_w1_k", "nsa_w2_k", "nsa_pe_v", "nsa_w1_v", "nsa_w2_v", "nsa_w_o",
        "s5_lam_re", "s5_lam_im", "s5_log_dt", "s5_b_re", "s5_b_im", "s5_c_re", "s5_c_im", "s5_d", "s5_w_glu",
        "ffn_w_up", "ffn_conv_w", "ffn_conv_b", "ffn_w_down"]


def shape_tables():
    import numpy as np
    eye = np.eye(P, dtype=np.float32)
    later = np.triu(np.ones((P, P), np.float32), 1) * np.float32(MASKED)
    half = ROPE // 2
    inv = (np.float32(10000.0) ** (-np.arange(half, dtype=np.float32) / np.float32(half))).astype(np.float32)
    ang = (inv[:, None] * np.arange(S, dtype=np.float32)[None, :]).astype(np.float32)
    cos, sin = np.cos(ang.astype(np.float64)), np.sin(ang.astype(np.float64))
    rope = np.stack([np.concatenate([cos, cos]), np.concatenate([-sin, sin])], 1).astype(np.float32)

    def bucket(dist):
        n = np.maximum(dist, 0)
        nf = np.maximum(n, 1).astype(np.float32)
        large = 16 + (np.log(nf / np.float32(16)) / np.float32(math.log(8)) * np.float32(16)).astype(np.int32)
        return np.where(n < 16, n, np.minimum(large, BUCKETS - 1))

    def hot(dist):
        at = np.zeros((BUCKETS + 1, len(dist)), np.float32)
        at[bucket(dist), np.arange(len(dist))] = 1.0
        at[BUCKETS] = np.where(dist < 0, np.float32(MASKED), np.float32(0))
        return at

    near = hot(255 - np.arange(384))
    far = hot(np.arange(1024) - 511 )
    return {"ident": eye, "flip": eye[::-1].copy(), "mask": later,
            "rope": rope, "near": near, "far": far}


def kernel(**inputs):
    import numpy as np
    import concourse.bacc as bacc
    from concourse.bass_utils import run_bass_kernel_spmd

    nc = bacc.Bacc("TRN2", target_bir_lowering=False, num_devices=1)
    arrays, aps = {}, {}
    given = {n: np.ascontiguousarray(inputs[n]) for n in _INS}
    given.update(shape_tables())
    for name, a in given.items():
        arrays[f"in_{name}"] = a
        aps[name] = nc.dram_tensor(f"in_{name}", a.shape, mybir.dt.from_np(a.dtype), kind="ExternalInput").ap()
    out = nc.dram_tensor("out", (1, S, D), F32, kind="ExternalOutput").ap()
    scratch = nc.dram_tensor("bias_rows", (HEADS, 2048), F32, kind="Internal").ap()
    trunk(nc, aps, out, scratch)
    got = run_bass_kernel_spmd(nc, [arrays], core_ids=[0]).results[0]
    return got["out"]
```

```python
import math
from contextlib import ExitStack, contextmanager

import concourse.bass as bass
from concourse import mybir

ALU = mybir.AluOpType
ACT = mybir.ActivationFunctionType
AX = mybir.AxisListType.X
F32 = mybir.dt.float32
F32R = mybir.dt.float32r
BF16 = mybir.dt.bfloat16

P = 128
D = 1024
S = 512
LAYERS = (0, 1, 2, 3)
DEPTH = 4
KT = D // P
TT = S // P
EPS = 1e-6
N_MOD = 6
MODS = N_MOD * KT

Q_LORA, KV_LORA, ROPE, NOPE = 512, 256, 64, 128
HEADS = 8
QK = NOPE + ROPE
CQ, CKV = Q_LORA // P, KV_LORA // P
MLA_SCALE = float(QK) ** -0.5
DKV_UNITS = 7

GROUPS, HPG, DK = 2, 4, 128
NSA_SCALE = float(DK) ** -0.5
CB, CS = 32, 16
NC = S // CS - 1
CH = 256
BUCKETS = 32
FAR = 2 * P
NSA_COL = {"q": 0, "kc": 1024, "vc": 1280, "ks": 1536, "vs": 1792, "kw": 2048, "vw": 2304, "gate": 2560}
MASKED = -1e30

SG, SN, SI = 64, 64, 16
ST = SG * SN // P
FINE, COARSE = 32, S // 32

FF = 2816
PAIRS = FF // P
HALF = PAIRS // 2
TAPS = 3
CHT = 2 * PAIRS

SERIES = 8
ROUND = 1.5 * 2.0 ** 23
TWO_PI = (6.28125, 0.0019350051879882812, 2 * math.pi - 6.28125 - 0.0019350051879882812)
PI_IN = 3.1415925
ADA_W = N_MOD * D // 2
LN_2 = (0.693359375, math.log(2) - 0.693359375)

UNIT = HALF * P
TRI = P * TT * (TT + 1) // 2
ROW_AT = [P * i * (i + 1) // 2 for i in range(TT)]
COL_AT = [P * sum(TT - c for c in range(j)) for j in range(TT)]

NORM_COLS = {"norm1": 0, "norm2": 32, "final": 64, "gq": 72, "gkv": 80, "d": 84}
MISC_ROWS = 92
CW_ROWS, CB_ROWS, AB_ROWS = 88, 88, 96


def reached(eng, sem, value):
    if not (isinstance(value, int) and value <= 0):
        eng.wait_ge(sem, value)


def repeat(eng, trips, per, total, step, chain=None, links=0, first=0):
    for r in range(first):
        step(0, r)
    if trips:
        with ExitStack() as ctx:
            i = ctx.enter_context(eng.Fori(0, trips))
            if chain is not None:
                ctx.enter_context(chain.loop(i, trips, per * links))
            for r in range(first, first + per):
                step(i, r)
    for n in range(first + trips * per, total):
        step(trips, n - trips * per)


class Chain:

    def __init__(self, eng, sem):
        self.eng, self.sem, self.n, self.i, self.per = eng, sem, 0, None, 0

    def step(self, ins):
        ins.then_inc(self.sem, 1)
        self.n += 1

    def wait(self):
        self.eng.wait_ge(self.sem, self.n if self.i is None else self.i * self.per + self.n)

    def link(self, ins):
        self.step(ins)
        self.wait()

    @contextmanager
    def loop(self, i, trips, per):
        first, self.i, self.per = self.n, i, per
        yield
        assert self.n == first + per, (self.n, first, per)
        self.n, self.i = first + per * trips, None


def units_of(layer):
    kind = layer % 3
    mixer = (DKV_UNITS + 2 * HEADS + KT) if kind == 0 else (8 + 16 + 4 + 1 + HEADS + KT) if kind == 1 else 2 * KT
    return mixer


def trunk(nc, t, out, scratch):
    with ExitStack() as ctx:
        def sb(name, shape, dt=F32, stack=ctx):
            return stack.enter_context(nc.sbuf_tensor(name, shape, dt))

        def sem(name):
            return ctx.enter_context(nc.semaphore(name))

        bank = ctx.enter_context(nc.psum_tensor("bank", [P, 8, 512], F32))

        x = sb("x", [P, KT, S])
        hf = sb("hf", [P, KT, S])
        h_hi = sb("h_hi", [P, KT, S], F32R)
        h_lo = sb("h_lo", [P, KT, S], F32R)
        stage = sb("stage", [P, 2, UNIT])
        w_hi = sb("w_hi", [P, 2, UNIT], F32R)
        w_lo = sb("w_lo", [P, 2, UNIT], F32R)
        rs = sb("rs", [P, S])
        sq_x = sb("sq_x", [P, 2, S])
        c_act = sb("c_act", [P, KT])
        ident = sb("ident", [P, P])
        ones = sb("ones", [P, P])
        eps = sb("eps", [P, 1])
        ident_b = sb("ident_b", [P, P], BF16)
        mask_b = sb("mask_b", [P, P], BF16)
        mask = sb("mask", [P, P])
        mod = sb("mod", [P, DEPTH * MODS])
        misc = sb("misc", [P, MISC_ROWS])
        cw = sb("cw", [P, DEPTH * TAPS * CHT])
        cb = sb("cb", [P, DEPTH * CHT])
        amp = sb("amp", [P, DEPTH * 2 * KT])

        landed = [sem("landed0"), sem("landed1")]
        hi_made, lo_made, weights_used, drained = sem("hi_made"), sem("lo_made"), sem("weights_used"), sem("drained")
        phase_end = sem("phase_end")
        act_chain, dve_chain, pool_chain = sem("act_chain"), sem("dve_chain"), sem("pool_chain")
        params_in, consts_in, turned_in, copied_in = sem("params_in"), sem("consts_in"), sem("turned_in"), sem("copied_in")
        rooted = sem("rooted")
        squares, h_made, h_high = sem("squares"), sem("h_made"), sem("h_high")
        cv_made, silu_made, g_made, g_high, g_low = sem("cv_made"), sem("silu_made"), sem("g_made"), sem("g_high"), sem("g_low")
        stored = sem("stored")
        ada_in = [sem("ada_in0"), sem("ada_in1")]
        ada_used, ada_done, ada_turned, sq_used, rs_made, x_scaled, h_low, c_in = (
            sem(n) for n in ("ada_used", "ada_done", "ada_turned", "sq_used", "rs_made", "x_scaled", "h_low", "c_in"))

        with ExitStack() as own:
            rows = sb("rows", [P, 20, P], stack=own)
            x_rows = sb("x_rows", [P, TT, D], stack=own)
        with ExitStack() as own:
            g_hi = sb("g_hi", [P, HALF, S], F32R, stack=own)
            g_lo = sb("g_lo", [P, HALF, S], F32R, stack=own)
            cv = sb("cv", [P, 2, 2, S], stack=own)
            sg = sb("sg", [P, 2, S], stack=own)
            gf = sb("gf", [P, 2, S], stack=own)
            ada_w = sb("ada_w", [P, 2, ADA_W], stack=own)
        with ExitStack() as own:
            out_rows = sb("out_rows", [P, TT, D], stack=own)
        with ExitStack() as own:
            sq = sb("sq", [P, CQ + CKV, S], stack=own)
            c_hi = sb("c_hi", [P, CQ + CKV, S], F32R, stack=own)
            c_lo = sb("c_lo", [P, CQ + CKV, S], F32R, stack=own)
            rope = sb("rope", [ROPE, 2, S], stack=own)
            k_rope = sb("k_rope", [ROPE, S], stack=own)
            swapped = sb("swapped", [ROPE, 2, S], stack=own)
            rs_kv = sb("rs_kv", [P, S], stack=own)
            with ExitStack() as part:
                q_nope = sb("q_nope", [P, 2, S], stack=part)
                q_rope = sb("q_rope", [ROPE, 2, S], stack=part)
                k_nope = sb("k_nope", [P, 2, S], stack=part)
                v_tok = sb("v_tok", [P, 2, S], stack=part)
                m_probs = sb("m_probs", [P, 2, TRI], stack=part)
                m_turned = sb("m_turned", [P, 2, TRI], stack=part)
        neg_max = sb("neg_max", [P, 2, TT])
        row_sum = sb("row_sum", [P, 2, TT])
        factor = sb("factor", [P, 2, TT])
        lat_summed, lat_rooted, c_made, c_high = sem("lat_summed"), sem("lat_rooted"), sem("c_made"), sem("c_high")
        mla_side = sem("mla_side")
        projected, fetched, roped = sem("projected"), sem("fetched"), sem("roped")
        scored, maxed, exped, factored, scaled = sem("scored"), sem("maxed"), sem("exped"), sem("factored"), sem("scaled")
        turned, pt_act, pt_dve = sem("turned"), sem("pt_act"), sem("pt_dve")
        valued, o_high, o_low = sem("valued"), sem("o_high"), sem("o_low")

        def score_tile(r, i):
            b, at = {3: (0, 0), 2: (1, 0), 1: (2, P), 0: (2, 0)}[i]
            return bank[:, 3 * r + b, at:at + P * (i + 1)]

        def turned_tile(r, j, i):
            b, at = min(j, 2), (i - j) * P + (2 * P if j == 3 else 0)
            return bank[:, 3 * r + b, at:at + P]
        with ExitStack() as own:
            kf = sb("kf", [P, 2 * GROUPS, S], stack=own)
            vt = sb("vt", [P, 2 * GROUPS, S], stack=own)
            kc_t = sb("kc_t", [P, GROUPS, NC], stack=own)
            vc_t = sb("vc_t", [NC, GROUPS, P], stack=own)
            gates = sb("gates", [P, TT, 3 * HEADS], stack=own)
            near_b = sb("near_b", [P, HEADS, FAR], stack=own)
            cmp_b = sb("cmp_b", [P, HEADS, TT, NC], stack=own)
            hid = sb("hid", [P, 2, 2, GROUPS * NC], stack=own)
            w2 = sb("w2", [P, 2, 2, P], stack=own)
            pe_rows = sb("pe_rows", [CB, 2, P], stack=own)
            pe_col = sb("pe_col", [P, 2, CB], stack=own)
            with ExitStack() as part:
                b_hi = sb("b_hi", [P, 2, CB, GROUPS, NC], F32R, stack=part)
                b_lo = sb("b_lo", [P, 2, CB, GROUPS, NC], F32R, stack=part)
                b_new = sb("b_new", [P, 2, CS, GROUPS, NC], stack=part)
                near_hot = sb("near_hot", [BUCKETS + 1, 3 * P], stack=part)
                far_hot = sb("far_hot", [BUCKETS + 1, 2 * S], stack=part)
                flip = sb("flip", [P, P], stack=part)
                rel = sb("rel", [HEADS, BUCKETS], stack=part)
                rel_t = sb("rel_t", [BUCKETS + 1, HEADS], stack=part)
                near_rows = sb("near_rows", [HEADS, 3 * P], stack=part)
                far_rows = sb("far_rows", [HEADS, 2 * S], stack=part)
            with ExitStack() as part:
                q_t = sb("q_t", [P, 2, S], stack=part)
                n_probs = sb("n_probs", [P, 2, TRI], stack=part)
                n_turned = sb("n_turned", [P, 2, TRI], stack=part)
                cmp_p = sb("cmp_p", [P, TT, NC], stack=part)
                cmp_t = sb("cmp_t", [NC, S], stack=part)
                o_hi = sb("o_hi", [P, KT, S], F32R, stack=part)
                o_lo = sb("o_lo", [P, KT, S], F32R, stack=part)
                cmp_max = sb("cmp_max", [P, TT], stack=part)
                cmp_sum = sb("cmp_sum", [P, TT], stack=part)
                cmp_f = sb("cmp_f", [P, TT], stack=part)
        near_back = hf[:, 4:8, :].rearrange("p k s -> p (k s)").rearrange("p (h n) -> p h n", h=HEADS)
        cmp_back = hf[0:NC, :, :]
        nsa_side, nsa_small, nsa_copied, b_made, b_high = (sem(n) for n in ("nsa_side", "nsa_small", "nsa_copied", "b_made", "b_high"))
        rows_out, rows_back, b_low = sem("rows_out"), sem("rows_back"), sem("b_low")
        cmp_scored, cmp_maxed, cmp_exped, cmp_scaled, cmp_turned = (sem(n) for n in ("cmp_scored", "cmp_maxed", "cmp_exped", "cmp_scaled", "cmp_turned"))
        bank7_free, q_ready, gates_in = sem("bank7_free"), sem("q_ready"), sem("gates_in")
        with ExitStack() as own:
            in_map = sb("in_map", [P, 2, KT, P], stack=own)
            out_map = sb("out_map", [P, 2, KT, 5 * P], stack=own)
            fine = sb("fine", [P, 2, ST, FINE], stack=own)
            coarse = sb("coarse", [P, 2, ST, COARSE], stack=own)
            decay = sb("decay", [P, ST], stack=own)
            with ExitStack() as part:
                small = sb("small", [P, 24, ST], stack=part)
                lam_rows = sb("lam_rows", [ST, 3, P], stack=part)
                dt_rows = sb("dt_rows", [ST, 2], stack=part)
                b_in = sb("b_in", [P, 2, ST, SI], stack=part)
                b_bar = sb("b_bar", [P, 2, ST, 2 * SI], stack=part)
                c_rows = sb("c_rows", [P, 2, KT, 2, SN], stack=part)
                work = sb("work", [P, 2, ST, SI], stack=part)
            with ExitStack() as part:
                turn_t = sb("turn_t", [P, 2, 2, S], stack=part)
                turn_w = sb("turn_w", [P, 2, S], stack=part)
                scan_w = sb("scan_w", [P, 4, S], stack=part)
                state_w = sb("state_w", [P, 2, 4, S], stack=part)
            with ExitStack() as part:
                sig = sb("sig", [P, 2, S], stack=part)
                gated = sb("gated", [P, 2, S], stack=part)
        s5_side, s5_small, s5_act, s5_dve = (sem(n) for n in ("s5_side", "s5_small", "s5_act", "s5_dve"))
        table_made, bu_made, bu_free, products_made, x_made, y_made = (
            sem(n) for n in ("table_made", "bu_made", "bu_free", "products_made", "x_made", "y_made"))
        products_used, s5_exp, s5_dve2, s5_ready = (sem(n) for n in ("products_used", "s5_exp", "s5_dve2", "s5_ready"))
        y_in, y_gelu, y_high, y_low, sig_made = (sem(n) for n in ("y_in", "y_gelu", "y_high", "y_low", "sig_made"))
        block = ctx.enter_context(nc.Block())

        plan, units, drains, norms = [], 0, 0, 0
        for l in LAYERS:
            kind = l % 3
            plan.append(("norm", l, 0, units, drains, norms))
            plan.append((("mla", "nsa", "s5")[kind], l, l // 3, units, drains, norms))
            units += units_of(l)
            drains += (DKV_UNITS + KT, 8 + 4 + 4 + 1 + KT, 2 * KT)[kind]
            plan.append(("norm", l, 1, units, drains, norms + 1))
            plan.append(("ffn", l, 0, units, drains, norms + 1))
            units += 2 * (2 * HALF + KT)
            drains += 2 * (2 * HALF + KT)
            norms += 2
        plan.append(("final", 0, 0, units, drains, norms))
        l_at = {l: n for n, l in enumerate(LAYERS)}
        mla_at, passes_at, heads_at, a, b, c = {}, {}, {}, 0, 0, 0
        for l in LAYERS:
            mla_at[l], passes_at[l], heads_at[l] = a, b, c
            a, b, c = a + (l % 3 == 0), b + (HEADS, 2 * HEADS, 0)[l % 3], c + (HEADS, HEADS, 0)[l % 3]

        def mod_col(l, part, m):
            return l * MODS + part * KT + m

        def end_phase(eng, state):
            state[0] += 1
            eng.drain().then_inc(phase_end, 1)
            eng.wait_ge(phase_end, 4 * state[0])

        following = dict(zip(LAYERS, LAYERS[1:]))
        ada_sum = hf[:, 0:ADA_W // S, :].rearrange("p k s -> p (k s)")

        def load_unit(sp, U, i, per, r, src, width):
            reached(sp, lo_made, i * per + (U + r - 1))
            dst = stage[:, (U + r) % 2, 0:width].rearrange("p (k m) -> p k m", m=src.shape[-1])
            sp.dma_start(dst, src).then_inc(landed[(U + r) % 2], 16)

        def split_high(act, U, i, per, r, width):
            s = (U + r) % 2
            act.wait_ge(landed[s], (i * (per // 2) + ((U + r) // 2 + 1)) * 16)
            reached(act, weights_used, i * per + (U + r - 1))
            nc.scalar.copy(w_hi[:, s, 0:width], stage[:, s, 0:width]).then_inc(hi_made, 1)

        def split_low(dve, U, i, per, r, width):
            s = (U + r) % 2
            dve.wait_ge(hi_made, i * per + (U + r + 1))
            nc.vector.tensor_tensor(w_lo[:, s, 0:width], stage[:, s, 0:width], w_hi[:, s, 0:width].bitcast(F32),
                                    ALU.subtract).then_inc(lo_made, 1)

        def three(dst, a_hi, a_lo, b_hi, b_lo, first, last):
            nc.tensor.matmul(dst, a_hi, b_hi, start=first, stop=False)
            nc.tensor.matmul(dst, a_hi, b_lo, start=False, stop=False)
            return nc.tensor.matmul(dst, a_lo, b_hi, start=False, stop=last)

        def feature_product(dst, s, k_tiles, stride, at, r_hi, r_lo, ready=None):
            for k in range(k_tiles):
                if ready is not None:
                    ready(k)
                a_hi = w_hi[:, s, k * stride + at:k * stride + at + P]
                a_lo = w_lo[:, s, k * stride + at:k * stride + at + P]
                last = three(dst, a_hi, a_lo, r_hi[:, k, :], r_lo[:, k, :], k == 0, k == k_tiles - 1)
            return last

        def token_product(dst, s, k_tiles, stride, at, m, a_hi, a_lo):
            for tt in range(TT):
                for k in range(k_tiles):
                    last = three(dst[:, tt * m:(tt + 1) * m], a_hi[:, k, tt * P:(tt + 1) * P], a_lo[:, k, tt * P:(tt + 1) * P],
                                 w_hi[:, s, k * stride + at:k * stride + at + m],
                                 w_lo[:, s, k * stride + at:k * stride + at + m], k == 0, k == k_tiles - 1)
            return last

        def w_view(w):
            return w.rearrange("(k p) m -> p k m", p=P)

        ab = t["ada_b"].rearrange("l (r f) -> (l r) f", f=P)
        cwr = t["ffn_conv_w"].rearrange("l w (c f) -> (l w c) f", f=P)
        cbr = t["ffn_conv_b"].rearrange("l (c f) -> (l c) f", f=P)
        row_loads = [(0, 0, ab[0:96]), (1, 0, ab[96:192])]
        row_loads += [(3 + g, 0, cwr[CW_ROWS * g:CW_ROWS * (g + 1)]) for g in range(6)]
        row_loads += [(9 + g, 0, cbr[CB_ROWS * g:CB_ROWS * (g + 1)]) for g in range(2)]
        for key, name in (("norm1", "norm1_g"), ("norm2", "norm2_g"), ("gq", "mla_g_q"), ("gkv", "mla_g_kv")):
            row_loads.append((2, NORM_COLS[key], t[name].rearrange("l (r f) -> (l r) f", f=P)))
        row_loads.append((2, NORM_COLS["final"], t["final_g"].rearrange("(r f) -> r f", f=P)))
        row_loads.append((2, NORM_COLS["d"], t["s5_d"].rearrange("n (r g) i -> (n r) (g i)", g=P // SI)))
        turns = [(0, AB_ROWS, mod, 0), (1, AB_ROWS, mod, AB_ROWS), (2, MISC_ROWS, misc, 0)]
        turns += [(3 + g, CW_ROWS, cw, CW_ROWS * g) for g in range(6)]
        turns += [(9 + g, CB_ROWS, cb, CB_ROWS * g) for g in range(2)]
        N_TURN = len(turns)
        x_view = t["x"].rearrange("b (t p) f -> p (b t) f", p=P)

        def load_ada(sp, l, n):
            g = 2 * KT * l_at[l] + n
            reached(sp, ada_used, g - 1)
            src = t["ada_w"][l].rearrange("(p k) f -> p k f", k=KT)[:, n % KT, (n // KT) * ADA_W:(n // KT + 1) * ADA_W]
            sp.dma_start(ada_w[:, g % 2, :], src).then_inc(ada_in[g % 2], 16)

        @block.sync
        def _(sp):
            for slot, at, src in row_loads:
                sp.dma_start(rows[at:at + src.shape[0], slot, :], src).then_inc(params_in, 16)
            sp.dma_start(x_rows[:], x_view).then_inc(params_in, 16)
            sp.dma_start(c_act[:], t["c"].rearrange("b (p k) -> (b p) k", k=KT)).then_inc(c_in, 16)
            for dst, name in ((ident, "ident"), (mask, "mask")):
                sp.dma_start(dst[:], t[name]).then_inc(consts_in, 16)
            for n in range(2 * KT):
                load_ada(sp, LAYERS[0], n)
            for name, l, j, U, _, _ in plan:
                if name == "ffn":
                    up, down = w_view(t["ffn_w_up"][l]), t["ffn_w_down"][l].rearrange("(k p) m -> p k m", p=P)
                    for half in range(2):
                        V = U + half * (2 * HALF + KT)

                        def up_pair(i, r):
                            for e in range(2):
                                load_unit(sp, V, i, 4, 2 * r + e,
                                          up[:, :, bass.ds((i * 2 + r) * P + (e * FF + half * HALF * P), P)], KT * P)

                        ada = following.get(l)
                        repeat(sp, 5, 2, HALF, up_pair)
                        for n in range(2 if ada is not None else 0):
                            load_ada(sp, ada, half * KT + n)
                        for n in range(KT):
                            load_unit(sp, V + 2 * HALF, 0, 2, n, down[:, half * HALF:(half + 1) * HALF, n * P:(n + 1) * P], UNIT)
                            if ada is not None and n >= 2:
                                load_ada(sp, ada, half * KT + n)
                if name == "mla":
                    dkv, uq, ukv, wo = (w_view(t[n][j]) for n in ("mla_w_dkv", "mla_w_uq", "mla_w_ukv", "mla_w_o"))
                    for n in range(DKV_UNITS):
                        c = min(n * P, Q_LORA + KV_LORA + ROPE - P)
                        load_unit(sp, U, 0, 2, n, dkv[:, :, c:c + P], KT * P)
                    W = U + DKV_UNITS

                    def head_units(i, r):
                        load_unit(sp, W, i, 4, 2 * r, uq[:, :, bass.ds((i * 2 + r) * QK, QK)], CQ * QK)
                        load_unit(sp, W, i, 4, 2 * r + 1, ukv[:, :, bass.ds((i * 2 + r) * 2 * P, 2 * P)], CKV * 2 * P)

                    repeat(sp, 4, 2, HEADS, head_units)
                    V = W + 2 * HEADS
                    repeat(sp, 4, 2, KT, lambda i, r: load_unit(sp, V, i, 2, r, wo[:, :, bass.ds((i * 2 + r) * P, P)], KT * P))
                if name == "nsa":
                    w_in, wo = w_view(t["nsa_w_in"][j]), w_view(t["nsa_w_o"][j])
                    first = NSA_COL["kc"]
                    repeat(sp, 2, 2, 4, lambda i, r: load_unit(sp, U, i, 2, r, w_in[:, :, bass.ds((i * 2 + r) * P + first, P)], KT * P))
                    for w, w1 in enumerate(("nsa_w1_k", "nsa_w1_v")):
                        w1 = w_view(t[w1][j])
                        for hh in range(2):
                            repeat(sp, 2, 2, 4, lambda i, r: load_unit(
                                sp, U + 4 + 8 * w + 4 * hh, i, 2, r,
                                w1[:, bass.ds((i * 2 + r) * KT, KT), hh * P:(hh + 1) * P], KT * P))
                    for n, key in enumerate(("ks", "kw", "vs", "vw")):
                        for g in range(GROUPS):
                            c = NSA_COL[key] + g * P
                            load_unit(sp, U + 20, 0, 2, 2 * n + g, w_in[:, :, c:c + P], KT * P)
                    load_unit(sp, U + 28, 0, 2, 0, w_in[:, :, NSA_COL["gate"]:], KT * 3 * HEADS)
                    repeat(sp, 4, 2, HEADS, lambda i, r: load_unit(sp, U + 29, i, 2, r, w_in[:, :, bass.ds((i * 2 + r) * P, P)], KT * P))
                    V = U + 29 + HEADS
                    repeat(sp, 4, 2, KT, lambda i, r: load_unit(sp, V, i, 2, r, wo[:, :, bass.ds((i * 2 + r) * P, P)], KT * P))
                if name == "s5":
                    glu = w_view(t["s5_w_glu"][j])

                    def glu_pair(i, r):
                        for e in range(2):
                            load_unit(sp, U, i, 4, 2 * r + e, glu[:, :, bass.ds((i * 2 + r) * P + e * D, P)], KT * P)

                    repeat(sp, 4, 2, KT, glu_pair)
            sp.wait_ge(copied_in, N_TURN + KT + KT)
            sp.dma_start(out.rearrange("b (t p) f -> p (b t) f", p=P), out_rows[:]).then_inc(stored, 16)
            sp.wait_ge(stored, 16)

        @block.tensor
        def _(pe):
            state = [0]
            pe.wait_ge(params_in, 16 * (len(row_loads) + 1))
            pe.wait_ge(consts_in, 32)
            for n, (slot, size, _, _) in enumerate(turns):
                reached(pe, copied_in, n - 3)
                nc.tensor.transpose(bank[:, n % 4, 0:size], rows[0:size, slot, :], ident[0:size, 0:size]).then_inc(turned_in, 1)
            for k in range(KT):
                reached(pe, copied_in, N_TURN + k - 3)
                for tt in range(TT):
                    last = nc.tensor.transpose(bank[:, (N_TURN + k) % 4, tt * P:(tt + 1) * P],
                                               x_rows[:, tt, k * P:(k + 1) * P], ident[:, :])
                last.then_inc(turned_in, 1)
            def modulate(l, half):
                pe.wait_ge(ada_done, 2 * l_at[l] + half + 1)
                for f in range(MODS // 2):
                    last = nc.tensor.matmul(bank[:, 6, f:f + 1], ada_sum[:, f * P:(f + 1) * P], ones[:, 0:1], start=True, stop=True)
                last.then_inc(ada_turned, 1)

            def add_squares(idx, m, slot):
                pe.wait_ge(squares, m + (KT * idx + 1) if not isinstance(m, int) else KT * idx + m + 1)
                nc.tensor.matmul(bank[:, 7, :], ones[:, :], sq_x[:, slot, :], start=isinstance(m, int) and m == 0,
                                 stop=isinstance(m, int) and m == KT - 1, skip_group_check=True).then_inc(sq_used, 1)

            for half in range(2):
                modulate(LAYERS[0], half)
            for m in range(KT):
                add_squares(0, m, m % 2)
            end_phase(pe, state)

            def residual_units(unit, idx):
                unit(0, 0)
                unit(0, 1)
                add_squares(idx, 0, 0)
                with pe.Fori(1, KT // 2) as i:
                    for r in range(2):
                        unit(i, r)
                        add_squares(idx, i * 2 + (r - 1), (r + 1) % 2)
                add_squares(idx, KT - 1, 1)

            def normed(idx):
                return lambda k: pe.wait_ge(h_low, KT * idx + k + 1)

            def ffn(l, U, drains, idx):
                for half in range(2):
                    V, G = U + half * (2 * HALF + KT), drains + half * (2 * HALF + KT)

                    def up_pair(i, r):
                        for e in range(2):
                            u, b = 2 * r + e, 2 * (r % 2) + e
                            pe.wait_ge(lo_made, i * 4 + (V + u + 1))
                            reached(pe, drained, i * 4 + (G + u - 3))
                            first = half == 0 and r == 0 and e == 0
                            feature_product(bank[:, b, :], (V + u) % 2, KT, P, 0, h_hi, h_lo,
                                            normed(idx) if first else None).then_inc(weights_used, 1)

                    def down_unit(i, r):
                        W = V + 2 * HALF
                        pe.wait_ge(lo_made, i * 2 + (W + r + 1))
                        reached(pe, drained, i * 2 + (G + 2 * HALF + r - 1))
                        feature_product(bank[:, 4 + r, :], (W + r) % 2, HALF, P, 0, g_hi, g_lo).then_inc(weights_used, 1)

                    repeat(pe, 5, 2, HALF, up_pair, first=1)
                    if half == 1 and l in following:
                        modulate(following[l], 0)
                    pe.wait_ge(g_low, HALF * (2 * l_at[l] + half + 1))
                    if half == 0:
                        repeat(pe, 4, 2, KT, down_unit)
                    else:
                        residual_units(down_unit, idx + 1)
                if l in following:
                    modulate(following[l], 1)

            def output_projection(U, G, a_hi, a_lo, idx):
                def unit(i, r):
                    pe.wait_ge(lo_made, i * 2 + (U + r + 1))
                    pe.wait_ge(drained, i * 2 + (G + r - 1))
                    feature_product(bank[:, r, :], (U + r) % 2, KT, P, 0, a_hi, a_lo).then_inc(weights_used, 1)

                residual_units(unit, idx)

            def turn(p, r, probs):
                pe.wait_ge(scaled, p + 1)
                for j in range(TT):
                    for i in range(j, TT):
                        last = nc.tensor.transpose(turned_tile(r, j, i), probs[:, r, ROW_AT[i] + j * P:ROW_AT[i] + (j + 1) * P],
                                                   ident[:, :])
                last.then_inc(turned, 1)

            def values(p, r, turned_sb, v, first, last):
                pe.wait_ge(pt_act, p + 3)
                pe.wait_ge(pt_dve, p + 3)
                for j in range(TT):
                    ins = nc.tensor.matmul(bank[:, 6, j * P:S], v[:, j * P:(j + 1) * P],
                                           turned_sb[:, r, COL_AT[j]:COL_AT[j] + S - j * P],
                                           start=first and j == 0, stop=last and j == TT - 1, skip_group_check=True)
                return ins

            def mla(l, j, U, dr, idx, state):
                o = mla_at[l]
                for n in range(DKV_UNITS):
                    pe.wait_ge(lo_made, U + n + 1)
                    reached(pe, drained, dr + n - 1)
                    feature_product(bank[:, n % 2, :], (U + n) % 2, KT, P, 0, h_hi, h_lo,
                                    normed(idx) if n == 0 else None).then_inc(weights_used, 1)
                for n in range(CQ + CKV):
                    pe.wait_ge(drained, dr + n + 1)
                    last = nc.tensor.matmul(bank[:, 4 if n < CQ else 5, :], ones[:, :], sq[:, n, :],
                                            start=n in (0, CQ), stop=n in (CQ - 1, CQ + CKV - 1))
                    if n in (CQ - 1, CQ + CKV - 1):
                        last.then_inc(lat_summed, 1)
                end_phase(pe, state)
                W, pb = U + DKV_UNITS, passes_at[l]

                def project(i, r):
                    s, c = r % 2, 4 * (HEADS * o + r)
                    pe.wait_ge(lo_made, i * 4 + (W + 2 * r + 1))
                    reached(pe, fetched, i * 8 + c)
                    feature_product(bank[:, 7, :], W % 2, CQ, QK, 0, c_hi, c_lo).then_inc(projected, 1)
                    pe.wait_ge(fetched, i * 8 + (c + 1))
                    feature_product(bank[:, 7, :], W % 2, CQ, QK, QK - P, c_hi, c_lo).then_inc(weights_used, 1)
                    pe.wait_ge(lo_made, i * 4 + (W + 2 * r + 2))
                    pe.wait_ge(fetched, i * 8 + (c + 2))
                    feature_product(bank[:, 7, :], (W + 1) % 2, CKV, 2 * P, 0, c_hi[:, CQ:], c_lo[:, CQ:]).then_inc(projected, 1)
                    pe.wait_ge(fetched, i * 8 + (c + 3))
                    token_product(bank[:, 7, :], (W + 1) % 2, CKV, 2 * P, P, P, c_hi[:, CQ:], c_lo[:, CQ:]) \
                        .then_inc(weights_used, 1)

                def scores(i, r):
                    s = r % 2
                    pe.wait_ge(fetched, i * 8 + 4 * (HEADS * o + r + 1))
                    pe.wait_ge(roped, i * 2 + (HEADS * o + r + 1))
                    pe.wait_ge(pt_act, i * 2 + (pb + r + 1))
                    pe.wait_ge(pt_dve, i * 2 + (pb + r + 1))
                    for q in reversed(range(TT)):
                        at, n = slice(q * P, (q + 1) * P), P * (q + 1)
                        nc.tensor.matmul(score_tile(s, q), q_nope[:, s, at], k_nope[:, s, 0:n], start=True, stop=False)
                        nc.tensor.matmul(score_tile(s, q), q_rope[:, s, at], k_rope[:, 0:n], start=False, stop=False)
                        last = nc.tensor.matmul(score_tile(s, q)[:, n - P:n], ident_b[:, :], mask_b[:, :], start=False, stop=True)
                    last.then_inc(scored, 1)

                def head(i, r):
                    s = r % 2
                    whole = not isinstance(i, int)
                    if whole or 2 * i + r + 1 < HEADS:
                        scores(i, r + 1)
                    turn(i * 2 + (pb + r), s, m_probs)
                    pe.wait_ge(o_low, i * 2 + (heads_at[l] + r + 1))
                    values(i * 2 + (pb + r), s, m_turned, v_tok[:, s, :], True, True).then_inc(valued, 1)
                    if whole or 2 * i + r + 2 < HEADS:
                        project(i, r + 2)

                project(0, 0)
                scores(0, 0)
                project(0, 1)
                repeat(pe, 3, 2, HEADS, head)
                end_phase(pe, state)
                output_projection(W + 2 * HEADS, dr + DKV_UNITS, h_hi, h_lo, idx + 1)
            def nsa(l, j, U, dr, idx, state):
                for n in range(4):
                    pe.wait_ge(lo_made, U + n + 1)
                    reached(pe, drained, dr + n - 1)
                    feature_product(bank[:, n % 2, :], (U + n) % 2, KT, P, 0, h_hi, h_lo,
                                    normed(idx) if n == 0 else None).then_inc(weights_used, 1)
                pe.wait_ge(nsa_side, 16 * 8)
                for w in range(2):
                    nc.tensor.transpose(bank[:, 4, w * CB:(w + 1) * CB], pe_rows[:, w, :], ident[0:CB, 0:CB])
                nc.tensor.transpose(bank[0:BUCKETS, 5, 0:HEADS], rel[:, :], ident[0:HEADS, 0:HEADS]).then_inc(nsa_small, 1)
                pe.wait_ge(nsa_copied, 1)
                nc.tensor.matmul(bank[0:HEADS, 6, 0:3 * P], rel_t[:, :], near_hot[:, :], start=True, stop=True)
                for w in range(2):
                    last = nc.tensor.matmul(bank[0:HEADS, 2 + w, :], rel_t[:, :], far_hot[:, w * S:(w + 1) * S], start=True, stop=True)
                last.then_inc(nsa_small, 1)
                end_phase(pe, state)
                for w in range(2):
                    for hh in range(2):
                        n = 2 * w + hh
                        for q in range(4):
                            s = (U + 4 + 4 * n + q) % 2
                            pe.wait_ge(lo_made, U + 4 + 4 * n + q + 1)
                            if q == 0:
                                pe.wait_ge(drained, dr + 4 + n - 1)
                            for c in range(KT):
                                at = slice(c * P, (c + 1) * P)
                                last = three(bank[:, n % 2, 0:GROUPS * NC], w_hi[:, s, at], w_lo[:, s, at],
                                             b_hi[:, w, q * KT + c, :, :], b_lo[:, w, q * KT + c, :, :],
                                             q == 0 and c == 0, q == 3 and c == KT - 1)
                            last.then_inc(weights_used, 1)
                pe.wait_ge(drained, dr + 8)
                for hh in range(2):
                    nc.tensor.matmul(bank[:, 4, 0:GROUPS * NC], w2[:, 0, hh, :], hid[:, 0, hh, :], start=hh == 0, stop=hh == 1)
                for g in range(GROUPS):
                    for hh in range(2):
                        last = nc.tensor.matmul(bank[0:NC, 5, g * P:(g + 1) * P], hid[:, 1, hh, g * NC:(g + 1) * NC], w2[:, 1, hh, :],
                                                start=hh == 0, stop=hh == 1)
                last.then_inc(nsa_small, 1)
                end_phase(pe, state)
                for n in range(9):
                    pe.wait_ge(lo_made, U + 20 + n + 1)
                    pe.wait_ge(drained, dr + 8 + n - 1)
                    s, b = (U + 20 + n) % 2, bank[:, n % 2, :]
                    if n < 4:
                        last = feature_product(b, s, KT, P, 0, h_hi, h_lo)
                    elif n < 8:
                        last = token_product(b, s, KT, P, 0, P, h_hi, h_lo)
                    else:
                        last = token_product(b, s, KT, 3 * HEADS, 0, 3 * HEADS, h_hi, h_lo)
                    last.then_inc(weights_used, 1)
                pe.wait_ge(rows_back, 16)
                for n in range(4):
                    last = nc.tensor.matmul(bank[:, 2 + n, :], flip[:, :], near_back[:, 2 * n:2 * n + 2, :], start=True, stop=True)
                last.then_inc(nsa_small, 1)
                pe.wait_ge(nsa_copied, 3)
                pe.wait_ge(rows_back, 32)
                for tt in range(TT):
                    for h in range(HEADS):
                        last = nc.tensor.matmul(bank[:, 2 + tt, h * NC:(h + 1) * NC], cmp_back[:, h, tt * P:(tt + 1) * P],
                                                flip[0:NC, P - NC:P], start=True, stop=True)
                last.then_inc(nsa_small, 1)
                end_phase(pe, state)

                W, pb, hb = U + 29, passes_at[l], heads_at[l]

                def project(h):
                    pe.wait_ge(lo_made, W + h + 1)
                    reached(pe, bank7_free, 3 * h)
                    feature_product(bank[:, 7, :], (W + h) % 2, KT, P, 0, h_hi, h_lo).then_inc(weights_used, 1)

                def scores(h, w):
                    pe.wait_ge(q_ready, h + 1)
                    p = pb + 2 * h + w
                    pe.wait_ge(pt_act, p + 1)
                    pe.wait_ge(pt_dve, p + 1)
                    for q in reversed(range(TT)):
                        last = nc.tensor.matmul(score_tile(w, q), q_t[:, h % 2, q * P:(q + 1) * P],
                                                kf[:, 2 * w + h // HPG, 0:P * (q + 1)], start=True, stop=True)
                    last.then_inc(scored, 1)

                project(0)
                scores(0, 0)
                for h in range(HEADS):
                    g = h // HPG
                    pe.wait_ge(bank7_free, 3 * h + 1)
                    for q in range(TT):
                        last = nc.tensor.matmul(bank[:, 7, q * NC:(q + 1) * NC], q_t[:, h % 2, q * P:(q + 1) * P], kc_t[:, g, :],
                                                start=True, stop=True)
                    last.then_inc(cmp_scored, 1)
                    scores(h, 1)
                    turn(pb + 2 * h, 0, n_probs)
                    pe.wait_ge(o_low, hb + h + 1)
                    values(pb + 2 * h, 0, n_turned, vt[:, g, :], True, False)
                    pe.wait_ge(cmp_scaled, h + 1)
                    for q in range(TT):
                        last = nc.tensor.transpose(bank[0:NC, 7, q * P:(q + 1) * P], cmp_p[:, q, :], ident[:, :])
                    last.then_inc(cmp_turned, 1)
                    pe.wait_ge(bank7_free, 3 * h + 3)
                    nc.tensor.matmul(bank[:, 6, :], vc_t[:, g, :], cmp_t[:, :], start=False, stop=False, skip_group_check=True)
                    if h + 1 < HEADS:
                        project(h + 1)
                        scores(h + 1, 0)
                    turn(pb + 2 * h + 1, 1, n_probs)
                    values(pb + 2 * h + 1, 1, n_turned, vt[:, GROUPS + g, :], False, True).then_inc(valued, 1)
                end_phase(pe, state)
                output_projection(W + HEADS, dr + 17, o_hi, o_lo, idx + 1)
            def s5(l, j, U, dr, idx, state):
                pe.wait_ge(s5_side, 16 * 9)
                pe.wait_ge(s5_dve, 1)
                for n in range(3):
                    last = nc.tensor.transpose(bank[:, 0, n * ST:(n + 1) * ST], lam_rows[:, n, :], ident[0:ST, 0:ST])
                last.then_inc(s5_small, 1)
                for k in range(KT):
                    for w in range(2):
                        n = 2 * k + w
                        reached(pe, s5_act, n - 1)
                        nc.tensor.transpose(bank[:, 1 + n % 2, 0:P], c_rows[:, w, k, :, :], ident[:, :]).then_inc(s5_small, 1)
                pe.wait_ge(s5_dve, 2)
                for k in range(KT):
                    for w in range(2):
                        n = 2 * k + w
                        pe.wait_ge(s5_act, 16 + n - 1)
                        nc.tensor.transpose(bank[:, 1 + n % 2, 0:P], b_bar[:, w, 4 * k:4 * k + 4, :], ident[:, :]).then_inc(s5_small, 1)
                end_phase(pe, state)

                def enter(q):
                    k, a, r = q // 4, 32 * (q % 4), q % 2
                    reached(pe, bu_free, q - 1)
                    for w in range(2):
                        last = nc.tensor.matmul(bank[:, 2 * r + w, :], in_map[a:a + 32, w, k, :], hf[a:a + 32, k, :],
                                                start=True, stop=True)
                    last.then_inc(bu_made, 1)

                enter(0)
                enter(1)
                for q in range(ST):
                    k, a, r = q // 4, q % 4, q % 2
                    if q + 2 < ST:
                        enter(q + 2)
                    pe.wait_ge(x_made, q + 1)
                    if a == 0:
                        reached(pe, y_in, k - 1)
                    for w in range(2):
                        last = nc.tensor.matmul(bank[:, 4 + k % 2, :], out_map[:, w, k, a * P:(a + 1) * P], state_w[:, r, 2 * w, :],
                                                start=(a == 0 and w == 0), stop=(a == 3 and w == 1))
                    if a == 3:
                        last.then_inc(y_made, 1)
                    else:
                        last.then_inc(products_used, 1)
                end_phase(pe, state)

                def glu_pair(i, r):
                    for e in range(2):
                        u = 2 * r + e
                        pe.wait_ge(lo_made, i * 4 + (U + u + 1))
                        reached(pe, drained, i * 4 + (dr + 2 * r - 2))
                        feature_product(bank[:, u, :], (U + u) % 2, KT, P, 0, h_hi, h_lo).then_inc(weights_used, 1)

                glu_pair(0, 0)
                glu_pair(0, 1)
                add_squares(idx + 1, 0, 0)
                with pe.Fori(1, KT // 2) as i:
                    for r in range(2):
                        glu_pair(i, r)
                        add_squares(idx + 1, i * 2 + (r - 1), (r + 1) % 2)
                add_squares(idx + 1, KT - 1, 1)
            for name, l, j, U, dr, idx in plan:
                if name == "norm":
                    continue
                elif name == "mla":
                    mla(l, j, U, dr, idx, state)
                elif name == "nsa":
                    nsa(l, j, U, dr, idx, state)
                elif name == "s5":
                    s5(l, j, U, dr, idx, state)
                elif name == "ffn":
                    ffn(l, U, dr, idx)
                else:
                    for k in range(KT):
                        pe.wait_ge(h_made, KT * idx + k + 1)
                        reached(pe, copied_in, N_TURN + KT + k - 1)
                        for tt in range(TT):
                            last = nc.tensor.transpose(bank[:, 4 + k % 2, tt * P:(tt + 1) * P],
                                                       hf[:, k, tt * P:(tt + 1) * P], ident[:, :])
                        last.then_inc(turned_in, 1)
                end_phase(pe, state)

        @block.scalar
        def _(act):
            state, chain = [0], Chain(act, act_chain)
            act.wait_ge(c_in, 16)
            nc.scalar.activation(c_act[:, :], c_act[:, :], ACT.Silu).then_inc(silu_made, 1)

            def square(idx, m):
                reached(act, sq_used, KT * idx + m - 1)
                nc.scalar.activation(sq_x[:, m % 2, :], x[:, m, :], ACT.Square).then_inc(squares, 1)

            for m in range(KT):
                act.wait_ge(copied_in, N_TURN + m + 1)
                square(0, m)
            end_phase(act, state)

            def norm(idx, split):
                act.wait_ge(sq_used, KT * (idx + 1))
                nc.scalar.activation(rs[:, :], bank[:, 7, :], ACT.Sqrt, bias=eps[:, :], scale=1.0 / D).then_inc(rooted, 1)
                for k in range(KT if split else 0):
                    act.wait_ge(h_made, KT * idx + k + 1)
                    nc.scalar.copy(h_hi[:, k, :], hf[:, k, :]).then_inc(h_high, 1)

            def residual_splits(U, G, idx, width):
                for n in range(2):
                    split_high(act, U, 0, 2, n, width)
                for n in range(KT):
                    if n + 2 < KT:
                        split_high(act, U, 0, 2, n + 2, width)
                    if idx is not None:
                        act.wait_ge(drained, G + n + 1)
                        square(idx, n)

            def ffn(l, U, drains, idx):
                for half in range(2):
                    V, G = U + half * (2 * HALF + KT), drains + half * (2 * HALF + KT)
                    Q = HALF * (2 * l_at[l] + half)
                    nc.scalar.preload_act_table(ACT.Silu)
                    for e in range(2):
                        split_high(act, V, 0, 4, e, KT * P)

                    def up_pair(i, r):
                        if not (isinstance(i, int) and 2 * i + r + 1 >= HALF):
                            for e in range(2):
                                split_high(act, V, i, 4, 2 * (r + 1) + e, KT * P)
                        act.wait_ge(g_made, i * 2 + (Q + r + 1))
                        s = r % 2
                        for e in range(2):
                            u, col = 2 * r + e, l * CHT + e * PAIRS + half * HALF
                            act.wait_ge(weights_used, i * 4 + (V + u + 1))
                            nc.scalar.activation(cv[:, s, e, :], bank[:, 2 * s + e, :], ACT.Identity,
                                                 bias=cb[:, bass.ds(i * 2 + (col + r), 1)],
                                                 scale=cw[:, bass.ds(i * 2 + ((TAPS * l + 2) * CHT + col - l * CHT + r), 1)]
                                                 ).then_inc(cv_made, 1)
                        act.wait_ge(drained, i * 4 + (G + 2 * r + 2))
                        nc.scalar.activation(sg[:, s, :], cv[:, s, 1, :], ACT.Silu).then_inc(silu_made, 1)
                        act.wait_ge(g_made, i * 2 + (Q + r + 3))
                        nc.scalar.copy(g_hi[:, bass.ds(i * 2 + r, 1), :], gf[:, s:s + 1, :]).then_inc(g_high, 1)

                    repeat(act, 4, 2, HALF, up_pair, first=1)
                    residual_splits(V + 2 * HALF, G + 2 * HALF, idx + 1 if half == 1 else None, UNIT)

            def exponents(p, r, probs):
                act.wait_ge(maxed, p + 1)
                for q in reversed(range(TT)):
                    last = nc.scalar.activation(probs[:, r, ROW_AT[q]:ROW_AT[q] + P * (q + 1)], score_tile(r, q), ACT.Exp,
                                                bias=neg_max[:, r, q:q + 1], accum_out=row_sum[:, r, q:q + 1])
                last.then_inc(exped, 1)

            def copy_turned(p, r, turned_sb):
                act.wait_ge(turned, p + 1)
                nc.scalar.copy(turned_sb[:, r, 0:S], bank[:, 3 * r, :]).then_inc(pt_act, 1)

            def head_high(h, m, dst):
                act.wait_ge(valued, h + 1)
                nc.scalar.copy(dst[:, m, :] if isinstance(m, int) else dst[:, bass.ds(m, 1), :].squeeze(1), bank[:, 6, :]) \
                    .then_inc(o_high, 1)

            def mla(l, j, U, dr, idx, state):
                o = mla_at[l]
                split_high(act, U, 0, 2, 0, KT * P)
                for n in range(DKV_UNITS):
                    if n + 1 < DKV_UNITS:
                        split_high(act, U, 0, 2, n + 1, KT * P)
                    act.wait_ge(weights_used, U + n + 1)
                    b = bank[:, n % 2, :]
                    if n < CQ + CKV:
                        nc.scalar.copy(hf[:, n, :], b)
                        nc.scalar.activation(sq[:, n, :], b, ACT.Square).then_inc(drained, 1)
                    else:
                        half = ROPE // 2
                        nc.scalar.copy(k_rope[:, :], b[ROPE:P])
                        nc.scalar.copy(swapped[0:half, 0, :], b[P - half:P])
                        nc.scalar.copy(swapped[half:ROPE, 0, :], b[ROPE:P - half]).then_inc(drained, 1)
                for b, dst, count in ((4, rs, Q_LORA), (5, rs_kv, KV_LORA)):
                    act.wait_ge(lat_summed, 2 * o + b - 3)
                    nc.scalar.activation(dst[:, :], bank[:, b, :], ACT.Sqrt, bias=eps[:, :], scale=1.0 / count).then_inc(lat_rooted, 1)
                for n in range(CQ + CKV):
                    act.wait_ge(c_made, 6 * o + n + 1)
                    nc.scalar.copy(c_hi[:, n, :], hf[:, n, :]).then_inc(c_high, 1)
                end_phase(act, state)
                W, pb = U + DKV_UNITS, passes_at[l]

                def splits(i, r):
                    split_high(act, W, i, 4, 2 * r, CQ * QK)
                    split_high(act, W, i, 4, 2 * r + 1, CKV * 2 * P)

                def fetch(i, r):
                    s, c, half = r % 2, 4 * (HEADS * o + r), ROPE // 2
                    act.wait_ge(projected, i * 4 + (2 * (HEADS * o + r) + 1))
                    nc.scalar.mul(q_nope[:, s, :], bank[:, 7, :], MLA_SCALE).then_inc(fetched, 1)
                    act.wait_ge(weights_used, i * 4 + (W + 2 * r + 1))
                    nc.scalar.mul(q_rope[:, s, :], bank[ROPE:P, 7, :], MLA_SCALE)
                    nc.scalar.mul(swapped[0:half, s, :], bank[P - half:P, 7, :], MLA_SCALE)
                    nc.scalar.mul(swapped[half:ROPE, s, :], bank[ROPE:P - half, 7, :], MLA_SCALE).then_inc(fetched, 1)
                    act.wait_ge(fetched, i * 8 + (c + 3))
                    act.wait_ge(weights_used, i * 4 + (W + 2 * r + 2))
                    nc.scalar.copy(v_tok[:, s, :], bank[:, 7, :]).then_inc(fetched, 1)

                def head(i, r):
                    s, whole = r % 2, not isinstance(i, int)
                    if whole or 2 * i + r + 2 < HEADS:
                        splits(i, r + 2)
                    if whole or 2 * i + r + 1 < HEADS:
                        exponents(i * 2 + (pb + r + 1), 1 - s, m_probs)
                    copy_turned(i * 2 + (pb + r), s, m_turned)
                    head_high(i * 2 + (heads_at[l] + r), i * 2 + r, h_hi)
                    if whole or 2 * i + r + 2 < HEADS:
                        fetch(i, r + 2)

                splits(0, 0)
                fetch(0, 0)
                splits(0, 1)
                exponents(pb, 0, m_probs)
                fetch(0, 1)
                nc.scalar.preload_act_table(ACT.Exp)
                repeat(act, 3, 2, HEADS, head)
                end_phase(act, state)
                residual_splits(W + 2 * HEADS, dr + DKV_UNITS, idx + 1, KT * P)
            def nsa(l, j, U, dr, idx, state):
                for n in range(4):
                    split_high(act, U, 0, 2, n, KT * P)
                for n in range(4):
                    act.wait_ge(b_made, n + 1)
                    nc.scalar.copy(b_hi[:, n // 2, (n % 2) * CS:(n % 2 + 1) * CS], b_new[:, n % 2]).then_inc(b_high, 1)
                end_phase(act, state)
                split_high(act, U + 4, 0, 2, 0, KT * P)
                for n in range(16):
                    if n + 1 < 16:
                        split_high(act, U + 4, 0, 2, n + 1, KT * P)
                    if n % 4 == 3:
                        act.wait_ge(weights_used, U + 4 + n + 1)
                        nc.scalar.activation(hid[:, n // 8, (n // 4) % 2, :], bank[:, (n // 4) % 2, 0:GROUPS * NC],
                                             ACT.Gelu_apprx_tanh).then_inc(drained, 1)
                end_phase(act, state)
                for n in range(9):
                    split_high(act, U + 20, 0, 2, n, KT * (P if n < 8 else 3 * HEADS))
                act.wait_ge(weights_used, U + 29)
                nc.scalar.activation(gates[:, :, :], bank[:, 0, 0:TT * 3 * HEADS], ACT.Sigmoid).then_inc(drained, 1)
                end_phase(act, state)
                W, pb, hb = U + 29, passes_at[l], heads_at[l]

                def fetch(h):
                    act.wait_ge(weights_used, W + h + 1)
                    nc.scalar.mul(q_t[:, h % 2, :], bank[:, 7, :], NSA_SCALE).then_inc(q_ready, 1)

                split_high(act, W, 0, 2, 0, KT * P)
                fetch(0)
                exponents(pb, 0, n_probs)
                for h in range(HEADS):
                    if h + 1 < HEADS:
                        split_high(act, W, 0, 2, h + 1, KT * P)
                    act.wait_ge(cmp_maxed, h + 1)
                    for q in range(TT):
                        last = nc.scalar.activation(cmp_p[:, q, :], cmp_p[:, q, :], ACT.Exp, bias=cmp_max[:, q:q + 1],
                                                    accum_out=cmp_sum[:, q:q + 1])
                    last.then_inc(cmp_exped, 1)
                    exponents(pb + 2 * h + 1, 1, n_probs)
                    copy_turned(pb + 2 * h, 0, n_turned)
                    act.wait_ge(cmp_turned, h + 1)
                    nc.scalar.copy(cmp_t[:, :], bank[0:NC, 7, :]).then_inc(bank7_free, 1)
                    if h + 1 < HEADS:
                        fetch(h + 1)
                        exponents(pb + 2 * h + 2, 0, n_probs)
                    copy_turned(pb + 2 * h + 1, 1, n_turned)
                    head_high(hb + h, h, o_hi)
                end_phase(act, state)
                residual_splits(W + HEADS, dr + 17, idx + 1, KT * P)
            def s5(l, j, U, dr, idx, state):
                act.wait_ge(s5_ready, 1)
                nc.scalar.activation(small[:, 11, :], small[:, 11, :], ACT.Exp).then_inc(s5_exp, 1)
                for k in range(KT):
                    for w in range(2):
                        n = 2 * k + w
                        act.wait_ge(s5_small, 2 + n)
                        src = bank[:, 1 + n % 2, 0:P].rearrange("p (q i) -> p q i", q=4)
                        dst = out_map[:, w, k, 0:640].rearrange("p (q i) -> p q i", q=4)
                        nc.scalar.mul(dst[0:SN, :, 0:SI], src[0:SN, :, 0:SI], 1.0 - 2 * w)
                        nc.scalar.mul(dst[SN:P, :, SI:2 * SI], src[SN:P, :, SI:2 * SI], 1.0 - 2 * w).then_inc(s5_act, 1)
                act.wait_ge(s5_dve2, 1)
                nc.scalar.activation(small[:, 5, :], small[:, 3, :], ACT.Exp).then_inc(s5_exp, 1)
                nc.scalar.activation(small[:, 6, :], small[:, 4, :], ACT.Sin)
                nc.scalar.activation(small[:, 7, :], small[:, 4, :], ACT.Sin, scale=0.5).then_inc(s5_exp, 1)
                for n in range(2 * KT):
                    act.wait_ge(s5_small, 18 + n)
                    nc.scalar.copy(in_map[:, n % 2, n // 2, :], bank[:, 1 + n % 2, 0:P]).then_inc(s5_act, 1)
                end_phase(act, state)
                for k in range(KT):
                    act.wait_ge(y_in, k + 1)
                    nc.scalar.activation(hf[:, k, :], hf[:, k, :], ACT.Gelu_apprx_tanh).then_inc(y_gelu, 1)
                    act.wait_ge(y_gelu, k + 1)
                    nc.scalar.copy(h_hi[:, k, :], hf[:, k, :]).then_inc(y_high, 1)
                end_phase(act, state)
                for e in range(2):
                    split_high(act, U, 0, 4, e, KT * P)

                def glu_pair(i, r):
                    if not (isinstance(i, int) and 2 * i + r + 1 >= KT):
                        for e in range(2):
                            split_high(act, U, i, 4, 2 * (r + 1) + e, KT * P)
                    act.wait_ge(weights_used, i * 4 + (U + 2 * r + 2))
                    nc.scalar.activation(sig[:, r, :], bank[:, 2 * r + 1, :], ACT.Sigmoid).then_inc(sig_made, 1)

                for n in range(KT):
                    glu_pair(n // 2, n % 2)
                    if n:
                        act.wait_ge(drained, dr + 2 * n)
                        square(idx + 1, n - 1)
                act.wait_ge(drained, dr + 2 * KT)
                square(idx + 1, KT - 1)
            for name, l, j, U, dr, idx in plan:
                if name == "norm":
                    norm(idx, True)
                    continue
                elif name == "mla":
                    mla(l, j, U, dr, idx, state)
                elif name == "nsa":
                    nsa(l, j, U, dr, idx, state)
                elif name == "s5":
                    s5(l, j, U, dr, idx, state)
                elif name == "ffn":
                    ffn(l, U, dr, idx)
                else:
                    norm(idx, False)
                end_phase(act, state)

        @block.vector
        def _(dve):
            state, chain = [0], Chain(dve, dve_chain)
            chain.link(nc.vector.memset(ones[:, :], 1.0))
            chain.link(nc.vector.memset(eps[:, :], EPS))
            dve.wait_ge(consts_in, 32)
            chain.link(nc.vector.tensor_copy(ident_b[:, :], ident[:, :]))
            chain.link(nc.vector.tensor_copy(mask_b[:, :], mask[:, :]))
            for n, (slot, size, dst, col) in enumerate(turns):
                dve.wait_ge(turned_in, n + 1)
                nc.vector.tensor_copy(dst[:, col:col + size], bank[:, n % 4, 0:size]).then_inc(copied_in, 1)
            for k in range(KT):
                dve.wait_ge(turned_in, N_TURN + k + 1)
                nc.vector.tensor_copy(x[:, k, :], bank[:, (N_TURN + k) % 4, :]).then_inc(copied_in, 1)
            dve.wait_ge(silu_made, 1)

            def ada_piece(l, n):
                g = 2 * KT * l_at[l] + n
                dve.wait_ge(ada_in[g % 2], 16 * (g // 2 + 1))
                reached(dve, ada_used, g)
                if n % KT == 0:
                    reached(dve, ada_turned, g // KT)
                    ins = nc.vector.tensor_scalar(ada_sum, ada_w[:, g % 2, :], c_act[:, 0:1], None, ALU.mult)
                else:
                    ins = nc.vector.scalar_tensor_tensor(out=ada_sum, in0=ada_w[:, g % 2, :], scalar=c_act[:, n % KT:n % KT + 1],
                                                         in1=ada_sum, op0=ALU.mult, op1=ALU.add)
                ins.then_inc(ada_used, 1)
                if n % KT == KT - 1:
                    dve.wait_ge(ada_used, g + 1)
                    dve.sem_inc(ada_done, 1)

            def take_modulation(l, half):
                dve.wait_ge(ada_turned, 2 * l_at[l] + half + 1)
                a = mod_col(l, 3 * half, 0)
                at = mod[:, a:a + MODS // 2]
                chain.link(nc.vector.tensor_tensor(at, bank[:, 6, 0:MODS // 2], at, ALU.add))
                g = 32 * half + KT * l
                chain.link(nc.vector.scalar_tensor_tensor(
                    out=amp[:, (2 * l + half) * KT:(2 * l + half + 1) * KT], in0=mod[:, a + KT:a + 2 * KT], scalar=1.0,
                    in1=misc[:, g:g + KT], op0=ALU.add, op1=ALU.mult))

            for half in range(2):
                for n in range(KT):
                    ada_piece(LAYERS[0], half * KT + n)
                take_modulation(LAYERS[0], half)
            end_phase(dve, state)


            def norm(l, which, idx):
                dve.wait_ge(rooted, idx + 1)
                nc.vector.reciprocal(rs[:, :], rs[:, :]).then_inc(rs_made, 1)

                def low(k):
                    dve.wait_ge(h_high, KT * idx + k + 1)
                    dve.wait_ge(h_made, KT * idx + k + 1)
                    nc.vector.tensor_tensor(h_lo[:, k, :], hf[:, k, :], h_hi[:, k, :].bitcast(F32), ALU.subtract).then_inc(h_low, 1)

                for k in range(KT):
                    dve.wait_ge(x_scaled, KT * idx + k + 1)
                    if which == 2:
                        a = NORM_COLS["final"] + k
                        nc.vector.tensor_scalar(hf[:, k, :], hf[:, k, :], misc[:, a:a + 1], None, ALU.mult).then_inc(h_made, 1)
                    else:
                        a, b = (2 * l + which) * KT + k, mod_col(l, 3 * which, k)
                        nc.vector.tensor_scalar(hf[:, k, :], hf[:, k, :], amp[:, a:a + 1], mod[:, b:b + 1],
                                                ALU.mult, ALU.add).then_inc(h_made, 1)
                        if k:
                            low(k - 1)
                if which != 2:
                    low(KT - 1)

            def residual(l, part, m, src, mark):
                nc.vector.scalar_tensor_tensor(
                    out=x[:, bass.ds(m, 1), :].squeeze(1) if not isinstance(m, int) else x[:, m, :], in0=src,
                    scalar=mod[:, bass.ds(m + mod_col(l, part, 0), 1)],
                    in1=x[:, bass.ds(m, 1), :].squeeze(1) if not isinstance(m, int) else x[:, m, :],
                    op0=ALU.mult, op1=ALU.add).then_inc(mark, 1)

            def residual_lows(l, part, U, b, width, ada_half=None):
                for n in range(2):
                    split_low(dve, U, 0, 2, n, width)
                for n in range(KT):
                    if n + 2 < KT:
                        split_low(dve, U, 0, 2, n + 2, width)
                    dve.wait_ge(weights_used, U + n + 1)
                    residual(l, part, n, bank[:, b + n % 2, :], drained)
                    if ada_half is not None and l in following:
                        ada_piece(following[l], ada_half * KT + n)

            def ffn(l, U, drains, idx):
                for half in range(2):
                    V, G = U + half * (2 * HALF + KT), drains + half * (2 * HALF + KT)
                    Q = HALF * (2 * l_at[l] + half)
                    for e in range(2):
                        split_low(dve, V, 0, 4, e, KT * P)

                    def up_pair(i, r):
                        if not (isinstance(i, int) and 2 * i + r + 1 >= HALF):
                            for e in range(2):
                                split_low(dve, V, i, 4, 2 * (r + 1) + e, KT * P)
                        s = r % 2
                        for tap in (1, 0):
                            back = 2 - tap
                            for e in range(2):
                                if tap == 1:
                                    dve.wait_ge(cv_made, i * 4 + (2 * Q + 2 * r + e + 1))
                                col = (TAPS * l + tap) * CHT + e * PAIRS + half * HALF
                                ins = nc.vector.scalar_tensor_tensor(
                                    out=cv[:, s, e, back:], in0=bank[:, 2 * s + e, 0:S - back],
                                    scalar=cw[:, bass.ds(i * 2 + (col + r), 1)], in1=cv[:, s, e, back:],
                                    op0=ALU.mult, op1=ALU.add)
                                if tap == 1:
                                    chain.step(ins)
                                else:
                                    ins.then_inc(drained, 1)
                            if tap == 1:
                                chain.wait()
                        dve.wait_ge(silu_made, i * 2 + (1 + Q + r + 1))
                        dve.wait_ge(drained, i * 4 + (G + 2 * r + 2))
                        nc.vector.tensor_tensor(gf[:, s, :], cv[:, s, 0, :], sg[:, s, :], ALU.mult).then_inc(g_made, 1)
                        dve.wait_ge(g_high, i * 2 + (Q + r + 1))
                        dve.wait_ge(g_made, i * 2 + (Q + r + 3))
                        nc.vector.tensor_tensor(g_lo[:, bass.ds(i * 2 + r, 1), :], gf[:, s:s + 1, :],
                                                g_hi[:, bass.ds(i * 2 + r, 1), :].bitcast(F32),
                                                ALU.subtract).then_inc(g_low, 1)

                    repeat(dve, 4, 2, HALF, up_pair, chain, 2, first=1)
                    if half == 1 and l in following:
                        take_modulation(following[l], 0)
                    residual_lows(l, 5, V + 2 * HALF, 4, UNIT, half)
                if l in following:
                    take_modulation(following[l], 1)

            def maxima(p, r, bias=None):
                dve.wait_ge(scored, p + 1)
                if bias is not None:
                    for q in reversed(range(TT)):
                        n = P * (q + 1)
                        w = min(n, FAR)
                        dst = score_tile(r, q)[:, n - w:n]
                        chain.step(nc.vector.tensor_tensor(dst, dst, bias[:, FAR - w:FAR], ALU.add))
                    chain.wait()
                for q in reversed(range(TT)):
                    last = nc.vector.tensor_reduce(neg_max[:, r, q:q + 1], score_tile(r, q), AX, ALU.max, negate=True)
                last.then_inc(maxed, 1)

            def factors(p, r, gate=None):
                dve.wait_ge(exped, p + 1)
                chain.link(nc.vector.tensor_scalar(row_sum[:, r, :], row_sum[:, r, :], 1e-30, None, ALU.max))
                if gate is None:
                    nc.vector.reciprocal(factor[:, r, :], row_sum[:, r, :]).then_inc(factored, 1)
                else:
                    chain.link(nc.vector.reciprocal(factor[:, r, :], row_sum[:, r, :]))
                    nc.vector.tensor_tensor(factor[:, r, :], factor[:, r, :], gate, ALU.mult).then_inc(factored, 1)

            def copy_turned(p, r, turned_sb):
                dve.wait_ge(turned, p + 1)
                nc.vector.tensor_copy(turned_sb[:, r, S:TRI].rearrange("p (b n) -> p b n", b=2),
                                      bank[:, 3 * r + 1:3 * r + 3, 0:3 * P]).then_inc(pt_dve, 1)

            def head_low(h, m, dst, high):
                dve.wait_ge(o_high, h + 1)
                if isinstance(m, int):
                    a, b = dst[:, m, :], high[:, m, :]
                else:
                    a, b = dst[:, bass.ds(m, 1), :].squeeze(1), high[:, bass.ds(m, 1), :].squeeze(1)
                nc.vector.tensor_tensor(a, bank[:, 6, :], b.bitcast(F32), ALU.subtract).then_inc(o_low, 1)

            def rotate(dst, swap, mark=None):
                chain.step(nc.vector.tensor_tensor(dst, dst, rope[:, 0, :], ALU.mult))
                chain.link(nc.vector.tensor_tensor(swap, swap, rope[:, 1, :], ALU.mult))
                ins = nc.vector.tensor_tensor(dst, dst, swap, ALU.add)
                if mark is not None:
                    ins.then_inc(mark, 1)

            def mla(l, j, U, dr, idx, state):
                o = mla_at[l]
                for n in range(DKV_UNITS):
                    split_low(dve, U, 0, 2, n, KT * P)
                dve.wait_ge(mla_side, 16 * (o + 1))
                dve.wait_ge(drained, dr + DKV_UNITS)
                rotate(k_rope[:, :], swapped[:, 0, :])
                dve.wait_ge(lat_rooted, 2 * o + 2)
                chain.step(nc.vector.reciprocal(rs[:, :], rs[:, :]))
                chain.link(nc.vector.reciprocal(rs_kv[:, :], rs_kv[:, :]))
                for n in range(CQ + CKV):
                    g = NORM_COLS["gq"] + CQ * j + n if n < CQ else NORM_COLS["gkv"] + CKV * j + n - CQ
                    nc.vector.scalar_tensor_tensor(out=hf[:, n, :], in0=hf[:, n, :], scalar=misc[:, g:g + 1],
                                                   in1=(rs if n < CQ else rs_kv)[:, :], op0=ALU.mult,
                                                   op1=ALU.mult).then_inc(c_made, 1)
                for n in range(CQ + CKV):
                    dve.wait_ge(c_high, 6 * o + n + 1)
                    dve.wait_ge(c_made, 6 * o + n + 1)
                    nc.vector.tensor_tensor(c_lo[:, n, :], hf[:, n, :], c_hi[:, n, :].bitcast(F32), ALU.subtract)
                end_phase(dve, state)
                W, pb = U + DKV_UNITS, passes_at[l]

                def splits(i, r):
                    split_low(dve, W, i, 4, 2 * r, CQ * QK)
                    split_low(dve, W, i, 4, 2 * r + 1, CKV * 2 * P)

                def fetch(i, r):
                    s, c = r % 2, 4 * (HEADS * o + r)
                    dve.wait_ge(fetched, i * 8 + (c + 2))
                    rotate(q_rope[:, s, :], swapped[:, s, :], roped)
                    dve.wait_ge(projected, i * 4 + (2 * (HEADS * o + r) + 2))
                    nc.vector.tensor_copy(k_nope[:, s, :], bank[:, 7, :]).then_inc(fetched, 1)

                def head(i, r):
                    s, whole = r % 2, not isinstance(i, int)
                    factors(i * 2 + (pb + r), s)
                    if whole or 2 * i + r + 1 < HEADS:
                        maxima(i * 2 + (pb + r + 1), 1 - s)
                    if whole or 2 * i + r + 2 < HEADS:
                        splits(i, r + 2)
                    copy_turned(i * 2 + (pb + r), s, m_turned)
                    head_low(i * 2 + (heads_at[l] + r), i * 2 + r, h_lo, h_hi)
                    if whole or 2 * i + r + 2 < HEADS:
                        fetch(i, r + 2)

                splits(0, 0)
                fetch(0, 0)
                splits(0, 1)
                maxima(pb, 0)
                fetch(0, 1)
                repeat(dve, 3, 2, HEADS, head, chain, 3)
                end_phase(dve, state)
                residual_lows(l, 2, W + 2 * HEADS, 0, KT * P)
            def nsa(l, j, U, dr, idx, state):
                split_low(dve, U, 0, 2, 0, KT * P)
                for n in range(4):
                    if n + 1 < 4:
                        split_low(dve, U, 0, 2, n + 1, KT * P)
                    dve.wait_ge(weights_used, U + n + 1)
                    nc.vector.tensor_copy(hf[:, n, :], bank[:, n % 2, :]).then_inc(drained, 1)
                chain.link(nc.vector.memset(rel_t[:, :], 1.0))
                dve.wait_ge(nsa_small, 1)
                chain.link(nc.vector.tensor_copy(pe_col[:, :, :], bank[:, 4, 0:2 * CB]))
                nc.vector.tensor_copy(rel_t[0:BUCKETS, :], bank[0:BUCKETS, 5, 0:HEADS]).then_inc(nsa_copied, 1)
                dve.wait_ge(drained, dr + 4)
                for n in range(4):
                    w, a = n // 2, n % 2
                    if n >= 2:
                        dve.wait_ge(b_low, n - 1)
                    src = hf[:, 2 * w:2 * w + 2, :].rearrange("p g (m b) -> p b g m", b=CS)[:, :, :, a:a + NC]
                    emb = pe_col[:, w, a * CS:(a + 1) * CS].unsqueeze(2).unsqueeze(3).broadcast_to([P, CS, GROUPS, NC])
                    for g in range(GROUPS):
                        ins = nc.vector.tensor_tensor(b_new[:, a, :, g, :], src[:, :, g, :], emb[:, :, g, :], ALU.add)
                        if g == 0:
                            chain.step(ins)
                        else:
                            ins.then_inc(b_made, 1)
                    dve.wait_ge(b_high, n + 1)
                    dve.wait_ge(b_made, n + 1)
                    chain.wait()
                    nc.vector.tensor_tensor(b_lo[:, w, a * CS:(a + 1) * CS], b_new[:, a],
                                            b_hi[:, w, a * CS:(a + 1) * CS].bitcast(F32), ALU.subtract).then_inc(b_low, 1)
                dve.wait_ge(nsa_small, 2)
                chain.step(nc.vector.tensor_scalar(near_rows[:, :], bank[0:HEADS, 6, 0:3 * P], rel[:, BUCKETS - 1:BUCKETS], None,
                                                   ALU.subtract))
                nc.vector.tensor_copy(far_rows[:, :].rearrange("p (b n) -> p b n", b=2), bank[0:HEADS, 2:4, :]).then_inc(nsa_copied, 1)
                end_phase(dve, state)
                for n in range(16):
                    split_low(dve, U + 4, 0, 2, n, KT * P)
                dve.wait_ge(nsa_small, 3)
                nc.vector.tensor_copy(kc_t[:, :, :], bank[:, 4, 0:GROUPS * NC])
                nc.vector.tensor_copy(vc_t[:, :, :], bank[0:NC, 5, 0:GROUPS * P])
                end_phase(dve, state)
                split_low(dve, U + 20, 0, 2, 0, KT * P)
                for n in range(8):
                    split_low(dve, U + 20, 0, 2, n + 1, KT * (P if n + 1 < 8 else 3 * HEADS))
                    dve.wait_ge(weights_used, U + 20 + n + 1)
                    dst = kf[:, n, :] if n < 4 else vt[:, n - 4, :]
                    nc.vector.tensor_copy(dst, bank[:, n % 2, :]).then_inc(drained, 1)
                dve.wait_ge(nsa_small, 4)
                nc.vector.tensor_copy(near_b[:, :, :].rearrange("p (b h) n -> p b (h n)", b=4), bank[:, 2:6, :]).then_inc(nsa_copied, 1)
                dve.wait_ge(nsa_small, 5)
                for tt in range(TT):
                    last = nc.vector.tensor_copy(cmp_b[:, :, tt, :], bank[:, 2 + tt, 0:HEADS * NC].rearrange("p (h n) -> p h n", h=HEADS))
                end_phase(dve, state)
                W, pb, hb = U + 29, passes_at[l], heads_at[l]

                def low_of_query(h):
                    split_low(dve, W, 0, 2, h, KT * P)

                low_of_query(0)
                dve.wait_ge(q_ready, 1)
                dve.sem_inc(bank7_free, 1)
                maxima(pb, 0, near_b[:, 0, :])
                for h in range(HEADS):
                    dve.wait_ge(cmp_scored, h + 1)
                    nc.vector.tensor_tensor(cmp_p[:, :, :], bank[:, 7, 0:TT * NC].rearrange("p (t n) -> p t n", t=TT),
                                            cmp_b[:, h, :, :], ALU.add).then_inc(bank7_free, 1)
                    dve.wait_ge(bank7_free, 3 * h + 2)
                    chain.link(nc.vector.tensor_reduce(cmp_max[:, :], cmp_p[:, :, :], AX, ALU.max))
                    nc.vector.tensor_scalar(cmp_max[:, :], cmp_max[:, :], MASKED * 1e-10, -1.0, ALU.max, ALU.mult).then_inc(cmp_maxed, 1)
                    maxima(pb + 2 * h + 1, 1, near_b[:, h, :])
                    factors(pb + 2 * h, 0, gates[:, :, HEADS + h])
                    dve.wait_ge(cmp_exped, h + 1)
                    chain.link(nc.vector.tensor_scalar(cmp_sum[:, :], cmp_sum[:, :], 1e-30, None, ALU.max))
                    chain.link(nc.vector.reciprocal(cmp_f[:, :], cmp_sum[:, :]))
                    chain.link(nc.vector.tensor_tensor(cmp_f[:, :], cmp_f[:, :], gates[:, :, h], ALU.mult))
                    nc.vector.tensor_tensor(cmp_p[:, :, :], cmp_p[:, :, :],
                                            cmp_f[:, :].unsqueeze(2).broadcast_to([P, TT, NC]), ALU.mult).then_inc(cmp_scaled, 1)
                    copy_turned(pb + 2 * h, 0, n_turned)
                    factors(pb + 2 * h + 1, 1, gates[:, :, 2 * HEADS + h])
                    if h + 1 < HEADS:
                        low_of_query(h + 1)
                        dve.wait_ge(q_ready, h + 2)
                        dve.sem_inc(bank7_free, 1)
                        maxima(pb + 2 * h + 2, 0, near_b[:, h + 1, :])
                    copy_turned(pb + 2 * h + 1, 1, n_turned)
                    head_low(hb + h, h, o_lo, o_hi)
                end_phase(dve, state)
                residual_lows(l, 2, W + HEADS, 0, KT * P)
            def s5(l, j, U, dr, idx, state):
                T = nc.vector.tensor_tensor
                TS = nc.vector.tensor_scalar

                def complex_product(o_re, o_im, a_re, a_im, b_re, b_im, w1, w2):
                    chain.step(T(w1, a_re, b_re, ALU.mult))
                    chain.link(T(w2, a_im, b_im, ALU.mult))
                    chain.link(T(o_re, w1, w2, ALU.subtract))
                    chain.step(T(w1, a_re, b_im, ALU.mult))
                    chain.link(T(w2, a_im, b_re, ALU.mult))
                    chain.link(T(o_im, w1, w2, ALU.add))

                dve.wait_ge(s5_side, 16 * 9)
                nc.vector.tensor_copy(lam_rows[:, 2, :].rearrange("q (a n) -> q a n", a=2),
                                      dt_rows[:, :].unsqueeze(2).broadcast_to([ST, 2, SN])).then_inc(s5_dve, 1)
                chain.step(nc.vector.memset(out_map[:, :, :, :], 0.0))
                chain.link(nc.vector.memset(b_bar[:, :, :, :], 0.0))
                dve.wait_ge(s5_small, 1)
                chain.link(nc.vector.tensor_copy(small[:, 0:3, :], bank[:, 0, 0:3 * ST].rearrange("p (n q) -> p n q", n=3)))
                lre, lim, dt, grow, ang = (small[:, n, :] for n in range(5))
                e_grow, sin, sin_half, cos, mag1, w1, w2, f_re, f_im, lb1, lb_im, turns, inside, poly = (small[:, n, :] for n in range(5, 19))
                chain.link(TS(turns, dt, 1.0 / math.log(2), ROUND, ALU.mult, ALU.add))
                chain.link(TS(turns, turns, ROUND, None, ALU.subtract))
                TS(w2, turns, math.log(2), 0.35, ALU.mult, ALU.add).then_inc(s5_ready, 1)
                for part in LN_2:
                    chain.link(nc.vector.scalar_tensor_tensor(out=dt, in0=turns, scalar=-part, in1=dt, op0=ALU.mult, op1=ALU.add))
                chain.link(TS(dt, dt, 1.0, -1.0, ALU.min, ALU.max))
                chain.link(TS(poly, dt, 1.0 / math.factorial(SERIES), 1.0 / math.factorial(SERIES - 1), ALU.mult, ALU.add))
                for n in range(SERIES - 2, -1, -1):
                    chain.link(T(poly, poly, dt, ALU.mult))
                    chain.link(TS(poly, poly, 1.0 / math.factorial(n), None, ALU.add))
                dve.wait_ge(s5_exp, 1)
                bits = w2.bitcast(mybir.dt.uint32)
                chain.link(TS(bits, bits, 0x7F800000, None, ALU.bitwise_and))
                chain.link(T(dt, poly, w2, ALU.mult))
                chain.step(T(grow, lre, dt, ALU.mult))
                chain.link(T(ang, lim, dt, ALU.mult))
                chain.link(TS(turns, ang, 1.0 / (2 * math.pi), ROUND, ALU.mult, ALU.add))
                chain.link(TS(turns, turns, ROUND, None, ALU.subtract))
                for part in TWO_PI:
                    chain.link(nc.vector.scalar_tensor_tensor(out=ang, in0=turns, scalar=-part, in1=ang, op0=ALU.mult, op1=ALU.add))
                TS(ang, ang, PI_IN, -PI_IN, ALU.min, ALU.max).then_inc(s5_dve2, 1)
                chain.link(TS(w1, grow, 0.5, -0.5, ALU.min, ALU.max))
                chain.link(TS(poly, w1, 1.0 / math.factorial(SERIES), 1.0 / math.factorial(SERIES - 1), ALU.mult, ALU.add))
                for n in range(SERIES - 2, 0, -1):
                    chain.link(T(poly, poly, w1, ALU.mult))
                    chain.link(TS(poly, poly, 1.0 / math.factorial(n), None, ALU.add))
                chain.link(T(poly, poly, w1, ALU.mult))
                chain.link(T(inside, w1, grow, ALU.is_equal))
                dve.wait_ge(s5_exp, 3)
                chain.link(TS(e_grow, e_grow, 1.0, None, ALU.subtract))
                chain.link(nc.vector.tensor_copy(mag1, e_grow))
                chain.link(nc.vector.copy_predicated(mag1, inside.bitcast(mybir.dt.uint32), poly))
                chain.link(T(w1, sin_half, sin_half, ALU.mult))
                chain.link(TS(w1, w1, -2.0, None, ALU.mult))
                chain.step(TS(cos, w1, 1.0, None, ALU.add))
                chain.link(TS(decay[:, :], mag1, 1.0, None, ALU.add))
                chain.link(T(w2, mag1, cos, ALU.mult))
                chain.step(T(lb1, w2, w1, ALU.add))
                chain.link(T(lb_im, decay[:, :], sin, ALU.mult))
                chain.step(T(w1, lre, lre, ALU.mult))
                chain.link(T(w2, lim, lim, ALU.mult))
                chain.link(T(turns, w1, w2, ALU.add))
                chain.link(nc.vector.reciprocal(turns, turns))
                chain.step(T(w1, lb1, lre, ALU.mult))
                chain.link(T(w2, lb_im, lim, ALU.mult))
                chain.link(T(f_re, w1, w2, ALU.add))
                chain.step(T(f_re, f_re, turns, ALU.mult))
                chain.step(T(w1, lb_im, lre, ALU.mult))
                chain.link(T(w2, lb1, lim, ALU.mult))
                chain.link(T(f_im, w1, w2, ALU.subtract))
                chain.link(T(f_im, f_im, turns, ALU.mult))
                fr, fi = (f.unsqueeze(2).broadcast_to([P, ST, SI]) for f in (f_re, f_im))
                for w, (x0, x1, op) in enumerate((((fr, 0), (fi, 1), ALU.subtract), ((fr, 1), (fi, 0), ALU.add))):
                    chain.step(T(work[:, 0], x0[0], b_in[:, x0[1]], ALU.mult))
                    chain.link(T(work[:, 1], x1[0], b_in[:, x1[1]], ALU.mult))
                    for g in range(2):
                        half = slice(g * SN, (g + 1) * SN)
                        chain.step(T(b_bar[half, w, :, g * SI:(g + 1) * SI], work[half, 0], work[half, 1], op))
                    chain.wait()
                dve.sem_inc(s5_dve, 1)
                p_re, p_im, n_re, n_im = sin_half, e_grow, mag1, poly
                chain.step(nc.vector.tensor_copy(p_re, cos))
                chain.step(nc.vector.tensor_copy(p_im, sin))
                for tab in (fine, coarse):
                    chain.step(nc.vector.memset(tab[:, 0, :, 0:1], 1.0))
                    chain.link(nc.vector.memset(tab[:, 1, :, 0:1], 0.0))
                    n, size = 1, tab.shape[-1]
                    while n < size:
                        b_re, b_im = (v.unsqueeze(2).broadcast_to([P, ST, n]) for v in (p_re, p_im))
                        complex_product(tab[:, 0, :, n:2 * n], tab[:, 1, :, n:2 * n], tab[:, 0, :, 0:n], tab[:, 1, :, 0:n],
                                        b_re, b_im, work[:, 0, :, 0:n], work[:, 1, :, 0:n])
                        complex_product(n_re, n_im, p_re, p_im, p_re, p_im, w1, w2)
                        p_re, p_im, n_re, n_im = n_re, n_im, p_re, p_im
                        n *= 2
                end_phase(dve, state)

                def leave(k):
                    dve.wait_ge(y_made, k + 1)
                    d = NORM_COLS["d"] + KT * j + k
                    nc.vector.scalar_tensor_tensor(out=hf[:, k, :], in0=hf[:, k, :], scalar=misc[:, d:d + 1],
                                                   in1=bank[:, 4 + k % 2, :], op0=ALU.mult, op1=ALU.add).then_inc(y_in, 1)

                for q in range(ST):
                    r = q % 2
                    if q >= 1:
                        dve.wait_ge(products_made, q)
                    dve.wait_ge(table_made, q + 1)
                    dve.wait_ge(bu_made, q + 1)
                    t_re, t_im, b_re, b_im = turn_t[:, r, 0, :], turn_t[:, r, 1, :], bank[:, 2 * r, :], bank[:, 2 * r + 1, :]
                    sw = [scan_w[:, n, :] for n in range(4)]
                    chain.step(T(sw[0], b_re, t_re, ALU.mult))
                    chain.step(T(sw[1], b_im, t_im, ALU.mult))
                    chain.step(T(sw[2], b_im, t_re, ALU.mult))
                    T(sw[3], b_re, t_im, ALU.mult).then_inc(bu_free, 1)
                    dve.wait_ge(bu_free, q + 1)
                    chain.wait()
                    chain.step(T(sw[0], sw[0], sw[1], ALU.add))
                    chain.link(T(sw[2], sw[2], sw[3], ALU.subtract))
                    mag = decay[:, q:q + 1].broadcast_to([P, S])
                    chain.step(nc.vector.tensor_tensor_scan(sw[1], mag, sw[0], 0.0, ALU.mult, ALU.add))
                    chain.link(nc.vector.tensor_tensor_scan(sw[3], mag, sw[2], 0.0, ALU.mult, ALU.add))
                    st = [state_w[:, r, n, :] for n in range(4)]
                    for need in ([q - 2] if q >= 2 else []):
                        if need % 4 == 3:
                            dve.wait_ge(y_made, need // 4 + 1)
                        else:
                            dve.wait_ge(products_used, 3 * (need // 4) + need % 4 + 1)
                    T(st[0], sw[1], t_re, ALU.mult)
                    T(st[1], sw[3], t_im, ALU.mult)
                    T(st[2], sw[3], t_re, ALU.mult)
                    T(st[3], sw[1], t_im, ALU.mult).then_inc(products_made, 1)
                    if q >= 5 and q % 4 == 1:
                        leave(q // 4 - 1)
                leave(KT - 1)
                for k in range(KT):
                    dve.wait_ge(y_high, k + 1)
                    T(h_lo[:, k, :], hf[:, k, :], h_hi[:, k, :].bitcast(F32), ALU.subtract)
                end_phase(dve, state)
                for e in range(2):
                    split_low(dve, U, 0, 4, e, KT * P)

                def glu_pair(i, r):
                    if not (isinstance(i, int) and 2 * i + r + 1 >= KT):
                        for e in range(2):
                            split_low(dve, U, i, 4, 2 * (r + 1) + e, KT * P)
                    m = i * 2 + r
                    dve.wait_ge(sig_made, i * 2 + (r + 1))
                    nc.vector.scalar_tensor_tensor(out=gated[:, r, :], in0=bank[:, 2 * r, :], scalar=mod[:, bass.ds(i * 2 + (mod_col(l, 2, 0) + r), 1)],
                                                   in1=sig[:, r, :], op0=ALU.mult, op1=ALU.mult).then_inc(drained, 1)
                    dve.wait_ge(drained, i * 4 + (dr + 2 * r + 1))
                    at = x[:, m, :] if isinstance(m, int) else x[:, bass.ds(m, 1), :].squeeze(1)
                    nc.vector.tensor_tensor(at, at, gated[:, r, :], ALU.add).then_inc(drained, 1)

                repeat(dve, 3, 2, KT, glu_pair)
            for name, l, j, U, dr, idx in plan:
                if name == "norm":
                    norm(l, j, idx)
                    continue
                elif name == "mla":
                    mla(l, j, U, dr, idx, state)
                elif name == "nsa":
                    nsa(l, j, U, dr, idx, state)
                elif name == "s5":
                    s5(l, j, U, dr, idx, state)
                elif name == "ffn":
                    ffn(l, U, dr, idx)
                else:
                    norm(0, 2, idx)
                    for k in range(KT):
                        dve.wait_ge(turned_in, N_TURN + KT + k + 1)
                        nc.vector.tensor_copy(out_rows[:, :, k * P:(k + 1) * P],
                                              bank[:, 4 + k % 2, :].rearrange("p (t f) -> p t f", t=TT)).then_inc(copied_in, 1)
                end_phase(dve, state)

        @block.gpsimd
        def _(pool):
            state, chain = [0], Chain(pool, pool_chain)
            pool.sem_inc(g_made, 2)
            end_phase(pool, state)
            pool.sem_inc(pt_act, 2)
            pool.sem_inc(pt_dve, 2)
            pool.sem_inc(o_low, 1)

            def scale(p, r, probs):
                pool.wait_ge(factored, p + 1)
                for q in range(TT):
                    at = probs[:, r, ROW_AT[q]:ROW_AT[q] + P * (q + 1)]
                    last = nc.gpsimd.tensor_tensor(at, at, factor[:, r, q:q + 1].broadcast_to([P, P * (q + 1)]), ALU.mult)
                last.then_inc(scaled, 1)

            def mla(l, j, U, dr, idx, state):
                pool.dma_start(rope[:], t["rope"]).then_inc(mla_side, 16)
                end_phase(pool, state)
                repeat(pool, 4, 2, HEADS, lambda i, r: scale(i * 2 + (passes_at[l] + r), r, m_probs))
                end_phase(pool, state)
            def nsa(l, j, U, dr, idx, state):
                for dst, src in ((pe_rows[:, 0, :], t["nsa_pe_k"][j]), (pe_rows[:, 1, :], t["nsa_pe_v"][j]),
                                 (w2[:, 0], t["nsa_w2_k"][j].rearrange("(k p) m -> p k m", p=P)),
                                 (w2[:, 1], t["nsa_w2_v"][j].rearrange("(k p) m -> p k m", p=P)),
                                 (near_hot[:], t["near"]), (far_hot[:], t["far"]), (flip[:], t["flip"]), (rel[:], t["rel_bias"])):
                    pool.dma_start(dst, src).then_inc(nsa_side, 16)
                end_phase(pool, state)
                near_d, far_d = scratch[:, 0:3 * P], scratch[:, 1024:1024 + 2 * S]
                pool.dma_start(near_d, near_rows[:]).then_inc(rows_out, 16)
                pool.dma_start(far_d, far_rows[:]).then_inc(rows_out, 16)
                end_phase(pool, state)
                pool.wait_ge(rows_out, 32)
                row = scratch.shape[1]
                pool.dma_start(near_back, bass.AP(tensor=scratch.tensor, offset=0, ap=[[1, P], [row, HEADS], [1, FAR]])).then_inc(rows_back, 16)
                pool.wait_ge(nsa_small, 4)
                pool.dma_start(cmp_back, bass.AP(tensor=scratch.tensor, offset=1024, ap=[[CS, NC], [row, HEADS], [1, S]])).then_inc(rows_back, 16)
                end_phase(pool, state)
                for h in range(HEADS):
                    scale(passes_at[l] + 2 * h, 0, n_probs)
                    scale(passes_at[l] + 2 * h + 1, 1, n_probs)
                end_phase(pool, state)
            def s5(l, j, U, dr, idx, state):
                for w, key in enumerate(("s5_lam_re", "s5_lam_im")):
                    pool.dma_start(lam_rows[:, w, :], t[key][j].rearrange("(q a) n -> q (a n)", a=2)).then_inc(s5_side, 16)
                pool.dma_start(dt_rows[:], t["s5_log_dt"][j].rearrange("(q a) -> q a", a=2)).then_inc(s5_side, 16)
                for w, key in enumerate(("s5_b_re", "s5_b_im")):
                    pool.dma_start(b_in[:, w], t[key][j].rearrange("(q a) n i -> (a n) q i", a=2)).then_inc(s5_side, 16)
                for w, key in enumerate(("s5_c_re", "s5_c_im")):
                    for twice in range(2):
                        src = t[key][j].rearrange("(k g) i n -> (g i) k n", g=P // SI)
                        pool.dma_start(c_rows[:, w, :, twice, :], src).then_inc(s5_side, 16)
                end_phase(pool, state)

                def sums(q):
                    r = q % 2
                    pool.wait_ge(products_made, q + 1)
                    st = [state_w[:, r, n, :] for n in range(4)]
                    nc.gpsimd.tensor_tensor(st[0], st[0], st[1], ALU.subtract)
                    nc.gpsimd.tensor_tensor(st[2], st[2], st[3], ALU.add).then_inc(x_made, 1)

                for q in range(ST):
                    r = q % 2
                    if q >= 2:
                        pool.wait_ge(products_made, q - 1)
                    if q >= 1:
                        pool.wait_ge(table_made, q)
                    shape = [P, COARSE, FINE]
                    c_re, c_im = (coarse[:, w, q, :].unsqueeze(2).broadcast_to(shape) for w in range(2))
                    f_re, f_im = (fine[:, w, q, :].unsqueeze(1).broadcast_to(shape) for w in range(2))
                    to, w1, w2 = (v.rearrange("p (c f) -> p c f", c=COARSE) for v in (turn_t[:, r, 0, :], turn_w[:, 0, :], turn_w[:, 1, :]))
                    ti = turn_t[:, r, 1, :].rearrange("p (c f) -> p c f", c=COARSE)
                    chain.step(nc.gpsimd.tensor_tensor(w1, c_re, f_re, ALU.mult))
                    chain.link(nc.gpsimd.tensor_tensor(w2, c_im, f_im, ALU.mult))
                    chain.link(nc.gpsimd.tensor_tensor(to, w1, w2, ALU.subtract))
                    chain.step(nc.gpsimd.tensor_tensor(w1, c_re, f_im, ALU.mult))
                    chain.link(nc.gpsimd.tensor_tensor(w2, c_im, f_re, ALU.mult))
                    nc.gpsimd.tensor_tensor(ti, w1, w2, ALU.add).then_inc(table_made, 1)
                    if q >= 1:
                        sums(q - 1)
                sums(ST - 1)
                end_phase(pool, state)
            for name, l, j, U, dr, idx in plan:
                if name in ("norm", "final"):
                    pool.wait_ge(rs_made, idx + 1)
                    pool.wait_ge(ada_turned, 2 * (l_at[l] + 1) if name == "norm" else 2 * len(LAYERS))
                    for k in range(KT):
                        nc.gpsimd.tensor_tensor(hf[:, k, :], x[:, k, :], rs[:, :], ALU.mult).then_inc(x_scaled, 1)
                    if name == "norm":
                        continue
                elif name == "mla":
                    mla(l, j, U, dr, idx, state)
                elif name == "nsa":
                    nsa(l, j, U, dr, idx, state)
                elif name == "s5":
                    s5(l, j, U, dr, idx, state)
                end_phase(pool, state)


_INS = ["x", "c", "ada_w", "ada_b", "norm1_g", "norm2_g", "final_g", "rel_bias",
        "mla_w_dkv", "mla_g_q", "mla_g_kv", "mla_w_uq", "mla_w_ukv", "mla_w_o",
        "nsa_w_in", "nsa_pe_k", "nsa_w1_k", "nsa_w2_k", "nsa_pe_v", "nsa_w1_v", "nsa_w2_v", "nsa_w_o",
        "s5_lam_re", "s5_lam_im", "s5_log_dt", "s5_b_re", "s5_b_im", "s5_c_re", "s5_c_im", "s5_d", "s5_w_glu",
        "ffn_w_up", "ffn_conv_w", "ffn_conv_b", "ffn_w_down"]


def shape_tables():
    import numpy as np
    eye = np.eye(P, dtype=np.float32)
    later = np.triu(np.ones((P, P), np.float32), 1) * np.float32(MASKED)
    half = ROPE // 2
    inv = (np.float32(10000.0) ** (-np.arange(half, dtype=np.float32) / np.float32(half))).astype(np.float32)
    ang = (inv[:, None] * np.arange(S, dtype=np.float32)[None, :]).astype(np.float32)
    cos, sin = np.cos(ang.astype(np.float64)), np.sin(ang.astype(np.float64))
    rope = np.stack([np.concatenate([cos, cos]), np.concatenate([-sin, sin])], 1).astype(np.float32)

    def bucket(dist):
        n = np.maximum(dist, 0)
        nf = np.maximum(n, 1).astype(np.float32)
        large = 16 + (np.log(nf / np.float32(16)) / np.float32(math.log(8)) * np.float32(16)).astype(np.int32)
        return np.where(n < 16, n, np.minimum(large, BUCKETS - 1))

    def hot(dist):
        at = np.zeros((BUCKETS + 1, len(dist)), np.float32)
        at[bucket(dist), np.arange(len(dist))] = 1.0
        at[BUCKETS] = np.where(dist < 0, np.float32(MASKED), np.float32(0))
        return at

    near = hot(255 - np.arange(384))
    far = hot(np.arange(1024) - 511 )
    return {"ident": eye, "flip": eye[::-1].copy(), "mask": later,
            "rope": rope, "near": near, "far": far}


def kernel(**inputs):
    import numpy as np
    import concourse.bacc as bacc
    from concourse.bass_utils import run_bass_kernel_spmd

    nc = bacc.Bacc("TRN2", target_bir_lowering=False, num_devices=1)
    arrays, aps = {}, {}
    given = {n: np.ascontiguousarray(inputs[n]) for n in _INS}
    given.update(shape_tables())
    for name, a in given.items():
        arrays[f"in_{name}"] = a
        aps[name] = nc.dram_tensor(f"in_{name}", a.shape, mybir.dt.from_np(a.dtype), kind="ExternalInput").ap()
    out = nc.dram_tensor("out", (1, S, D), F32, kind="ExternalOutput").ap()
    scratch = nc.dram_tensor("bias_rows", (HEADS, 2048), F32, kind="Internal").ap()
    trunk(nc, aps, out, scratch)
    got = run_bass_kernel_spmd(nc, [arrays], core_ids=[0]).results[0]
    return got["out"]
```

```python
import math
from contextlib import ExitStack, contextmanager

import concourse.bass as bass
from concourse import mybir

ALU = mybir.AluOpType
ACT = mybir.ActivationFunctionType
AX = mybir.AxisListType.X
F32 = mybir.dt.float32
F32R = mybir.dt.float32r
BF16 = mybir.dt.bfloat16

P = 128
D = 1024
S = 512
LAYERS = (0, 1, 2, 3)
DEPTH = 4
KT = D // P
TT = S // P
EPS = 1e-6
N_MOD = 6
MODS = N_MOD * KT

Q_LORA, KV_LORA, ROPE, NOPE = 512, 256, 64, 128
HEADS = 8
QK = NOPE + ROPE
CQ, CKV = Q_LORA // P, KV_LORA // P
MLA_SCALE = float(QK) ** -0.5
DKV_UNITS = 7

GROUPS, HPG, DK = 2, 4, 128
NSA_SCALE = float(DK) ** -0.5
CB, CS = 32, 16
NC = S // CS - 1
CH = 256
BUCKETS = 32
FAR = 2 * P
NSA_COL = {"q": 0, "kc": 1024, "vc": 1280, "ks": 1536, "vs": 1792, "kw": 2048, "vw": 2304, "gate": 2560}
MASKED = -1e30

SG, SN, SI = 64, 64, 16
ST = SG * SN // P
FINE, COARSE = 32, S // 32

FF = 2816
PAIRS = FF // P
HALF = PAIRS // 2
TAPS = 3
CHT = 2 * PAIRS

SERIES = 8
ROUND = 1.5 * 2.0 ** 23
TWO_PI = (6.28125, 0.0019350051879882812, 2 * math.pi - 6.28125 - 0.0019350051879882812)
PI_IN = 3.1415925
ADA_W = N_MOD * D // 2
LN_2 = (0.693359375, math.log(2) - 0.693359375)

UNIT = HALF * P
TRI = P * TT * (TT + 1) // 2
ROW_AT = [P * i * (i + 1) // 2 for i in range(TT)]
COL_AT = [P * sum(TT - c for c in range(j)) for j in range(TT)]

NORM_COLS = {"norm1": 0, "norm2": 32, "final": 64, "gq": 72, "gkv": 80, "d": 84}
MISC_ROWS = 92
CW_ROWS, CB_ROWS, AB_ROWS = 88, 88, 96


def reached(eng, sem, value):
    if not (isinstance(value, int) and value <= 0):
        eng.wait_ge(sem, value)


def repeat(eng, trips, per, total, step, chain=None, links=0, first=0):
    for r in range(first):
        step(0, r)
    if trips:
        with ExitStack() as ctx:
            i = ctx.enter_context(eng.Fori(0, trips))
            if chain is not None:
                ctx.enter_context(chain.loop(i, trips, per * links))
            for r in range(first, first + per):
                step(i, r)
    for n in range(first + trips * per, total):
        step(trips, n - trips * per)


class Chain:

    def __init__(self, eng, sem):
        self.eng, self.sem, self.n, self.i, self.per = eng, sem, 0, None, 0

    def step(self, ins):
        ins.then_inc(self.sem, 1)
        self.n += 1

    def wait(self):
        self.eng.wait_ge(self.sem, self.n if self.i is None else self.i * self.per + self.n)

    def link(self, ins):
        self.step(ins)
        self.wait()

    @contextmanager
    def loop(self, i, trips, per):
        first, self.i, self.per = self.n, i, per
        yield
        assert self.n == first + per, (self.n, first, per)
        self.n, self.i = first + per * trips, None


def units_of(layer):
    kind = layer % 3
    mixer = (DKV_UNITS + 2 * HEADS + KT) if kind == 0 else (8 + 16 + 4 + 1 + HEADS + KT) if kind == 1 else 2 * KT
    return mixer


def trunk(nc, t, out, scratch):
    with ExitStack() as ctx:
        def sb(name, shape, dt=F32, stack=ctx):
            return stack.enter_context(nc.sbuf_tensor(name, shape, dt))

        def sem(name):
            return ctx.enter_context(nc.semaphore(name))

        bank = ctx.enter_context(nc.psum_tensor("bank", [P, 8, 512], F32))

        x = sb("x", [P, KT, S])
        hf = sb("hf", [P, KT, S])
        h_hi = sb("h_hi", [P, KT, S], F32R)
        h_lo = sb("h_lo", [P, KT, S], F32R)
        stage = sb("stage", [P, 2, UNIT])
        w_hi = sb("w_hi", [P, 2, UNIT], F32R)
        w_lo = sb("w_lo", [P, 2, UNIT], F32R)
        rs = sb("rs", [P, S])
        sq_x = sb("sq_x", [P, 2, S])
        c_act = sb("c_act", [P, KT])
        ident = sb("ident", [P, P])
        ones = sb("ones", [P, P])
        eps = sb("eps", [P, 1])
        ident_b = sb("ident_b", [P, P], BF16)
        mask_b = sb("mask_b", [P, P], BF16)
        mask = sb("mask", [P, P])
        mod = sb("mod", [P, DEPTH * MODS])
        misc = sb("misc", [P, MISC_ROWS])
        cw = sb("cw", [P, DEPTH * TAPS * CHT])
        cb = sb("cb", [P, DEPTH * CHT])
        amp = sb("amp", [P, DEPTH * 2 * KT])

        landed = [sem("landed0"), sem("landed1")]
        hi_made, lo_made, weights_used, drained = sem("hi_made"), sem("lo_made"), sem("weights_used"), sem("drained")
        phase_end = sem("phase_end")
        act_chain, dve_chain, pool_chain = sem("act_chain"), sem("dve_chain"), sem("pool_chain")
        params_in, consts_in, turned_in, copied_in = sem("params_in"), sem("consts_in"), sem("turned_in"), sem("copied_in")
        rooted = sem("rooted")
        squares, h_made, h_high = sem("squares"), sem("h_made"), sem("h_high")
        cv_made, silu_made, g_made, g_high, g_low = sem("cv_made"), sem("silu_made"), sem("g_made"), sem("g_high"), sem("g_low")
        stored = sem("stored")
        ada_first_in = [sem(f"ada_first_in{n}") for n in range(4)]
        ada_in = [sem(f"ada_in{n}") for n in range(2)]
        ada_used, ada_done, ada_turned, sq_used, rs_made, x_scaled, h_low, c_in = (
            sem(n) for n in ("ada_used", "ada_done", "ada_turned", "sq_used", "rs_made", "x_scaled", "h_low", "c_in"))

        with ExitStack() as own:
            rows = sb("rows", [P, 20, P], stack=own)
            x_rows = sb("x_rows", [P, TT, D], stack=own)
            ada_first = sb("ada_first", [P, 4, ADA_W], stack=own)
        with ExitStack() as own:
            g_hi = sb("g_hi", [P, HALF, S], F32R, stack=own)
            g_lo = sb("g_lo", [P, HALF, S], F32R, stack=own)
            cv = sb("cv", [P, 2, 2, S], stack=own)
            sg = sb("sg", [P, 2, S], stack=own)
            gf = sb("gf", [P, 2, S], stack=own)
            ada_w = sb("ada_w", [P, 2, ADA_W], stack=own)
        with ExitStack() as own:
            out_rows = sb("out_rows", [P, TT, D], stack=own)
        with ExitStack() as own:
            sq = sb("sq", [P, CQ + CKV, S], stack=own)
            c_hi = sb("c_hi", [P, CQ + CKV, S], F32R, stack=own)
            c_lo = sb("c_lo", [P, CQ + CKV, S], F32R, stack=own)
            rope = sb("rope", [ROPE, 2, S], stack=own)
            k_rope = sb("k_rope", [ROPE, S], stack=own)
            swapped = sb("swapped", [ROPE, 2, S], stack=own)
            rs_kv = sb("rs_kv", [P, S], stack=own)
            with ExitStack() as part:
                q_nope = sb("q_nope", [P, 2, S], stack=part)
                q_rope = sb("q_rope", [ROPE, 2, S], stack=part)
                k_nope = sb("k_nope", [P, 2, S], stack=part)
                v_tok = sb("v_tok", [P, 2, S], stack=part)
                m_probs = sb("m_probs", [P, 2, TRI], stack=part)
                m_turned = sb("m_turned", [P, 2, TRI], stack=part)
        neg_max = sb("neg_max", [P, 2, TT])
        row_sum = sb("row_sum", [P, 2, TT])
        factor = sb("factor", [P, 2, TT])
        lat_summed, lat_rooted, c_made, c_high = sem("lat_summed"), sem("lat_rooted"), sem("c_made"), sem("c_high")
        mla_side = sem("mla_side")
        projected, fetched, roped = sem("projected"), sem("fetched"), sem("roped")
        scored, maxed, exped, factored, scaled = sem("scored"), sem("maxed"), sem("exped"), sem("factored"), sem("scaled")
        turned, pt_act, pt_dve = sem("turned"), sem("pt_act"), sem("pt_dve")
        valued, o_high, o_low = sem("valued"), sem("o_high"), sem("o_low")

        def score_tile(r, i):
            b, at = {3: (0, 0), 2: (1, 0), 1: (2, P), 0: (2, 0)}[i]
            return bank[:, 3 * r + b, at:at + P * (i + 1)]

        def turned_tile(r, j, i):
            b, at = min(j, 2), (i - j) * P + (2 * P if j == 3 else 0)
            return bank[:, 3 * r + b, at:at + P]
        with ExitStack() as own:
            kf = sb("kf", [P, 2 * GROUPS, S], stack=own)
            vt = sb("vt", [P, 2 * GROUPS, S], stack=own)
            kc_t = sb("kc_t", [P, GROUPS, NC], stack=own)
            vc_t = sb("vc_t", [NC, GROUPS, P], stack=own)
            gates = sb("gates", [P, TT, 3 * HEADS], stack=own)
            near_b = sb("near_b", [P, HEADS, FAR], stack=own)
            cmp_b = sb("cmp_b", [P, HEADS, TT, NC], stack=own)
            hid = sb("hid", [P, 2, 2, GROUPS * NC], stack=own)
            w2 = sb("w2", [P, 2, 2, P], stack=own)
            pe_rows = sb("pe_rows", [CB, 2, P], stack=own)
            pe_col = sb("pe_col", [P, 2, CB], stack=own)
            with ExitStack() as part:
                b_hi = sb("b_hi", [P, 2, CB, GROUPS, NC], F32R, stack=part)
                b_lo = sb("b_lo", [P, 2, CB, GROUPS, NC], F32R, stack=part)
                b_new = sb("b_new", [P, 2, CS, GROUPS, NC], stack=part)
                near_hot = sb("near_hot", [BUCKETS + 1, 3 * P], stack=part)
                far_hot = sb("far_hot", [BUCKETS + 1, 2 * S], stack=part)
                flip = sb("flip", [P, P], stack=part)
                rel = sb("rel", [HEADS, BUCKETS], stack=part)
                rel_t = sb("rel_t", [BUCKETS + 1, HEADS], stack=part)
                near_rows = sb("near_rows", [HEADS, 3 * P], stack=part)
                far_rows = sb("far_rows", [HEADS, 2 * S], stack=part)
                hid_rows = sb("hid_rows", [GROUPS * NC, 2, 2 * P], stack=part)
                gate_rows = sb("gate_rows", [3 * HEADS, S], stack=part)
            with ExitStack() as part:
                q_t = sb("q_t", [P, 2, S], stack=part)
                n_probs = sb("n_probs", [P, 2, TRI], stack=part)
                n_turned = sb("n_turned", [P, 2, TRI], stack=part)
                cmp_p = sb("cmp_p", [P, TT, NC], stack=part)
                cmp_t = sb("cmp_t", [NC, S], stack=part)
                o_hi = sb("o_hi", [P, KT, S], F32R, stack=part)
                o_lo = sb("o_lo", [P, KT, S], F32R, stack=part)
                cmp_max = sb("cmp_max", [P, TT], stack=part)
                cmp_sum = sb("cmp_sum", [P, TT], stack=part)
                cmp_f = sb("cmp_f", [P, TT], stack=part)
        near_back = hf[:, 4:8, :].rearrange("p k s -> p (k s)").rearrange("p (h n) -> p h n", h=HEADS)
        cmp_back = hf[0:NC * HEADS // 2, 0:2, :]
        nsa_side, nsa_small, nsa_copied, b_made, b_high = (sem(n) for n in ("nsa_side", "nsa_small", "nsa_copied", "b_made", "b_high"))

        def value_bank(branch, tt):
            return (2 + 4 * branch + tt) % 8

        rows_out, rows_back, b_low = sem("rows_out"), sem("rows_back"), sem("b_low")
        cmp_scored, cmp_maxed, cmp_exped, cmp_scaled, cmp_turned = (sem(n) for n in ("cmp_scored", "cmp_maxed", "cmp_exped", "cmp_scaled", "cmp_turned"))
        cmp_copied, q_ready = sem("cmp_copied"), sem("q_ready")
        with ExitStack() as own:
            in_map = sb("in_map", [P, 2, KT, P], stack=own)
            out_map = sb("out_map", [P, 2, KT, 5 * P], stack=own)
            fine = sb("fine", [P, 2, ST, FINE], stack=own)
            coarse = sb("coarse", [P, 2, ST, COARSE], stack=own)
            decay = sb("decay", [P, ST], stack=own)
            with ExitStack() as part:
                small = sb("small", [P, 26, ST], stack=part)
                work_c = sb("work_c", [P, 2, ST, COARSE // 2], stack=part)
                lam_rows = sb("lam_rows", [ST, 3, P], stack=part)
                dt_rows = sb("dt_rows", [ST, 2], stack=part)
                b_in = sb("b_in", [P, 2, ST, SI], stack=part)
                b_bar = sb("b_bar", [P, 2, ST, 2 * SI], stack=part)
                c_rows = sb("c_rows", [P, 2, KT, 2, SN], stack=part)
                work = sb("work", [P, 2, ST, SI], stack=part)
            with ExitStack() as part:
                turn_t = sb("turn_t", [P, 2, 2, S], stack=part)
                turn_w = sb("turn_w", [P, 2, S], stack=part)
                scan_w = sb("scan_w", [P, 4, S], stack=part)
                state_w = sb("state_w", [P, 2, 4, S], stack=part)
            with ExitStack() as part:
                sig = sb("sig", [P, 2, S], stack=part)
                gated = sb("gated", [P, 2, S], stack=part)
        s5_side, s5_small, s5_act, s5_dve = (sem(n) for n in ("s5_side", "s5_small", "s5_act", "s5_dve"))
        table_made, bu_made, bu_free, products_made, y_made = (
            sem(n) for n in ("table_made", "bu_made", "bu_free", "products_made", "y_made"))
        products_used, s5_exp, s5_dve2, s5_ready, s5_zeroed, s5_trig = (sem(n) for n in ("products_used", "s5_exp", "s5_dve2", "s5_ready", "s5_zeroed", "s5_trig"))
        y_in, y_gelu, y_high, y_low, sig_made = (sem(n) for n in ("y_in", "y_gelu", "y_high", "y_low", "sig_made"))
        block = ctx.enter_context(nc.Block())

        plan, units, drains, norms = [], 0, 0, 0
        for l in LAYERS:
            kind = l % 3
            plan.append(("norm", l, 0, units, drains, norms))
            plan.append((("mla", "nsa", "s5")[kind], l, l // 3, units, drains, norms))
            units += units_of(l)
            drains += (DKV_UNITS + KT, 8 + 4 + 4 + 1 + KT, 2 * KT)[kind]
            plan.append(("norm", l, 1, units, drains, norms + 1))
            plan.append(("ffn", l, 0, units, drains, norms + 1))
            units += 2 * (2 * HALF + KT)
            drains += 2 * (2 * HALF + KT)
            norms += 2
        plan.append(("final", 0, 0, units, drains, norms))
        l_at = {l: n for n, l in enumerate(LAYERS)}
        mla_at, passes_at, heads_at, phases_at, a, b, c, d = {}, {}, {}, {}, 0, 0, 0, 1
        for l in LAYERS:
            phases_at[l] = d
            d += (3, 5, 3)[l % 3] + 1
            mla_at[l], passes_at[l], heads_at[l] = a, b, c
            a, b, c = a + (l % 3 == 0), b + (HEADS, 2 * HEADS, 0)[l % 3], c + (HEADS, HEADS, 0)[l % 3]

        def mod_col(l, part, m):
            return l * MODS + part * KT + m

        def end_phase(eng, state):
            state[0] += 1
            eng.drain().then_inc(phase_end, 1)
            eng.wait_ge(phase_end, 4 * state[0])

        following = dict(zip(LAYERS, LAYERS[1:]))
        l_at = {l: n for n, l in enumerate(LAYERS)}
        ada_sum = hf[:, 0:ADA_W // S, :].rearrange("p k s -> p (k s)")

        def load_unit(sp, U, i, per, r, src, width):
            reached(sp, lo_made, i * per + (U + r - 1))
            dst = stage[:, (U + r) % 2, 0:width].rearrange("p (k m) -> p k m", m=src.shape[-1])
            sp.dma_start(dst, src).then_inc(landed[(U + r) % 2], 16)

        def split_high(act, U, i, per, r, width):
            s = (U + r) % 2
            act.wait_ge(landed[s], (i * (per // 2) + ((U + r) // 2 + 1)) * 16)
            reached(act, weights_used, i * per + (U + r - 1))
            nc.scalar.copy(w_hi[:, s, 0:width], stage[:, s, 0:width]).then_inc(hi_made, 1)

        def split_low(dve, U, i, per, r, width):
            s = (U + r) % 2
            dve.wait_ge(hi_made, i * per + (U + r + 1))
            nc.vector.tensor_tensor(w_lo[:, s, 0:width], stage[:, s, 0:width], w_hi[:, s, 0:width].bitcast(F32),
                                    ALU.subtract).then_inc(lo_made, 1)

        def three(dst, a_hi, a_lo, b_hi, b_lo, first, last):
            nc.tensor.matmul(dst, a_hi, b_hi, start=first, stop=False)
            nc.tensor.matmul(dst, a_hi, b_lo, start=False, stop=False)
            return nc.tensor.matmul(dst, a_lo, b_hi, start=False, stop=last)

        def feature_product(dst, s, k_tiles, stride, at, r_hi, r_lo, ready=None):
            for k in range(k_tiles):
                if ready is not None:
                    ready(k)
                a_hi = w_hi[:, s, k * stride + at:k * stride + at + P]
                a_lo = w_lo[:, s, k * stride + at:k * stride + at + P]
                last = three(dst, a_hi, a_lo, r_hi[:, k, :], r_lo[:, k, :], k == 0, k == k_tiles - 1)
            return last

        def token_product(dst, s, k_tiles, stride, at, m, a_hi, a_lo):
            for tt in range(TT):
                for k in range(k_tiles):
                    last = three(dst[:, tt * m:(tt + 1) * m], a_hi[:, k, tt * P:(tt + 1) * P], a_lo[:, k, tt * P:(tt + 1) * P],
                                 w_hi[:, s, k * stride + at:k * stride + at + m],
                                 w_lo[:, s, k * stride + at:k * stride + at + m], k == 0, k == k_tiles - 1)
            return last

        def w_view(w):
            return w.rearrange("(k p) m -> p k m", p=P)

        ab = t["ada_b"].rearrange("l (r f) -> (l r) f", f=P)
        cwr = t["ffn_conv_w"].rearrange("l w (c f) -> (l w c) f", f=P)
        cbr = t["ffn_conv_b"].rearrange("l (c f) -> (l c) f", f=P)
        row_loads = [(0, 0, ab[0:96]), (1, 0, ab[96:192])]
        row_loads += [(3 + g, 0, cwr[CW_ROWS * g:CW_ROWS * (g + 1)]) for g in range(6)]
        row_loads += [(9 + g, 0, cbr[CB_ROWS * g:CB_ROWS * (g + 1)]) for g in range(2)]
        for key, name in (("norm1", "norm1_g"), ("norm2", "norm2_g"), ("gq", "mla_g_q"), ("gkv", "mla_g_kv")):
            row_loads.append((2, NORM_COLS[key], t[name].rearrange("l (r f) -> (l r) f", f=P)))
        row_loads.append((2, NORM_COLS["final"], t["final_g"].rearrange("(r f) -> r f", f=P)))
        row_loads.append((2, NORM_COLS["d"], t["s5_d"].rearrange("n (r g) i -> (n r) (g i)", g=P // SI)))
        turns = [(0, AB_ROWS, mod, 0), (1, AB_ROWS, mod, AB_ROWS), (2, MISC_ROWS, misc, 0)]
        turns += [(3 + g, CW_ROWS, cw, CW_ROWS * g) for g in range(6)]
        turns += [(9 + g, CB_ROWS, cb, CB_ROWS * g) for g in range(2)]
        N_TURN = len(turns)
        x_view = t["x"].rearrange("b (t p) f -> p (b t) f", p=P)

        def ada_slot(g):
            if g < KT:
                return ada_first[:, g % 4, :], ada_first_in[g % 4], g // 4 + 1
            return ada_w[:, g % 2, :], ada_in[g % 2], (g - KT) // 2 + 1

        def load_ada(eng, l, n):
            g = 2 * KT * l_at[l] + n
            dst, arrived, _ = ada_slot(g)
            reached(eng, ada_used, g - 3 if g < KT else g - 1)
            src = t["ada_w"][l].rearrange("(p k) f -> p k f", k=KT)[:, n % KT, (n // KT) * ADA_W:(n // KT + 1) * ADA_W]
            eng.dma_start(dst, src).then_inc(arrived, 16)

        @block.sync
        def _(sp):
            for slot, at, src in row_loads:
                sp.dma_start(rows[at:at + src.shape[0], slot, :], src).then_inc(params_in, 16)
            sp.dma_start(x_rows[:], x_view).then_inc(params_in, 16)
            sp.dma_start(c_act[:], t["c"].rearrange("b (p k) -> (b p) k", k=KT)).then_inc(c_in, 16)
            for dst, name in ((ident, "ident"), (mask, "mask")):
                sp.dma_start(dst[:], t[name]).then_inc(consts_in, 16)
            for n in range(KT):
                load_ada(sp, LAYERS[0], n)
            for name, l, j, U, _, _ in plan:
                if name == "ffn":
                    up, down = w_view(t["ffn_w_up"][l]), t["ffn_w_down"][l].rearrange("(k p) m -> p k m", p=P)
                    for half in range(2):
                        V = U + half * (2 * HALF + KT)

                        def up_pair(i, r):
                            for e in range(2):
                                load_unit(sp, V, i, 4, 2 * r + e,
                                          up[:, :, bass.ds((i * 2 + r) * P + (e * FF + half * HALF * P), P)], KT * P)

                        repeat(sp, 5, 2, HALF, up_pair)
                        for n in range(KT):
                            load_unit(sp, V + 2 * HALF, 0, 2, n, down[:, half * HALF:(half + 1) * HALF, n * P:(n + 1) * P], UNIT)
                if name == "mla":
                    dkv, uq, ukv, wo = (w_view(t[n][j]) for n in ("mla_w_dkv", "mla_w_uq", "mla_w_ukv", "mla_w_o"))
                    for n in range(DKV_UNITS):
                        c = min(n * P, Q_LORA + KV_LORA + ROPE - P)
                        load_unit(sp, U, 0, 2, n, dkv[:, :, c:c + P], KT * P)
                    W = U + DKV_UNITS

                    def head_units(i, r):
                        load_unit(sp, W, i, 4, 2 * r, uq[:, :, bass.ds((i * 2 + r) * QK, QK)], CQ * QK)
                        load_unit(sp, W, i, 4, 2 * r + 1, ukv[:, :, bass.ds((i * 2 + r) * 2 * P, 2 * P)], CKV * 2 * P)

                    repeat(sp, 4, 2, HEADS, head_units)
                    V = W + 2 * HEADS
                    repeat(sp, 4, 2, KT, lambda i, r: load_unit(sp, V, i, 2, r, wo[:, :, bass.ds((i * 2 + r) * P, P)], KT * P))
                if name == "nsa":
                    w_in, wo = w_view(t["nsa_w_in"][j]), w_view(t["nsa_w_o"][j])
                    first = NSA_COL["kc"]
                    repeat(sp, 2, 2, 4, lambda i, r: load_unit(sp, U, i, 2, r, w_in[:, :, bass.ds((i * 2 + r) * P + first, P)], KT * P))
                    for w, w1 in enumerate(("nsa_w1_k", "nsa_w1_v")):
                        w1 = w_view(t[w1][j])
                        repeat(sp, 4, 2, 8, lambda i, r: load_unit(sp, U + 4 + 8 * w, i, 2, r,
                                                                   w1[:, bass.ds((i * 2 + r) * 4, 4), :], KT * P))
                    for n, key in enumerate(("ks", "kw")):
                        for g in range(GROUPS):
                            c = NSA_COL[key] + g * P
                            load_unit(sp, U + 20, 0, 2, 2 * n + g, w_in[:, :, c:c + P], KT * P)
                    for n, key in enumerate(("vs", "vw")):
                        for half in range(2):
                            c = NSA_COL[key]
                            load_unit(sp, U + 24, 0, 2, 2 * n + half, w_in[:, 4 * half:4 * half + 4, c:c + 2 * P], KT * P)
                    load_unit(sp, U + 28, 0, 2, 0, w_in[:, :, NSA_COL["gate"]:], KT * 3 * HEADS)
                    repeat(sp, 4, 2, HEADS, lambda i, r: load_unit(sp, U + 29, i, 2, r, w_in[:, :, bass.ds((i * 2 + r) * P, P)], KT * P))
                    V = U + 29 + HEADS
                    repeat(sp, 4, 2, KT, lambda i, r: load_unit(sp, V, i, 2, r, wo[:, :, bass.ds((i * 2 + r) * P, P)], KT * P))
                if name == "s5":
                    glu = w_view(t["s5_w_glu"][j])

                    def glu_pair(i, r):
                        for e in range(2):
                            load_unit(sp, U, i, 4, 2 * r + e, glu[:, :, bass.ds((i * 2 + r) * P + e * D, P)], KT * P)

                    glu_pair(0, 0)
                    sp.wait_ge(phase_end, 4 * phases_at[l])
                    for w, key in enumerate(("s5_lam_re", "s5_lam_im")):
                        sp.dma_start(lam_rows[:, w, :], t[key][j].rearrange("(q a) n -> q (a n)", a=2)).then_inc(s5_side, 16)
                    sp.dma_start(dt_rows[:], t["s5_log_dt"][j].rearrange("(q a) -> q a", a=2)).then_inc(s5_side, 16)
                    for w, key in enumerate(("s5_b_re", "s5_b_im")):
                        sp.dma_start(b_in[:, w], t[key][j].rearrange("(q a) n i -> (a n) q i", a=2)).then_inc(s5_side, 16)
                    for w, key in enumerate(("s5_c_re", "s5_c_im")):
                        for twice in range(2):
                            src = t[key][j].rearrange("(k g) i n -> (g i) k n", g=P // SI)
                            sp.dma_start(c_rows[:, w, :, twice, :], src).then_inc(s5_side, 16)
                    repeat(sp, 3, 2, KT - 1, lambda i, r: glu_pair(i, r + 1))
            sp.wait_ge(copied_in, N_TURN + KT + KT)
            sp.dma_start(out.rearrange("b (t p) f -> p (b t) f", p=P), out_rows[:]).then_inc(stored, 16)
            sp.wait_ge(stored, 16)

        @block.tensor
        def _(pe):
            state = [0]
            pe.wait_ge(params_in, 16 * (len(row_loads) + 1))
            pe.wait_ge(consts_in, 32)
            for n, (slot, size, _, _) in enumerate(turns):
                reached(pe, copied_in, n - 3)
                nc.tensor.transpose(bank[:, n % 4, 0:size], rows[0:size, slot, :], ident[0:size, 0:size]).then_inc(turned_in, 1)
            for k in range(KT):
                reached(pe, copied_in, N_TURN + k - 3)
                for tt in range(TT):
                    last = nc.tensor.transpose(bank[:, (N_TURN + k) % 4, tt * P:(tt + 1) * P],
                                               x_rows[:, tt, k * P:(k + 1) * P], ident[:, :])
                last.then_inc(turned_in, 1)
            def modulate(l, half):
                pe.wait_ge(ada_done, 2 * l_at[l] + half + 1)
                for f in range(MODS // 2):
                    last = nc.tensor.matmul(bank[:, 6, f:f + 1], ada_sum[:, f * P:(f + 1) * P], ones[:, 0:1], start=True, stop=True)
                last.then_inc(ada_turned, 1)

            def add_squares(idx, m, slot):
                pe.wait_ge(squares, m + (KT * idx + 1) if not isinstance(m, int) else KT * idx + m + 1)
                nc.tensor.matmul(bank[:, 7, :], ones[:, :], sq_x[:, slot, :], start=isinstance(m, int) and m == 0,
                                 stop=isinstance(m, int) and m == KT - 1, skip_group_check=True).then_inc(sq_used, 1)

            modulate(LAYERS[0], 0)
            for m in range(KT):
                add_squares(0, m, m % 2)
            end_phase(pe, state)

            def residual_units(unit, idx):
                unit(0, 0)
                unit(0, 1)
                add_squares(idx, 0, 0)
                with pe.Fori(1, KT // 2) as i:
                    for r in range(2):
                        unit(i, r)
                        add_squares(idx, i * 2 + (r - 1), (r + 1) % 2)
                add_squares(idx, KT - 1, 1)

            def normed(idx):
                return lambda k: pe.wait_ge(h_low, KT * idx + k + 1)

            def ffn(l, U, drains, idx):
                for half in range(2):
                    V, G = U + half * (2 * HALF + KT), drains + half * (2 * HALF + KT)
                    Q = HALF * (2 * l_at[l] + half)

                    def up_pair(i, r):
                        for e in range(2):
                            u, b = 2 * r + e, 2 * (r % 2) + e
                            pe.wait_ge(lo_made, i * 4 + (V + u + 1))
                            reached(pe, drained, i * 4 + (G + u - 3))
                            first = half == 0 and r == 0 and e == 0
                            feature_product(bank[:, b, :], (V + u) % 2, KT, P, 0, h_hi, h_lo,
                                            normed(idx) if first else None).then_inc(weights_used, 1)

                    def down_unit(i, r):
                        W = V + 2 * HALF
                        pe.wait_ge(lo_made, i * 2 + (W + r + 1))
                        reached(pe, drained, i * 2 + (G + 2 * HALF + r - 1))
                        first = isinstance(i, int) and i == 0 and r == 0
                        feature_product(bank[:, 4 + r % 2, :], (W + r) % 2, HALF, P, 0, g_hi, g_lo,
                                        (lambda k: pe.wait_ge(g_low, Q + k + 1)) if first else None).then_inc(weights_used, 1)

                    repeat(pe, 5, 2, HALF, up_pair, first=1)
                    if half == 1 and l in following:
                        modulate(following[l], 0)
                    if half == 0:
                        repeat(pe, 3, 2, KT, down_unit, first=2)
                    else:
                        residual_units(down_unit, idx + 1)
                if l in following:
                    modulate(following[l], 1)

            def output_projection(U, G, a_hi, a_lo, idx):
                def unit(i, r):
                    pe.wait_ge(lo_made, i * 2 + (U + r + 1))
                    pe.wait_ge(drained, i * 2 + (G + r - 1))
                    feature_product(bank[:, r, :], (U + r) % 2, KT, P, 0, a_hi, a_lo).then_inc(weights_used, 1)

                residual_units(unit, idx)

            def turn(p, r, probs):
                pe.wait_ge(scaled, p + 1)
                for j in range(TT):
                    for i in range(j, TT):
                        last = nc.tensor.transpose(turned_tile(r, j, i), probs[:, r, ROW_AT[i] + j * P:ROW_AT[i] + (j + 1) * P],
                                                   ident[:, :])
                last.then_inc(turned, 1)

            def values(p, r, turned_sb, v, first, last):
                pe.wait_ge(pt_act, p + 3)
                pe.wait_ge(pt_dve, p + 3)
                for j in range(TT):
                    ins = nc.tensor.matmul(bank[:, 6, j * P:S], v[:, j * P:(j + 1) * P],
                                           turned_sb[:, r, COL_AT[j]:COL_AT[j] + S - j * P],
                                           start=first and j == 0, stop=last and j == TT - 1, skip_group_check=True)
                return ins

            def mla(l, j, U, dr, idx, state):
                o = mla_at[l]
                for n in range(DKV_UNITS):
                    pe.wait_ge(lo_made, U + n + 1)
                    reached(pe, drained, dr + n - 1)
                    feature_product(bank[:, n % 2, :], (U + n) % 2, KT, P, 0, h_hi, h_lo,
                                    normed(idx) if n == 0 else None).then_inc(weights_used, 1)
                for n in range(CQ + CKV):
                    pe.wait_ge(drained, dr + n + 1)
                    last = nc.tensor.matmul(bank[:, 4 if n < CQ else 5, :], ones[:, :], sq[:, n, :],
                                            start=n in (0, CQ), stop=n in (CQ - 1, CQ + CKV - 1))
                    if n in (CQ - 1, CQ + CKV - 1):
                        last.then_inc(lat_summed, 1)
                end_phase(pe, state)
                W, pb = U + DKV_UNITS, passes_at[l]

                def project(i, r):
                    s, c = r % 2, 4 * (HEADS * o + r)
                    pe.wait_ge(lo_made, i * 4 + (W + 2 * r + 1))
                    feature_product(bank[:, 3 * s, :], W % 2, CQ, QK, 0, c_hi, c_lo).then_inc(projected, 1)
                    feature_product(bank[:, 3 * s + 1, :], W % 2, CQ, QK, QK - P, c_hi, c_lo).then_inc(weights_used, 1)
                    pe.wait_ge(lo_made, i * 4 + (W + 2 * r + 2))
                    feature_product(bank[:, 3 * s + 2, :], (W + 1) % 2, CKV, 2 * P, 0, c_hi[:, CQ:], c_lo[:, CQ:]).then_inc(projected, 1)
                    reached(pe, fetched, i * 8 + c)
                    token_product(bank[:, 7, :], (W + 1) % 2, CKV, 2 * P, P, P, c_hi[:, CQ:], c_lo[:, CQ:]) \
                        .then_inc(weights_used, 1)

                def scores(i, r):
                    s = r % 2
                    pe.wait_ge(fetched, i * 8 + 4 * (HEADS * o + r + 1))
                    pe.wait_ge(roped, i * 2 + (HEADS * o + r + 1))
                    pe.wait_ge(pt_act, i * 2 + (pb + r + 1))
                    pe.wait_ge(pt_dve, i * 2 + (pb + r + 1))
                    for q in reversed(range(TT)):
                        at, n = slice(q * P, (q + 1) * P), P * (q + 1)
                        nc.tensor.matmul(score_tile(s, q), q_nope[:, s, at], k_nope[:, s, 0:n], start=True, stop=False)
                        nc.tensor.matmul(score_tile(s, q), q_rope[:, s, at], k_rope[:, 0:n], start=False, stop=False)
                        last = nc.tensor.matmul(score_tile(s, q)[:, n - P:n], ident_b[:, :], mask_b[:, :], start=False, stop=True)
                    last.then_inc(scored, 1)

                def head(i, r):
                    s = r % 2
                    whole = not isinstance(i, int)
                    turn(i * 2 + (pb + r), s, m_probs)
                    if whole or 2 * i + r + 1 < HEADS:
                        scores(i, r + 1)
                    pe.wait_ge(o_low, i * 2 + (heads_at[l] + r + 1))
                    values(i * 2 + (pb + r), s, m_turned, v_tok[:, s, :], True, True).then_inc(valued, 1)
                    if whole or 2 * i + r + 2 < HEADS:
                        project(i, r + 2)

                project(0, 0)
                scores(0, 0)
                project(0, 1)
                repeat(pe, 3, 2, HEADS, head)
                end_phase(pe, state)
                output_projection(W + 2 * HEADS, dr + DKV_UNITS, h_hi, h_lo, idx + 1)
                if l == LAYERS[0]:
                    modulate(l, 1)
            def nsa(l, j, U, dr, idx, state):
                for n in range(4):
                    pe.wait_ge(lo_made, U + n + 1)
                    reached(pe, drained, dr + n - 1)
                    feature_product(bank[:, n % 2, :], (U + n) % 2, KT, P, 0, h_hi, h_lo,
                                    normed(idx) if n == 0 else None).then_inc(weights_used, 1)
                pe.wait_ge(nsa_side, 16 * 8)
                for w in range(2):
                    nc.tensor.transpose(bank[:, 4, w * CB:(w + 1) * CB], pe_rows[:, w, :], ident[0:CB, 0:CB])
                nc.tensor.transpose(bank[0:BUCKETS, 5, 0:HEADS], rel[:, :], ident[0:HEADS, 0:HEADS]).then_inc(nsa_small, 1)
                pe.wait_ge(nsa_copied, 1)
                nc.tensor.matmul(bank[0:HEADS, 6, 0:3 * P], rel_t[:, :], near_hot[:, :], start=True, stop=True)
                for w in range(2):
                    last = nc.tensor.matmul(bank[0:HEADS, 2 + w, :], rel_t[:, :], far_hot[:, w * S:(w + 1) * S], start=True, stop=True)
                last.then_inc(nsa_small, 1)
                end_phase(pe, state)
                for w in range(2):
                    for q in range(8):
                        s = (U + 4 + 8 * w + q) % 2
                        pe.wait_ge(lo_made, U + 4 + 8 * w + q + 1)
                        for c in range(4):
                            at = slice(c * 2 * P, (c + 1) * 2 * P)
                            blocks = [b[:, w, q * 4 + c, :, :].rearrange("p g n -> p (g n)") for b in (b_hi, b_lo)]
                            last = three(bank[0:GROUPS * NC, w, 0:2 * P], blocks[0], blocks[1], w_hi[:, s, at], w_lo[:, s, at],
                                         q == 0 and c == 0, q == 7 and c == 3)
                        last.then_inc(weights_used, 1)
                pe.wait_ge(drained, dr + 8)
                for n in range(4):
                    w, hh = n // 2, n % 2
                    last = nc.tensor.transpose(bank[:, 3, n * GROUPS * NC:(n + 1) * GROUPS * NC],
                                               hid_rows[:, w, hh * P:(hh + 1) * P], ident[0:GROUPS * NC, 0:GROUPS * NC])
                last.then_inc(nsa_small, 1)
                pe.wait_ge(nsa_copied, 3)
                for hh in range(2):
                    nc.tensor.matmul(bank[:, 4, 0:GROUPS * NC], w2[:, 0, hh, :], hid[:, 0, hh, :], start=hh == 0, stop=hh == 1)
                for g in range(GROUPS):
                    for hh in range(2):
                        last = nc.tensor.matmul(bank[0:NC, 5, g * P:(g + 1) * P], hid[:, 1, hh, g * NC:(g + 1) * NC], w2[:, 1, hh, :],
                                                start=hh == 0, stop=hh == 1)
                last.then_inc(nsa_small, 1)
                end_phase(pe, state)
                for n in range(4):
                    pe.wait_ge(lo_made, U + 20 + n + 1)
                    pe.wait_ge(drained, dr + 8 + n - 1)
                    feature_product(bank[:, n % 2, :], (U + 20 + n) % 2, KT, P, 0, h_hi, h_lo).then_inc(weights_used, 1)
                for n in range(4):
                    pe.wait_ge(lo_made, U + 24 + n + 1)
                    if n == 2:
                        pe.wait_ge(drained, dr + 12)
                    s = (U + 24 + n) % 2
                    for tt in range(TT):
                        for k in range(4):
                            at, kk = slice(k * 2 * P, (k + 1) * 2 * P), 4 * (n % 2) + k
                            last = three(bank[:, value_bank(n // 2, tt), 0:2 * P], h_hi[:, kk, tt * P:(tt + 1) * P],
                                         h_lo[:, kk, tt * P:(tt + 1) * P], w_hi[:, s, at], w_lo[:, s, at], kk == 0, kk == KT - 1)
                    last.then_inc(weights_used, 1)
                pe.wait_ge(lo_made, U + 29)
                pe.wait_ge(drained, dr + 14)
                s, G = (U + 28) % 2, 3 * HEADS
                for k in range(KT):
                    last = three(bank[0:G, 2, :], w_hi[:, s, k * G:(k + 1) * G], w_lo[:, s, k * G:(k + 1) * G],
                                 h_hi[:, k, :], h_lo[:, k, :], k == 0, k == KT - 1)
                last.then_inc(weights_used, 1)
                pe.wait_ge(drained, dr + 17)
                for tt in range(TT):
                    last = nc.tensor.transpose(bank[:, 6, tt * G:(tt + 1) * G], gate_rows[:, tt * P:(tt + 1) * P], ident[0:G, 0:G])
                last.then_inc(nsa_small, 1)
                pe.wait_ge(rows_back, 16 * (1 + HEADS))
                for n in range(4):
                    last = nc.tensor.matmul(bank[:, 2 + n, :], flip[:, :], near_back[:, 2 * n:2 * n + 2, :], start=True, stop=True)
                last.then_inc(nsa_small, 1)
                pe.wait_ge(nsa_copied, 4)
                rows4 = NC * HEADS // 2
                for tt in range(TT):
                    for n in range(2):
                        last = nc.tensor.matmul(bank[:, 2 + tt, n * rows4:(n + 1) * rows4], cmp_back[:, n, tt * P:(tt + 1) * P],
                                                flip[0:rows4, P - rows4:P], start=True, stop=True)
                last.then_inc(nsa_small, 1)
                end_phase(pe, state)

                W, pb, hb = U + 29, passes_at[l], heads_at[l]

                def project(h):
                    pe.wait_ge(lo_made, W + h + 1)
                    if h == 1:
                        pe.wait_ge(q_ready, 1)
                    else:
                        reached(pe, cmp_copied, h - 1)
                    feature_product(bank[:, 7, :], (W + h) % 2, KT, P, 0, h_hi, h_lo).then_inc(weights_used, 1)

                def scores(h, w):
                    pe.wait_ge(q_ready, h + 1)
                    p = pb + 2 * h + w
                    pe.wait_ge(pt_act, p + 1)
                    pe.wait_ge(pt_dve, p + 1)
                    for q in reversed(range(TT)):
                        last = nc.tensor.matmul(score_tile(w, q), q_t[:, h % 2, q * P:(q + 1) * P],
                                                kf[:, 2 * w + h // HPG, 0:P * (q + 1)], start=True, stop=True)
                    last.then_inc(scored, 1)

                project(0)
                scores(0, 0)
                project(1)
                for h in range(HEADS):
                    g = h // HPG
                    pe.wait_ge(q_ready, min(h + 2, HEADS))
                    for q in range(TT):
                        last = nc.tensor.matmul(bank[:, 7, q * NC:(q + 1) * NC], q_t[:, h % 2, q * P:(q + 1) * P], kc_t[:, g, :],
                                                start=True, stop=True)
                    last.then_inc(cmp_scored, 1)
                    scores(h, 1)
                    turn(pb + 2 * h, 0, n_probs)
                    pe.wait_ge(cmp_scaled, h + 1)
                    for q in range(TT):
                        last = nc.tensor.transpose(bank[0:NC, 7, q * P:(q + 1) * P], cmp_p[:, q, :], ident[:, :])
                    last.then_inc(cmp_turned, 1)
                    pe.wait_ge(o_low, hb + h + 1)
                    values(pb + 2 * h, 0, n_turned, vt[:, g, :], True, False)
                    if h + 1 < HEADS:
                        scores(h + 1, 0)
                    pe.wait_ge(cmp_copied, h + 1)
                    nc.tensor.matmul(bank[:, 6, :], vc_t[:, g, :], cmp_t[:, :], start=False, stop=False, skip_group_check=True)
                    turn(pb + 2 * h + 1, 1, n_probs)
                    if h + 2 < HEADS:
                        project(h + 2)
                    values(pb + 2 * h + 1, 1, n_turned, vt[:, GROUPS + g, :], False, True).then_inc(valued, 1)
                end_phase(pe, state)
                output_projection(W + HEADS, dr + 17, o_hi, o_lo, idx + 1)
            def s5(l, j, U, dr, idx, state):
                pe.wait_ge(s5_side, 16 * 9)
                pe.wait_ge(s5_dve, 1)
                for n in range(3):
                    last = nc.tensor.transpose(bank[:, 0, n * ST:(n + 1) * ST], lam_rows[:, n, :], ident[0:ST, 0:ST])
                last.then_inc(s5_small, 1)
                for k in range(KT):
                    for w in range(2):
                        n = 2 * k + w
                        reached(pe, s5_act, n - 1)
                        nc.tensor.transpose(bank[:, 1 + n % 2, 0:P], c_rows[:, w, k, :, :], ident[:, :]).then_inc(s5_small, 1)
                pe.wait_ge(s5_dve, 2)
                for k in range(KT):
                    for w in range(2):
                        n = 2 * k + w
                        pe.wait_ge(s5_act, 16 + n - 1)
                        nc.tensor.transpose(bank[:, 1 + n % 2, 0:P], b_bar[:, w, 4 * k:4 * k + 4, :], ident[:, :]).then_inc(s5_small, 1)
                end_phase(pe, state)

                def enter(q):
                    k, a, r = q // 4, 32 * (q % 4), q % 2
                    reached(pe, bu_free, q - 1)
                    for w in range(2):
                        last = nc.tensor.matmul(bank[:, 2 * r + w, :], in_map[a:a + 32, w, k, :], hf[a:a + 32, k, :],
                                                start=True, stop=True)
                    last.then_inc(bu_made, 1)

                enter(0)
                enter(1)
                for q in range(ST):
                    k, a, r = q // 4, q % 4, q % 2
                    if q + 2 < ST:
                        enter(q + 2)
                    pe.wait_ge(products_made, q + 1)
                    if a == 0:
                        reached(pe, y_in, k - 1)
                    for n in range(4):
                        last = nc.tensor.matmul(bank[:, 4 + k % 2, :], out_map[:, n // 2, k, a * P:(a + 1) * P], state_w[:, r, n, :],
                                                start=(a == 0 and n == 0), stop=(a == 3 and n == 3))
                    if a == 3:
                        last.then_inc(y_made, 1)
                    else:
                        last.then_inc(products_used, 1)
                end_phase(pe, state)

                def glu_pair(i, r):
                    for e in range(2):
                        u = 2 * r + e
                        pe.wait_ge(lo_made, i * 4 + (U + u + 1))
                        reached(pe, drained, i * 4 + (dr + 2 * r - 2))
                        feature_product(bank[:, u, :], (U + u) % 2, KT, P, 0, h_hi, h_lo).then_inc(weights_used, 1)

                glu_pair(0, 0)
                glu_pair(0, 1)
                add_squares(idx + 1, 0, 0)
                with pe.Fori(1, KT // 2) as i:
                    for r in range(2):
                        glu_pair(i, r)
                        add_squares(idx + 1, i * 2 + (r - 1), (r + 1) % 2)
                add_squares(idx + 1, KT - 1, 1)
            for name, l, j, U, dr, idx in plan:
                if name == "norm":
                    continue
                elif name == "mla":
                    mla(l, j, U, dr, idx, state)
                elif name == "nsa":
                    nsa(l, j, U, dr, idx, state)
                elif name == "s5":
                    s5(l, j, U, dr, idx, state)
                elif name == "ffn":
                    ffn(l, U, dr, idx)
                else:
                    for k in range(KT):
                        pe.wait_ge(h_made, KT * idx + k + 1)
                        reached(pe, copied_in, N_TURN + KT + k - 1)
                        for tt in range(TT):
                            last = nc.tensor.transpose(bank[:, 4 + k % 2, tt * P:(tt + 1) * P],
                                                       hf[:, k, tt * P:(tt + 1) * P], ident[:, :])
                        last.then_inc(turned_in, 1)
                end_phase(pe, state)

        @block.scalar
        def _(act):
            state, chain = [0], Chain(act, act_chain)
            act.wait_ge(c_in, 16)
            nc.scalar.activation(c_act[:, :], c_act[:, :], ACT.Silu).then_inc(silu_made, 1)

            def square(idx, m):
                reached(act, sq_used, KT * idx + m - 1)
                nc.scalar.activation(sq_x[:, m % 2, :], x[:, m, :], ACT.Square).then_inc(squares, 1)

            for m in range(KT):
                act.wait_ge(copied_in, N_TURN + m + 1)
                square(0, m)
            end_phase(act, state)

            def norm(idx, U):
                act.wait_ge(sq_used, KT * (idx + 1))
                nc.scalar.activation(rs[:, :], bank[:, 7, :], ACT.Sqrt, bias=eps[:, :], scale=1.0 / D).then_inc(rooted, 1)
                if U is None:
                    return
                for r in range(2):
                    split_high(act, U, 0, 2, r, KT * P)
                for k in range(KT):
                    act.wait_ge(h_made, KT * idx + k + 1)
                    nc.scalar.copy(h_hi[:, k, :], hf[:, k, :]).then_inc(h_high, 1)

            def residual_splits(U, G, idx, width, primed=0, more=False):
                if idx is not None:
                    nc.scalar.preload_act_table(ACT.Sqrt)
                for n in range(primed, 2):
                    split_high(act, U, 0, 2, n, width)
                for n in range(KT):
                    if n + 2 < KT or more:
                        split_high(act, U, 0, 2, n + 2, width if n + 2 < KT else KT * P)
                    if idx is not None:
                        act.wait_ge(drained, G + n + 1)
                        square(idx, n)

            def ffn(l, U, drains, idx):
                for half in range(2):
                    V, G = U + half * (2 * HALF + KT), drains + half * (2 * HALF + KT)
                    Q = HALF * (2 * l_at[l] + half)
                    nc.scalar.preload_act_table(ACT.Silu)

                    def up_pair(i, r):
                        final = isinstance(i, int) and 2 * i + r + 1 >= HALF
                        for e in range(2):
                            split_high(act, V, i, 4, 2 * (r + 1) + e, UNIT if final else KT * P)
                        act.wait_ge(g_made, i * 2 + (Q + r + 1))
                        s = r % 2
                        for e in range(2):
                            u, col = 2 * r + e, l * CHT + e * PAIRS + half * HALF
                            act.wait_ge(weights_used, i * 4 + (V + u + 1))
                            nc.scalar.activation(cv[:, s, e, :], bank[:, 2 * s + e, :], ACT.Identity,
                                                 bias=cb[:, bass.ds(i * 2 + (col + r), 1)],
                                                 scale=cw[:, bass.ds(i * 2 + ((TAPS * l + 2) * CHT + col - l * CHT + r), 1)]
                                                 ).then_inc(cv_made, 1)
                        act.wait_ge(drained, i * 4 + (G + 2 * r + 2))
                        nc.scalar.activation(sg[:, s, :], cv[:, s, 1, :], ACT.Silu).then_inc(silu_made, 1)
                        act.wait_ge(g_made, i * 2 + (Q + r + 3))
                        nc.scalar.copy(g_hi[:, bass.ds(i * 2 + r, 1), :], gf[:, s:s + 1, :]).then_inc(g_high, 1)

                    repeat(act, 4, 2, HALF, up_pair, first=1)
                    residual_splits(V + 2 * HALF, G + 2 * HALF, idx + 1 if half == 1 else None, UNIT, 2, half == 0)

            def exponents(p, r, probs):
                act.wait_ge(maxed, p + 1)
                for q in reversed(range(TT)):
                    last = nc.scalar.activation(probs[:, r, ROW_AT[q]:ROW_AT[q] + P * (q + 1)], score_tile(r, q), ACT.Exp,
                                                bias=neg_max[:, r, q:q + 1], accum_out=row_sum[:, r, q:q + 1])
                last.then_inc(exped, 1)

            def copy_turned(p, r, turned_sb):
                act.wait_ge(turned, p + 1)
                nc.scalar.copy(turned_sb[:, r, 0:S], bank[:, 3 * r, :]).then_inc(pt_act, 1)

            def head_high(h, m, dst):
                act.wait_ge(valued, h + 1)
                nc.scalar.copy(dst[:, m, :] if isinstance(m, int) else dst[:, bass.ds(m, 1), :].squeeze(1), bank[:, 6, :]) \
                    .then_inc(o_high, 1)

            def mla(l, j, U, dr, idx, state):
                o = mla_at[l]
                for n in range(DKV_UNITS):
                    act.wait_ge(weights_used, U + n + 1)
                    if n + 2 < DKV_UNITS:
                        split_high(act, U, 0, 2, n + 2, KT * P)
                    b = bank[:, n % 2, :]
                    if n < CQ + CKV:
                        nc.scalar.copy(hf[:, n, :], b)
                        nc.scalar.activation(sq[:, n, :], b, ACT.Square).then_inc(drained, 1)
                    else:
                        half = ROPE // 2
                        nc.scalar.copy(k_rope[:, :], b[ROPE:P])
                        nc.scalar.copy(swapped[0:half, 0, :], b[P - half:P])
                        nc.scalar.copy(swapped[half:ROPE, 0, :], b[ROPE:P - half]).then_inc(drained, 1)
                for b, dst, count in ((4, rs, Q_LORA), (5, rs_kv, KV_LORA)):
                    act.wait_ge(lat_summed, 2 * o + b - 3)
                    nc.scalar.activation(dst[:, :], bank[:, b, :], ACT.Sqrt, bias=eps[:, :], scale=1.0 / count).then_inc(lat_rooted, 1)
                for n in range(CQ + CKV):
                    act.wait_ge(c_made, 6 * o + n + 1)
                    nc.scalar.copy(c_hi[:, n, :], hf[:, n, :]).then_inc(c_high, 1)
                end_phase(act, state)
                W, pb = U + DKV_UNITS, passes_at[l]

                def splits(i, r):
                    split_high(act, W, i, 4, 2 * r, CQ * QK)
                    split_high(act, W, i, 4, 2 * r + 1, CKV * 2 * P)

                def fetch(i, r):
                    s, c, half = r % 2, 4 * (HEADS * o + r), ROPE // 2
                    act.wait_ge(projected, i * 4 + (2 * (HEADS * o + r) + 1))
                    nc.scalar.mul(q_nope[:, s, :], bank[:, 3 * s, :], MLA_SCALE).then_inc(fetched, 1)
                    act.wait_ge(weights_used, i * 4 + (W + 2 * r + 1))
                    nc.scalar.mul(q_rope[:, s, :], bank[ROPE:P, 3 * s + 1, :], MLA_SCALE)
                    nc.scalar.mul(swapped[0:half, s, :], bank[P - half:P, 3 * s + 1, :], MLA_SCALE)
                    nc.scalar.mul(swapped[half:ROPE, s, :], bank[ROPE:P - half, 3 * s + 1, :], MLA_SCALE).then_inc(fetched, 1)
                    act.wait_ge(fetched, i * 8 + (c + 3))
                    act.wait_ge(weights_used, i * 4 + (W + 2 * r + 2))
                    nc.scalar.copy(v_tok[:, s, :], bank[:, 7, :]).then_inc(fetched, 1)

                def head(i, r):
                    s, whole = r % 2, not isinstance(i, int)
                    if whole or 2 * i + r + 2 < HEADS:
                        splits(i, r + 2)
                    copy_turned(i * 2 + (pb + r), s, m_turned)
                    if whole or 2 * i + r + 1 < HEADS:
                        exponents(i * 2 + (pb + r + 1), 1 - s, m_probs)
                    head_high(i * 2 + (heads_at[l] + r), i * 2 + r, h_hi)
                    if whole or 2 * i + r + 2 < HEADS:
                        fetch(i, r + 2)

                splits(0, 0)
                fetch(0, 0)
                splits(0, 1)
                exponents(pb, 0, m_probs)
                fetch(0, 1)
                nc.scalar.preload_act_table(ACT.Exp)
                repeat(act, 3, 2, HEADS, head)
                end_phase(act, state)
                residual_splits(W + 2 * HEADS, dr + DKV_UNITS, idx + 1, KT * P)
            def nsa(l, j, U, dr, idx, state):
                for n in range(2, 4):
                    split_high(act, U, 0, 2, n, KT * P)
                for n in range(4):
                    act.wait_ge(b_made, n + 1)
                    nc.scalar.copy(b_hi[:, n // 2, (n % 2) * CS:(n % 2 + 1) * CS], b_new[:, n % 2]).then_inc(b_high, 1)
                end_phase(act, state)
                nc.scalar.preload_act_table(ACT.Gelu_apprx_tanh)
                split_high(act, U + 4, 0, 2, 0, KT * P)
                for n in range(16):
                    if n + 1 < 16:
                        split_high(act, U + 4, 0, 2, n + 1, KT * P)
                    if n % 8 == 7:
                        act.wait_ge(weights_used, U + 4 + n + 1)
                        for hh in range(2):
                            at = slice(hh * P, (hh + 1) * P)
                            nc.scalar.activation(hid_rows[:, n // 8, at], bank[0:GROUPS * NC, n // 8, at],
                                                 ACT.Gelu_apprx_tanh).then_inc(drained, 1)
                end_phase(act, state)
                for n in range(9):
                    split_high(act, U + 20, 0, 2, n, KT * (P if n < 8 else 3 * HEADS))
                act.wait_ge(weights_used, U + 29)
                act.wait_ge(drained, dr + 16)
                nc.scalar.activation(gate_rows[:, :], bank[0:3 * HEADS, 2, :], ACT.Sigmoid).then_inc(drained, 1)
                act.wait_ge(nsa_small, 5)
                nc.scalar.copy(gates[:, :, :], bank[:, 6, 0:TT * 3 * HEADS].rearrange("p (t n) -> p t n", t=TT))
                end_phase(act, state)
                W, pb, hb = U + 29, passes_at[l], heads_at[l]

                def fetch(h):
                    act.wait_ge(weights_used, W + h + 1)
                    nc.scalar.mul(q_t[:, h % 2, :], bank[:, 7, :], NSA_SCALE).then_inc(q_ready, 1)

                split_high(act, W, 0, 2, 0, KT * P)
                split_high(act, W, 0, 2, 1, KT * P)
                fetch(0)
                exponents(pb, 0, n_probs)
                fetch(1)
                for h in range(HEADS):
                    act.wait_ge(cmp_maxed, h + 1)
                    for q in range(TT):
                        last = nc.scalar.activation(cmp_p[:, q, :], cmp_p[:, q, :], ACT.Exp, bias=cmp_max[:, q:q + 1],
                                                    accum_out=cmp_sum[:, q:q + 1])
                    last.then_inc(cmp_exped, 1)
                    if h:
                        head_high(hb + h - 1, h - 1, o_hi)
                    if h + 2 < HEADS:
                        split_high(act, W, 0, 2, h + 2, KT * P)
                    copy_turned(pb + 2 * h, 0, n_turned)
                    act.wait_ge(cmp_turned, h + 1)
                    nc.scalar.copy(cmp_t[:, :], bank[0:NC, 7, :]).then_inc(cmp_copied, 1)
                    exponents(pb + 2 * h + 1, 1, n_probs)
                    copy_turned(pb + 2 * h + 1, 1, n_turned)
                    if h + 1 < HEADS:
                        exponents(pb + 2 * h + 2, 0, n_probs)
                    if h + 2 < HEADS:
                        fetch(h + 2)
                head_high(hb + HEADS - 1, HEADS - 1, o_hi)
                end_phase(act, state)
                residual_splits(W + HEADS, dr + 17, idx + 1, KT * P)
            def s5(l, j, U, dr, idx, state):
                act.wait_ge(s5_ready, 1)
                nc.scalar.activation(small[:, 11, :], small[:, 11, :], ACT.Exp).then_inc(s5_exp, 1)
                act.wait_ge(s5_zeroed, 2)
                for k in range(KT):
                    for w in range(2):
                        n = 2 * k + w
                        act.wait_ge(s5_small, 2 + n)
                        src = bank[:, 1 + n % 2, 0:P].rearrange("p (q i) -> p q i", q=4)
                        dst = out_map[:, w, k, 0:640].rearrange("p (q i) -> p q i", q=4)
                        nc.scalar.mul(dst[0:SN, :, 0:SI], src[0:SN, :, 0:SI], 1.0 - 2 * w)
                        nc.scalar.mul(dst[SN:P, :, SI:2 * SI], src[SN:P, :, SI:2 * SI], 1.0 - 2 * w).then_inc(s5_act, 1)
                act.wait_ge(s5_dve2, 1)
                nc.scalar.activation(small[:, 5, :], small[:, 3, :], ACT.Exp).then_inc(s5_exp, 1)
                nc.scalar.activation(small[:, 6, :], small[:, 4, :], ACT.Sin)
                nc.scalar.activation(small[:, 7, :], small[:, 4, :], ACT.Sin, scale=0.5).then_inc(s5_exp, 1)
                for n in range(2 * KT):
                    act.wait_ge(s5_small, 18 + n)
                    nc.scalar.copy(in_map[:, n % 2, n // 2, :], bank[:, 1 + n % 2, 0:P]).then_inc(s5_act, 1)
                end_phase(act, state)
                for k in range(KT):
                    act.wait_ge(y_in, k + 1)
                    nc.scalar.activation(hf[:, k, :], hf[:, k, :], ACT.Gelu_apprx_tanh).then_inc(y_gelu, 1)
                    act.wait_ge(y_gelu, k + 1)
                    nc.scalar.copy(h_hi[:, k, :], hf[:, k, :]).then_inc(y_high, 1)
                end_phase(act, state)

                nc.scalar.preload_act_table(ACT.Sigmoid)
                for n in range(KT):
                    if n + 1 < KT:
                        split_high(act, U, 0, 2, 2 * n + 2, KT * P)
                    if n:
                        act.wait_ge(drained, dr + 2 * n)
                        square(idx + 1, n - 1)
                    if n + 1 < KT:
                        split_high(act, U, 0, 2, 2 * n + 3, KT * P)
                    act.wait_ge(weights_used, U + 2 * n + 2)
                    nc.scalar.activation(sig[:, n % 2, :], bank[:, 2 * (n % 2) + 1, :], ACT.Sigmoid).then_inc(sig_made, 1)
                act.wait_ge(drained, dr + 2 * KT)
                square(idx + 1, KT - 1)
            for name, l, j, U, dr, idx in plan:
                if name == "norm":
                    norm(idx, U)
                    continue
                elif name == "mla":
                    mla(l, j, U, dr, idx, state)
                elif name == "nsa":
                    nsa(l, j, U, dr, idx, state)
                elif name == "s5":
                    s5(l, j, U, dr, idx, state)
                elif name == "ffn":
                    ffn(l, U, dr, idx)
                else:
                    norm(idx, None)
                end_phase(act, state)

        @block.vector
        def _(dve):
            state, chain = [0], Chain(dve, dve_chain)
            chain.link(nc.vector.memset(ones[:, :], 1.0))
            chain.link(nc.vector.memset(eps[:, :], EPS))
            dve.wait_ge(consts_in, 32)
            chain.link(nc.vector.tensor_copy(ident_b[:, :], ident[:, :]))
            chain.link(nc.vector.tensor_copy(mask_b[:, :], mask[:, :]))
            for n, (slot, size, dst, col) in enumerate(turns):
                dve.wait_ge(turned_in, n + 1)
                nc.vector.tensor_copy(dst[:, col:col + size], bank[:, n % 4, 0:size]).then_inc(copied_in, 1)
            for k in range(KT):
                dve.wait_ge(turned_in, N_TURN + k + 1)
                nc.vector.tensor_copy(x[:, k, :], bank[:, (N_TURN + k) % 4, :]).then_inc(copied_in, 1)
            dve.wait_ge(silu_made, 1)

            def ada_piece(l, n):
                g = 2 * KT * l_at[l] + n
                src, arrived, count = ada_slot(g)
                dve.wait_ge(arrived, 16 * count)
                reached(dve, ada_used, g)
                if n % KT == 0:
                    reached(dve, ada_turned, g // KT)
                    ins = nc.vector.tensor_scalar(ada_sum, src, c_act[:, 0:1], None, ALU.mult)
                else:
                    ins = nc.vector.scalar_tensor_tensor(out=ada_sum, in0=src, scalar=c_act[:, n % KT:n % KT + 1],
                                                         in1=ada_sum, op0=ALU.mult, op1=ALU.add)
                ins.then_inc(ada_used, 1)
                if n % KT == KT - 1:
                    dve.wait_ge(ada_used, g + 1)
                    dve.sem_inc(ada_done, 1)

            def take_modulation(l, half):
                dve.wait_ge(ada_turned, 2 * l_at[l] + half + 1)
                a = mod_col(l, 3 * half, 0)
                at = mod[:, a:a + MODS // 2]
                chain.link(nc.vector.tensor_tensor(at, bank[:, 6, 0:MODS // 2], at, ALU.add))
                g = 32 * half + KT * l
                chain.link(nc.vector.scalar_tensor_tensor(
                    out=amp[:, (2 * l + half) * KT:(2 * l + half + 1) * KT], in0=mod[:, a + KT:a + 2 * KT], scalar=1.0,
                    in1=misc[:, g:g + KT], op0=ALU.add, op1=ALU.mult))

            for n in range(KT):
                ada_piece(LAYERS[0], n)
            take_modulation(LAYERS[0], 0)
            end_phase(dve, state)


            def norm(l, which, idx, U=None):
                dve.wait_ge(rooted, idx + 1)
                nc.vector.reciprocal(rs[:, :], rs[:, :]).then_inc(rs_made, 1)

                def low(k):
                    dve.wait_ge(h_high, KT * idx + k + 1)
                    dve.wait_ge(h_made, KT * idx + k + 1)
                    nc.vector.tensor_tensor(h_lo[:, k, :], hf[:, k, :], h_hi[:, k, :].bitcast(F32), ALU.subtract).then_inc(h_low, 1)

                if U is not None:
                    split_low(dve, U, 0, 2, 0, KT * P)
                for k in range(KT):
                    if U is not None and k == KT // 2:
                        split_low(dve, U, 0, 2, 1, KT * P)
                    dve.wait_ge(x_scaled, KT * idx + k + 1)
                    if which == 2:
                        a = NORM_COLS["final"] + k
                        nc.vector.tensor_scalar(hf[:, k, :], hf[:, k, :], misc[:, a:a + 1], None, ALU.mult).then_inc(h_made, 1)
                    else:
                        a, b = (2 * l + which) * KT + k, mod_col(l, 3 * which, k)
                        nc.vector.tensor_scalar(hf[:, k, :], hf[:, k, :], amp[:, a:a + 1], mod[:, b:b + 1],
                                                ALU.mult, ALU.add).then_inc(h_made, 1)
                        if k:
                            low(k - 1)
                if which != 2:
                    low(KT - 1)

            def residual(l, part, m, src, mark):
                nc.vector.scalar_tensor_tensor(
                    out=x[:, bass.ds(m, 1), :].squeeze(1) if not isinstance(m, int) else x[:, m, :], in0=src,
                    scalar=mod[:, bass.ds(m + mod_col(l, part, 0), 1)],
                    in1=x[:, bass.ds(m, 1), :].squeeze(1) if not isinstance(m, int) else x[:, m, :],
                    op0=ALU.mult, op1=ALU.add).then_inc(mark, 1)

            def residual_lows(l, part, U, b, width, ada=None, primed=0, more=False):
                for n in range(primed, 2):
                    split_low(dve, U, 0, 2, n, width)
                for n in range(KT):
                    dve.wait_ge(weights_used, U + n + 1)
                    residual(l, part, n, bank[:, b + n % 2, :], drained)
                    if n + 2 < KT or more:
                        split_low(dve, U, 0, 2, n + 2, width if n + 2 < KT else KT * P)
                    if ada is not None:
                        ada_piece(ada[0], ada[1] * KT + n)

            def ffn(l, U, drains, idx):
                for half in range(2):
                    V, G = U + half * (2 * HALF + KT), drains + half * (2 * HALF + KT)
                    Q = HALF * (2 * l_at[l] + half)

                    def up_pair(i, r):
                        final = isinstance(i, int) and 2 * i + r + 1 >= HALF
                        for e in range(2):
                            split_low(dve, V, i, 4, 2 * (r + 1) + e, UNIT if final else KT * P)
                        s = r % 2
                        for tap in (1, 0):
                            back = 2 - tap
                            for e in range(2):
                                if tap == 1:
                                    dve.wait_ge(cv_made, i * 4 + (2 * Q + 2 * r + e + 1))
                                col = (TAPS * l + tap) * CHT + e * PAIRS + half * HALF
                                ins = nc.vector.scalar_tensor_tensor(
                                    out=cv[:, s, e, back:], in0=bank[:, 2 * s + e, 0:S - back],
                                    scalar=cw[:, bass.ds(i * 2 + (col + r), 1)], in1=cv[:, s, e, back:],
                                    op0=ALU.mult, op1=ALU.add)
                                if tap == 1:
                                    chain.step(ins)
                                else:
                                    ins.then_inc(drained, 1)
                            if tap == 1:
                                chain.wait()
                        dve.wait_ge(silu_made, i * 2 + (1 + Q + r + 1))
                        dve.wait_ge(drained, i * 4 + (G + 2 * r + 2))
                        nc.vector.tensor_tensor(gf[:, s, :], cv[:, s, 0, :], sg[:, s, :], ALU.mult).then_inc(g_made, 1)
                        dve.wait_ge(g_high, i * 2 + (Q + r + 1))
                        dve.wait_ge(g_made, i * 2 + (Q + r + 3))
                        nc.vector.tensor_tensor(g_lo[:, bass.ds(i * 2 + r, 1), :], gf[:, s:s + 1, :],
                                                g_hi[:, bass.ds(i * 2 + r, 1), :].bitcast(F32),
                                                ALU.subtract).then_inc(g_low, 1)

                    repeat(dve, 4, 2, HALF, up_pair, chain, 2, first=1)
                    if half == 1 and l in following:
                        take_modulation(following[l], 0)
                    residual_lows(l, 5, V + 2 * HALF, 4, UNIT, (following[l], half) if l in following else None, 2, half == 0)
                if l in following:
                    take_modulation(following[l], 1)

            def maxima(p, r, bias=None):
                dve.wait_ge(scored, p + 1)
                if bias is not None:
                    for q in reversed(range(TT)):
                        n = P * (q + 1)
                        w = min(n, FAR)
                        dst = score_tile(r, q)[:, n - w:n]
                        chain.step(nc.vector.tensor_tensor(dst, dst, bias[:, FAR - w:FAR], ALU.add))
                    chain.wait()
                for q in reversed(range(TT)):
                    last = nc.vector.tensor_reduce(neg_max[:, r, q:q + 1], score_tile(r, q), AX, ALU.max, negate=True)
                last.then_inc(maxed, 1)

            def factors(p, r, gate=None):
                dve.wait_ge(exped, p + 1)
                chain.link(nc.vector.tensor_scalar(row_sum[:, r, :], row_sum[:, r, :], 1e-30, None, ALU.max))
                if gate is None:
                    nc.vector.reciprocal(factor[:, r, :], row_sum[:, r, :]).then_inc(factored, 1)
                else:
                    chain.link(nc.vector.reciprocal(factor[:, r, :], row_sum[:, r, :]))
                    nc.vector.tensor_tensor(factor[:, r, :], factor[:, r, :], gate, ALU.mult).then_inc(factored, 1)

            def copy_turned(p, r, turned_sb):
                dve.wait_ge(turned, p + 1)
                nc.vector.tensor_copy(turned_sb[:, r, S:TRI].rearrange("p (b n) -> p b n", b=2),
                                      bank[:, 3 * r + 1:3 * r + 3, 0:3 * P]).then_inc(pt_dve, 1)

            def head_low(h, m, dst, high):
                dve.wait_ge(o_high, h + 1)
                if isinstance(m, int):
                    a, b = dst[:, m, :], high[:, m, :]
                else:
                    a, b = dst[:, bass.ds(m, 1), :].squeeze(1), high[:, bass.ds(m, 1), :].squeeze(1)
                nc.vector.tensor_tensor(a, bank[:, 6, :], b.bitcast(F32), ALU.subtract).then_inc(o_low, 1)

            def rotate(dst, swap, mark=None):
                chain.step(nc.vector.tensor_tensor(dst, dst, rope[:, 0, :], ALU.mult))
                chain.link(nc.vector.tensor_tensor(swap, swap, rope[:, 1, :], ALU.mult))
                ins = nc.vector.tensor_tensor(dst, dst, swap, ALU.add)
                if mark is not None:
                    ins.then_inc(mark, 1)

            def mla(l, j, U, dr, idx, state):
                o = mla_at[l]
                for n in range(2, DKV_UNITS):
                    split_low(dve, U, 0, 2, n, KT * P)
                dve.wait_ge(mla_side, 16 * (o + 1))
                dve.wait_ge(drained, dr + DKV_UNITS)
                rotate(k_rope[:, :], swapped[:, 0, :])
                dve.wait_ge(lat_rooted, 2 * o + 2)
                chain.step(nc.vector.reciprocal(rs[:, :], rs[:, :]))
                chain.link(nc.vector.reciprocal(rs_kv[:, :], rs_kv[:, :]))
                for n in range(CQ + CKV):
                    g = NORM_COLS["gq"] + CQ * j + n if n < CQ else NORM_COLS["gkv"] + CKV * j + n - CQ
                    nc.vector.scalar_tensor_tensor(out=hf[:, n, :], in0=hf[:, n, :], scalar=misc[:, g:g + 1],
                                                   in1=(rs if n < CQ else rs_kv)[:, :], op0=ALU.mult,
                                                   op1=ALU.mult).then_inc(c_made, 1)
                for n in range(CQ + CKV):
                    dve.wait_ge(c_high, 6 * o + n + 1)
                    dve.wait_ge(c_made, 6 * o + n + 1)
                    nc.vector.tensor_tensor(c_lo[:, n, :], hf[:, n, :], c_hi[:, n, :].bitcast(F32), ALU.subtract)
                end_phase(dve, state)
                W, pb = U + DKV_UNITS, passes_at[l]

                def splits(i, r):
                    split_low(dve, W, i, 4, 2 * r, CQ * QK)
                    split_low(dve, W, i, 4, 2 * r + 1, CKV * 2 * P)

                def fetch(i, r):
                    s, c = r % 2, 4 * (HEADS * o + r)
                    dve.wait_ge(fetched, i * 8 + (c + 2))
                    rotate(q_rope[:, s, :], swapped[:, s, :], roped)
                    dve.wait_ge(projected, i * 4 + (2 * (HEADS * o + r) + 2))
                    nc.vector.tensor_copy(k_nope[:, s, :], bank[:, 3 * s + 2, :]).then_inc(fetched, 1)

                def head(i, r):
                    s, whole = r % 2, not isinstance(i, int)
                    if whole or 2 * i + r + 2 < HEADS:
                        splits(i, r + 2)
                    copy_turned(i * 2 + (pb + r), s, m_turned)
                    if whole or 2 * i + r + 1 < HEADS:
                        maxima(i * 2 + (pb + r + 1), 1 - s)
                    head_low(i * 2 + (heads_at[l] + r), i * 2 + r, h_lo, h_hi)
                    if whole or 2 * i + r + 1 < HEADS:
                        factors(i * 2 + (pb + r + 1), 1 - s)
                    if whole or 2 * i + r + 2 < HEADS:
                        fetch(i, r + 2)

                splits(0, 0)
                fetch(0, 0)
                splits(0, 1)
                maxima(pb, 0)
                factors(pb, 0)
                fetch(0, 1)
                repeat(dve, 3, 2, HEADS, head, chain, 3)
                end_phase(dve, state)
                first = l == LAYERS[0]
                residual_lows(l, 2, W + 2 * HEADS, 0, KT * P, (l, 1) if first else None)
                if first:
                    take_modulation(l, 1)
            def nsa(l, j, U, dr, idx, state):
                for n in range(4):
                    if n + 2 < 4:
                        split_low(dve, U, 0, 2, n + 2, KT * P)
                    dve.wait_ge(weights_used, U + n + 1)
                    nc.vector.tensor_copy(hf[:, n, :], bank[:, n % 2, :]).then_inc(drained, 1)
                chain.link(nc.vector.memset(rel_t[:, :], 1.0))
                dve.wait_ge(nsa_small, 1)
                chain.link(nc.vector.tensor_copy(pe_col[:, :, :], bank[:, 4, 0:2 * CB]))
                nc.vector.tensor_copy(rel_t[0:BUCKETS, :], bank[0:BUCKETS, 5, 0:HEADS]).then_inc(nsa_copied, 1)
                dve.wait_ge(drained, dr + 4)
                for n in range(4):
                    w, a = n // 2, n % 2
                    if n >= 2:
                        dve.wait_ge(b_low, n - 1)
                    src = hf[:, 2 * w:2 * w + 2, :].rearrange("p g (m b) -> p b g m", b=CS)[:, :, :, a:a + NC]
                    emb = pe_col[:, w, a * CS:(a + 1) * CS].unsqueeze(2).unsqueeze(3).broadcast_to([P, CS, GROUPS, NC])
                    for g in range(GROUPS):
                        ins = nc.vector.tensor_tensor(b_new[:, a, :, g, :], src[:, :, g, :], emb[:, :, g, :], ALU.add)
                        if g == 0:
                            chain.step(ins)
                        else:
                            ins.then_inc(b_made, 1)
                    dve.wait_ge(b_high, n + 1)
                    dve.wait_ge(b_made, n + 1)
                    chain.wait()
                    nc.vector.tensor_tensor(b_lo[:, w, a * CS:(a + 1) * CS], b_new[:, a],
                                            b_hi[:, w, a * CS:(a + 1) * CS].bitcast(F32), ALU.subtract).then_inc(b_low, 1)
                dve.wait_ge(nsa_small, 2)
                chain.step(nc.vector.tensor_scalar(near_rows[:, :], bank[0:HEADS, 6, 0:3 * P], rel[:, BUCKETS - 1:BUCKETS], None,
                                                   ALU.subtract))
                nc.vector.tensor_copy(far_rows[:, :].rearrange("p (b n) -> p b n", b=2), bank[0:HEADS, 2:4, :]).then_inc(nsa_copied, 1)
                end_phase(dve, state)
                for n in range(16):
                    split_low(dve, U + 4, 0, 2, n, KT * P)
                dve.wait_ge(nsa_small, 3)
                nc.vector.tensor_copy(hid[:, :, :, :].rearrange("p w h n -> p (w h n)"), bank[:, 3, 0:4 * GROUPS * NC]).then_inc(nsa_copied, 1)
                dve.wait_ge(nsa_small, 4)
                nc.vector.tensor_copy(kc_t[:, :, :], bank[:, 4, 0:GROUPS * NC])
                nc.vector.tensor_copy(vc_t[:, :, :], bank[0:NC, 5, 0:GROUPS * P])
                end_phase(dve, state)
                split_low(dve, U + 20, 0, 2, 0, KT * P)
                for n in range(8):
                    split_low(dve, U + 20, 0, 2, n + 1, KT * (P if n + 1 < 8 else 3 * HEADS))
                    dve.wait_ge(weights_used, U + 20 + n + 1)
                    if n < 4:
                        nc.vector.tensor_copy(kf[:, n, :], bank[:, n % 2, :]).then_inc(drained, 1)
                    elif n % 2 == 1:
                        v = (n - 4) // 2
                        for tt in (0, 2):
                            b = value_bank(v, tt)
                            nc.vector.tensor_copy(vt[:, 2 * v:2 * v + 2, tt * P:(tt + 2) * P].rearrange("p g (t f) -> p t g f", t=2),
                                                  bank[:, b:b + 2, 0:2 * P].rearrange("p t (g f) -> p t g f", g=2)).then_inc(drained, 1)
                dve.wait_ge(nsa_small, 6)
                nc.vector.tensor_copy(near_b[:, :, :].rearrange("p (b h) n -> p b (h n)", b=4), bank[:, 2:6, :]).then_inc(nsa_copied, 1)
                dve.wait_ge(nsa_small, 7)
                for h in range(HEADS):
                    a = (h // 4) * NC * HEADS // 2 + NC * (3 - h % 4)
                    nc.vector.tensor_copy(cmp_b[:, h, :, :], bank[:, 2:6, a:a + NC])
                end_phase(dve, state)
                W, pb, hb = U + 29, passes_at[l], heads_at[l]

                def low_of_query(h):
                    split_low(dve, W, 0, 2, h, KT * P)

                low_of_query(0)
                low_of_query(1)
                maxima(pb, 0, near_b[:, 0, :])
                factors(pb, 0, gates[:, :, HEADS])
                for h in range(HEADS):
                    dve.wait_ge(cmp_scored, h + 1)
                    chain.link(nc.vector.tensor_tensor(cmp_p[:, :, :], bank[:, 7, 0:TT * NC].rearrange("p (t n) -> p t n", t=TT),
                                                       cmp_b[:, h, :, :], ALU.add))
                    chain.link(nc.vector.tensor_reduce(cmp_max[:, :], cmp_p[:, :, :], AX, ALU.max))
                    nc.vector.tensor_scalar(cmp_max[:, :], cmp_max[:, :], MASKED * 1e-10, -1.0, ALU.max, ALU.mult).then_inc(cmp_maxed, 1)
                    if h:
                        head_low(hb + h - 1, h - 1, o_lo, o_hi)
                    dve.wait_ge(cmp_exped, h + 1)
                    chain.link(nc.vector.tensor_scalar(cmp_sum[:, :], cmp_sum[:, :], 1e-30, None, ALU.max))
                    chain.link(nc.vector.reciprocal(cmp_f[:, :], cmp_sum[:, :]))
                    chain.link(nc.vector.tensor_tensor(cmp_f[:, :], cmp_f[:, :], gates[:, :, h], ALU.mult))
                    nc.vector.tensor_tensor(cmp_p[:, :, :], cmp_p[:, :, :],
                                            cmp_f[:, :].unsqueeze(2).broadcast_to([P, TT, NC]), ALU.mult).then_inc(cmp_scaled, 1)
                    maxima(pb + 2 * h + 1, 1, near_b[:, h, :])
                    copy_turned(pb + 2 * h, 0, n_turned)
                    if h + 2 < HEADS:
                        low_of_query(h + 2)
                    factors(pb + 2 * h + 1, 1, gates[:, :, 2 * HEADS + h])
                    if h + 1 < HEADS:
                        maxima(pb + 2 * h + 2, 0, near_b[:, h + 1, :])
                    copy_turned(pb + 2 * h + 1, 1, n_turned)
                    if h + 1 < HEADS:
                        factors(pb + 2 * h + 2, 0, gates[:, :, HEADS + h + 1])
                head_low(hb + HEADS - 1, HEADS - 1, o_lo, o_hi)
                end_phase(dve, state)
                residual_lows(l, 2, W + HEADS, 0, KT * P)
            def s5(l, j, U, dr, idx, state):
                T = nc.vector.tensor_tensor
                TS = nc.vector.tensor_scalar

                def complex_product(o_re, o_im, a_re, a_im, b_re, b_im, w1, w2):
                    chain.step(T(w1, a_re, b_re, ALU.mult))
                    chain.link(T(w2, a_im, b_im, ALU.mult))
                    chain.link(T(o_re, w1, w2, ALU.subtract))
                    chain.step(T(w1, a_re, b_im, ALU.mult))
                    chain.link(T(w2, a_im, b_re, ALU.mult))
                    chain.link(T(o_im, w1, w2, ALU.add))

                dve.wait_ge(s5_side, 16 * 9)
                nc.vector.tensor_copy(lam_rows[:, 2, :].rearrange("q (a n) -> q a n", a=2),
                                      dt_rows[:, :].unsqueeze(2).broadcast_to([ST, 2, SN])).then_inc(s5_dve, 1)
                dve.wait_ge(s5_small, 1)
                chain.link(nc.vector.tensor_copy(small[:, 0:3, :], bank[:, 0, 0:3 * ST].rearrange("p (n q) -> p n q", n=3)))
                lre, lim, dt, grow, ang = (small[:, n, :] for n in range(5))
                e_grow, sin, sin_half, cos, mag1, w1, w2, f_re, f_im, lb1, lb_im, turns, inside, poly = (small[:, n, :] for n in range(5, 19))
                chain.link(TS(turns, dt, 1.0 / math.log(2), ROUND, ALU.mult, ALU.add))
                chain.link(TS(turns, turns, ROUND, None, ALU.subtract))
                TS(w2, turns, math.log(2), 0.35, ALU.mult, ALU.add).then_inc(s5_ready, 1)
                for part in LN_2:
                    chain.link(nc.vector.scalar_tensor_tensor(out=dt, in0=turns, scalar=-part, in1=dt, op0=ALU.mult, op1=ALU.add))
                chain.link(TS(dt, dt, 1.0, -1.0, ALU.min, ALU.max))
                chain.link(TS(poly, dt, 1.0 / math.factorial(SERIES), 1.0 / math.factorial(SERIES - 1), ALU.mult, ALU.add))
                for n in range(SERIES - 2, -1, -1):
                    chain.link(T(poly, poly, dt, ALU.mult))
                    chain.link(TS(poly, poly, 1.0 / math.factorial(n), None, ALU.add))
                dve.wait_ge(s5_exp, 1)
                bits = w2.bitcast(mybir.dt.uint32)
                chain.link(TS(bits, bits, 0x7F800000, None, ALU.bitwise_and))
                chain.link(T(dt, poly, w2, ALU.mult))
                chain.step(T(grow, lre, dt, ALU.mult))
                chain.link(T(ang, lim, dt, ALU.mult))
                chain.link(TS(turns, ang, 1.0 / (2 * math.pi), ROUND, ALU.mult, ALU.add))
                chain.link(TS(turns, turns, ROUND, None, ALU.subtract))
                for part in TWO_PI:
                    chain.link(nc.vector.scalar_tensor_tensor(out=ang, in0=turns, scalar=-part, in1=ang, op0=ALU.mult, op1=ALU.add))
                TS(ang, ang, PI_IN, -PI_IN, ALU.min, ALU.max).then_inc(s5_dve2, 1)
                chain.link(TS(w1, grow, 0.5, -0.5, ALU.min, ALU.max))
                chain.link(TS(poly, w1, 1.0 / math.factorial(SERIES), 1.0 / math.factorial(SERIES - 1), ALU.mult, ALU.add))
                for n in range(SERIES - 2, 0, -1):
                    chain.link(T(poly, poly, w1, ALU.mult))
                    chain.link(TS(poly, poly, 1.0 / math.factorial(n), None, ALU.add))
                chain.link(T(poly, poly, w1, ALU.mult))
                chain.link(T(inside, w1, grow, ALU.is_equal))
                dve.wait_ge(s5_exp, 3)
                chain.link(TS(e_grow, e_grow, 1.0, None, ALU.subtract))
                chain.link(nc.vector.tensor_copy(mag1, e_grow))
                chain.link(nc.vector.copy_predicated(mag1, inside.bitcast(mybir.dt.uint32), poly))
                chain.link(T(w1, sin_half, sin_half, ALU.mult))
                chain.link(TS(w1, w1, -2.0, None, ALU.mult))
                chain.step(TS(cos, w1, 1.0, None, ALU.add))
                chain.link(TS(decay[:, :], mag1, 1.0, None, ALU.add))
                chain.link(T(w2, mag1, cos, ALU.mult))
                chain.step(T(lb1, w2, w1, ALU.add))
                chain.link(T(lb_im, decay[:, :], sin, ALU.mult))
                dve.sem_inc(s5_trig, 1)
                chain.step(T(w1, lre, lre, ALU.mult))
                chain.link(T(w2, lim, lim, ALU.mult))
                chain.link(T(turns, w1, w2, ALU.add))
                chain.link(nc.vector.reciprocal(turns, turns))
                chain.step(T(w1, lb1, lre, ALU.mult))
                chain.link(T(w2, lb_im, lim, ALU.mult))
                chain.link(T(f_re, w1, w2, ALU.add))
                chain.step(T(f_re, f_re, turns, ALU.mult))
                chain.step(T(w1, lb_im, lre, ALU.mult))
                chain.link(T(w2, lb1, lim, ALU.mult))
                chain.link(T(f_im, w1, w2, ALU.subtract))
                chain.link(T(f_im, f_im, turns, ALU.mult))
                dve.wait_ge(s5_zeroed, 1)
                fr, fi = (f.unsqueeze(2).broadcast_to([P, ST, SI]) for f in (f_re, f_im))
                for w, (x0, x1, op) in enumerate((((fr, 0), (fi, 1), ALU.subtract), ((fr, 1), (fi, 0), ALU.add))):
                    chain.step(T(work[:, 0], x0[0], b_in[:, x0[1]], ALU.mult))
                    chain.link(T(work[:, 1], x1[0], b_in[:, x1[1]], ALU.mult))
                    for g in range(2):
                        half = slice(g * SN, (g + 1) * SN)
                        chain.step(T(b_bar[half, w, :, g * SI:(g + 1) * SI], work[half, 0], work[half, 1], op))
                    chain.wait()
                dve.sem_inc(s5_dve, 1)
                p_re, p_im, n_re, n_im = sin_half, e_grow, mag1, poly
                chain.step(nc.vector.tensor_copy(p_re, cos))
                chain.step(nc.vector.tensor_copy(p_im, sin))
                chain.step(nc.vector.memset(fine[:, 0, :, 0:1], 1.0))
                chain.link(nc.vector.memset(fine[:, 1, :, 0:1], 0.0))
                n = 1
                while n < FINE:
                    b_re, b_im = (v.unsqueeze(2).broadcast_to([P, ST, n]) for v in (p_re, p_im))
                    complex_product(fine[:, 0, :, n:2 * n], fine[:, 1, :, n:2 * n], fine[:, 0, :, 0:n], fine[:, 1, :, 0:n],
                                    b_re, b_im, work[:, 0, :, 0:n], work[:, 1, :, 0:n])
                    complex_product(n_re, n_im, p_re, p_im, p_re, p_im, w1, w2)
                    p_re, p_im, n_re, n_im = n_re, n_im, p_re, p_im
                    n *= 2
                end_phase(dve, state)

                def leave(k):
                    dve.wait_ge(y_made, k + 1)
                    d = NORM_COLS["d"] + KT * j + k
                    nc.vector.scalar_tensor_tensor(out=hf[:, k, :], in0=hf[:, k, :], scalar=misc[:, d:d + 1],
                                                   in1=bank[:, 4 + k % 2, :], op0=ALU.mult, op1=ALU.add).then_inc(y_in, 1)

                for q in range(ST):
                    r = q % 2
                    if q >= 1:
                        dve.wait_ge(products_made, q)
                    dve.wait_ge(table_made, q + 1)
                    dve.wait_ge(bu_made, q + 1)
                    t_re, t_im, b_re, b_im = turn_t[:, r, 0, :], turn_t[:, r, 1, :], bank[:, 2 * r, :], bank[:, 2 * r + 1, :]
                    sw = [scan_w[:, n, :] for n in range(4)]
                    chain.step(T(sw[0], b_re, t_re, ALU.mult))
                    chain.step(T(sw[1], b_im, t_im, ALU.mult))
                    chain.step(T(sw[2], b_im, t_re, ALU.mult))
                    T(sw[3], b_re, t_im, ALU.mult).then_inc(bu_free, 1)
                    dve.wait_ge(bu_free, q + 1)
                    chain.wait()
                    chain.step(T(sw[0], sw[0], sw[1], ALU.add))
                    chain.link(T(sw[2], sw[2], sw[3], ALU.subtract))
                    mag = decay[:, q:q + 1].broadcast_to([P, S])
                    chain.step(nc.vector.tensor_tensor_scan(sw[1], mag, sw[0], 0.0, ALU.mult, ALU.add))
                    chain.link(nc.vector.tensor_tensor_scan(sw[3], mag, sw[2], 0.0, ALU.mult, ALU.add))
                    st = [state_w[:, r, n, :] for n in range(4)]
                    for need in ([q - 2] if q >= 2 else []):
                        if need % 4 == 3:
                            dve.wait_ge(y_made, need // 4 + 1)
                        else:
                            dve.wait_ge(products_used, 3 * (need // 4) + need % 4 + 1)
                    T(st[0], sw[1], t_re, ALU.mult)
                    nc.vector.scalar_tensor_tensor(out=st[1], in0=sw[3], scalar=-1.0, in1=t_im, op0=ALU.mult, op1=ALU.mult)
                    T(st[2], sw[3], t_re, ALU.mult)
                    T(st[3], sw[1], t_im, ALU.mult).then_inc(products_made, 1)
                    if q >= 5 and q % 4 == 1:
                        leave(q // 4 - 1)
                leave(KT - 1)
                for k in range(KT):
                    dve.wait_ge(y_high, k + 1)
                    T(h_lo[:, k, :], hf[:, k, :], h_hi[:, k, :].bitcast(F32), ALU.subtract)
                end_phase(dve, state)

                def glu_pair(i, r):
                    if not (isinstance(i, int) and 2 * i + r + 1 >= KT):
                        for e in range(2):
                            split_low(dve, U, i, 4, 2 * (r + 1) + e, KT * P)
                    m = i * 2 + r
                    dve.wait_ge(sig_made, i * 2 + (r + 1))
                    nc.vector.scalar_tensor_tensor(out=gated[:, r, :], in0=bank[:, 2 * r, :], scalar=mod[:, bass.ds(i * 2 + (mod_col(l, 2, 0) + r), 1)],
                                                   in1=sig[:, r, :], op0=ALU.mult, op1=ALU.mult).then_inc(drained, 1)
                    dve.wait_ge(drained, i * 4 + (dr + 2 * r + 1))
                    at = x[:, m, :] if isinstance(m, int) else x[:, bass.ds(m, 1), :].squeeze(1)
                    nc.vector.tensor_tensor(at, at, gated[:, r, :], ALU.add).then_inc(drained, 1)

                repeat(dve, 3, 2, KT, glu_pair)
            for name, l, j, U, dr, idx in plan:
                if name == "norm":
                    norm(l, j, idx, U)
                    continue
                elif name == "mla":
                    mla(l, j, U, dr, idx, state)
                elif name == "nsa":
                    nsa(l, j, U, dr, idx, state)
                elif name == "s5":
                    s5(l, j, U, dr, idx, state)
                elif name == "ffn":
                    ffn(l, U, dr, idx)
                else:
                    norm(0, 2, idx)
                    for k in range(KT):
                        dve.wait_ge(turned_in, N_TURN + KT + k + 1)
                        nc.vector.tensor_copy(out_rows[:, :, k * P:(k + 1) * P],
                                              bank[:, 4 + k % 2, :].rearrange("p (t f) -> p t f", t=TT)).then_inc(copied_in, 1)
                end_phase(dve, state)

        @block.gpsimd
        def _(pool):
            state, chain = [0], Chain(pool, pool_chain)
            pool.sem_inc(g_made, 2)
            end_phase(pool, state)
            pool.sem_inc(pt_act, 2)
            pool.sem_inc(pt_dve, 2)
            pool.sem_inc(o_low, 1)

            def scale(p, r, probs):
                pool.wait_ge(factored, p + 1)
                for q in range(TT):
                    at = probs[:, r, ROW_AT[q]:ROW_AT[q] + P * (q + 1)]
                    last = nc.gpsimd.tensor_tensor(at, at, factor[:, r, q:q + 1].broadcast_to([P, P * (q + 1)]), ALU.mult)
                last.then_inc(scaled, 1)

            def mla(l, j, U, dr, idx, state):
                pool.dma_start(rope[:], t["rope"]).then_inc(mla_side, 16)
                end_phase(pool, state)
                repeat(pool, 4, 2, HEADS, lambda i, r: scale(i * 2 + (passes_at[l] + r), r, m_probs))
                end_phase(pool, state)
                if l == LAYERS[0]:
                    for n in range(KT, 2 * KT):
                        load_ada(pool, l, n)
            def nsa(l, j, U, dr, idx, state):
                for dst, src in ((pe_rows[:, 0, :], t["nsa_pe_k"][j]), (pe_rows[:, 1, :], t["nsa_pe_v"][j]),
                                 (w2[:, 0], t["nsa_w2_k"][j].rearrange("(k p) m -> p k m", p=P)),
                                 (w2[:, 1], t["nsa_w2_v"][j].rearrange("(k p) m -> p k m", p=P)),
                                 (near_hot[:], t["near"]), (far_hot[:], t["far"]), (flip[:], t["flip"]), (rel[:], t["rel_bias"])):
                    pool.dma_start(dst, src).then_inc(nsa_side, 16)
                end_phase(pool, state)
                near_d, far_d = scratch[:, 0:3 * P], scratch[:, 1024:1024 + 2 * S]
                pool.dma_start(near_d, near_rows[:]).then_inc(rows_out, 16)
                pool.dma_start(far_d, far_rows[:]).then_inc(rows_out, 16)
                pool.wait_ge(rows_out, 32)
                row = scratch.shape[1]
                pool.dma_start(near_back, bass.AP(tensor=scratch.tensor, offset=0, ap=[[1, P], [row, HEADS], [1, FAR]])).then_inc(rows_back, 16)
                for h in range(HEADS):
                    at = NC * (h % 4)
                    src = bass.AP(tensor=scratch.tensor, offset=1024 + row * h, ap=[[CS, NC], [1, S]])
                    pool.dma_start(cmp_back[at:at + NC, h // 4, :], src).then_inc(rows_back, 16)
                end_phase(pool, state)
                end_phase(pool, state)
                for h in range(HEADS):
                    scale(passes_at[l] + 2 * h, 0, n_probs)
                    scale(passes_at[l] + 2 * h + 1, 1, n_probs)
                end_phase(pool, state)
            def s5(l, j, U, dr, idx, state):
                T = nc.gpsimd.tensor_tensor
                nc.gpsimd.memset(b_bar[:, :, :, :], 0.0).then_inc(s5_zeroed, 1)
                nc.gpsimd.memset(out_map[:, :, :, :], 0.0).then_inc(s5_zeroed, 1)

                def complex_product(o_re, o_im, a_re, a_im, b_re, b_im, w1, w2):
                    chain.step(T(w1, a_re, b_re, ALU.mult))
                    chain.link(T(w2, a_im, b_im, ALU.mult))
                    chain.link(T(o_re, w1, w2, ALU.subtract))
                    chain.step(T(w1, a_re, b_im, ALU.mult))
                    chain.link(T(w2, a_im, b_re, ALU.mult))
                    chain.link(T(o_im, w1, w2, ALU.add))

                pool.wait_ge(s5_trig, 1)
                sin, cos = small[:, 6, :], small[:, 8, :]
                c0_re, c0_im, c1_re, c1_im, w1, w2 = (small[:, n, :] for n in range(20, 26))
                complex_product(c0_re, c0_im, cos, sin, cos, sin, w1, w2)
                p_re, p_im, n_re, n_im = c0_re, c0_im, c1_re, c1_im
                for _ in range(int(math.log2(FINE)) - 1):
                    complex_product(n_re, n_im, p_re, p_im, p_re, p_im, w1, w2)
                    p_re, p_im, n_re, n_im = n_re, n_im, p_re, p_im
                chain.step(nc.gpsimd.memset(coarse[:, 0, :, 0:1], 1.0))
                chain.link(nc.gpsimd.memset(coarse[:, 1, :, 0:1], 0.0))
                n = 1
                while n < COARSE:
                    b_re, b_im = (v.unsqueeze(2).broadcast_to([P, ST, n]) for v in (p_re, p_im))
                    complex_product(coarse[:, 0, :, n:2 * n], coarse[:, 1, :, n:2 * n], coarse[:, 0, :, 0:n], coarse[:, 1, :, 0:n],
                                    b_re, b_im, work_c[:, 0, :, 0:n], work_c[:, 1, :, 0:n])
                    complex_product(n_re, n_im, p_re, p_im, p_re, p_im, w1, w2)
                    p_re, p_im, n_re, n_im = n_re, n_im, p_re, p_im
                    n *= 2
                end_phase(pool, state)

                for q in range(ST):
                    r = q % 2
                    if q >= 2:
                        pool.wait_ge(products_made, q - 1)
                    if q >= 1:
                        pool.wait_ge(table_made, q)
                    shape = [P, COARSE, FINE]
                    c_re, c_im = (coarse[:, w, q, :].unsqueeze(2).broadcast_to(shape) for w in range(2))
                    f_re, f_im = (fine[:, w, q, :].unsqueeze(1).broadcast_to(shape) for w in range(2))
                    to, w1, w2 = (v.rearrange("p (c f) -> p c f", c=COARSE) for v in (turn_t[:, r, 0, :], turn_w[:, 0, :], turn_w[:, 1, :]))
                    ti = turn_t[:, r, 1, :].rearrange("p (c f) -> p c f", c=COARSE)
                    chain.step(nc.gpsimd.tensor_tensor(w1, c_re, f_re, ALU.mult))
                    chain.link(nc.gpsimd.tensor_tensor(w2, c_im, f_im, ALU.mult))
                    chain.link(nc.gpsimd.tensor_tensor(to, w1, w2, ALU.subtract))
                    chain.step(nc.gpsimd.tensor_tensor(w1, c_re, f_im, ALU.mult))
                    chain.link(nc.gpsimd.tensor_tensor(w2, c_im, f_re, ALU.mult))
                    nc.gpsimd.tensor_tensor(ti, w1, w2, ALU.add).then_inc(table_made, 1)
                end_phase(pool, state)
            for name, l, j, U, dr, idx in plan:
                if name in ("norm", "final"):
                    pool.wait_ge(rs_made, idx + 1)
                    pool.wait_ge(ada_turned, 2 * len(LAYERS) if name == "final" else 1 if idx == 0 else 2 * (l_at[l] + 1))
                    for k in range(KT):
                        nc.gpsimd.tensor_tensor(hf[:, k, :], x[:, k, :], rs[:, :], ALU.mult).then_inc(x_scaled, 1)
                    if name == "norm":
                        continue
                elif name == "mla":
                    mla(l, j, U, dr, idx, state)
                elif name == "nsa":
                    nsa(l, j, U, dr, idx, state)
                elif name == "s5":
                    s5(l, j, U, dr, idx, state)
                elif l in following:
                    for n in range(2 * KT):
                        load_ada(pool, following[l], n)
                end_phase(pool, state)


_INS = ["x", "c", "ada_w", "ada_b", "norm1_g", "norm2_g", "final_g", "rel_bias",
        "mla_w_dkv", "mla_g_q", "mla_g_kv", "mla_w_uq", "mla_w_ukv", "mla_w_o",
        "nsa_w_in", "nsa_pe_k", "nsa_w1_k", "nsa_w2_k", "nsa_pe_v", "nsa_w1_v", "nsa_w2_v", "nsa_w_o",
        "s5_lam_re", "s5_lam_im", "s5_log_dt", "s5_b_re", "s5_b_im", "s5_c_re", "s5_c_im", "s5_d", "s5_w_glu",
        "ffn_w_up", "ffn_conv_w", "ffn_conv_b", "ffn_w_down"]


def shape_tables():
    import numpy as np
    eye = np.eye(P, dtype=np.float32)
    later = np.triu(np.ones((P, P), np.float32), 1) * np.float32(MASKED)
    half = ROPE // 2
    inv = (np.float32(10000.0) ** (-np.arange(half, dtype=np.float32) / np.float32(half))).astype(np.float32)
    ang = (inv[:, None] * np.arange(S, dtype=np.float32)[None, :]).astype(np.float32)
    cos, sin = np.cos(ang.astype(np.float64)), np.sin(ang.astype(np.float64))
    rope = np.stack([np.concatenate([cos, cos]), np.concatenate([-sin, sin])], 1).astype(np.float32)

    def bucket(dist):
        n = np.maximum(dist, 0)
        nf = np.maximum(n, 1).astype(np.float32)
        large = 16 + (np.log(nf / np.float32(16)) / np.float32(math.log(8)) * np.float32(16)).astype(np.int32)
        return np.where(n < 16, n, np.minimum(large, BUCKETS - 1))

    def hot(dist):
        at = np.zeros((BUCKETS + 1, len(dist)), np.float32)
        at[bucket(dist), np.arange(len(dist))] = 1.0
        at[BUCKETS] = np.where(dist < 0, np.float32(MASKED), np.float32(0))
        return at

    near = hot(255 - np.arange(384))
    far = hot(np.arange(1024) - 511 )
    return {"ident": eye, "flip": eye[::-1].copy(), "mask": later,
            "rope": rope, "near": near, "far": far}


def kernel(**inputs):
    import numpy as np
    import concourse.bacc as bacc
    from concourse.bass_utils import run_bass_kernel_spmd

    nc = bacc.Bacc("TRN2", target_bir_lowering=False, num_devices=1)
    arrays, aps = {}, {}
    given = {n: np.ascontiguousarray(inputs[n]) for n in _INS}
    given.update(shape_tables())
    for name, a in given.items():
        arrays[f"in_{name}"] = a
        aps[name] = nc.dram_tensor(f"in_{name}", a.shape, mybir.dt.from_np(a.dtype), kind="ExternalInput").ap()
    out = nc.dram_tensor("out", (1, S, D), F32, kind="ExternalOutput").ap()
    scratch = nc.dram_tensor("bias_rows", (HEADS, 2048), F32, kind="Internal").ap()
    trunk(nc, aps, out, scratch)
    got = run_bass_kernel_spmd(nc, [arrays], core_ids=[0]).results[0]
    return got["out"]
```
